# Optimizing a Trainium2 kernel written in Bass

```python
import jax, jax.numpy as jnp
from jax import lax
import numpy as np

D_MODEL = 1024
BATCH = 1
SEQ = 512
DEPTH = 1
DEC_BATCH = 8
DEC_SEQ = 8
PAST_LEN = 4096
PAGE_SIZE = 128

POOL_WIDTH = D_MODEL
POOL_WINDOWS = (2, 4, 8, 16)
POOL_GROUPS = len(POOL_WINDOWS)
POOL_GROUP_DIM = POOL_WIDTH // POOL_GROUPS
POOL_BUF = max(POOL_WINDOWS) - 1
LRU_WIDTH = D_MODEL
LRU_HEADS = 8
LRU_HEAD_DIM = LRU_WIDTH // LRU_HEADS
CONV_WIDTH = 4
LRU_C = 8.0
N_BRANCH = 2
IN_WIDTH = POOL_WIDTH + 2 * LRU_WIDTH + N_BRANCH * D_MODEL
PEER_HEADS = 8
PEER_NKEYS = 128
PEER_EXPERTS = PEER_NKEYS * PEER_NKEYS
PEER_TOPK = 16
PEER_DKEY = 256
PEER_DHALF = PEER_DKEY // 2
PEER_BLOCK = 256

NORM_EPS = 1e-6
F32 = jnp.float32

kernel_name = "hybrid_pool_rglru_peer_adaln_step"

def rmsnorm(x, g):
    xf = x.astype(F32)
    y = xf * lax.rsqrt(jnp.mean(xf * xf, axis=-1, keepdims=True) + NORM_EPS) * g.astype(F32)
    return y.astype(x.dtype)

def modulate(h, shift, scale):
    return h * (1 + scale[:, None, :]) + shift[:, None, :]

def lru_scan(a, bx, h0):
    def step(h, ab):
        a_t, b_t = ab
        h = a_t * h + b_t
        return h, h
    h_last, hs = lax.scan(step, h0, (jnp.swapaxes(a, 0, 1), jnp.swapaxes(bx, 0, 1)))
    return jnp.swapaxes(hs, 0, 1), h_last

def mixer_block(h, pos, pool_buf, conv_buf, lru_h, w_in, b_gate, pool_mix, pool_scale,
                conv_w, conv_b, w_rg, b_rg, w_ig, b_ig, lru_lambda,
                w_branch_a, w_branch_b, w_out):
    B, T, _ = h.shape
    proj = h @ w_in
    u, xb, yb, gate_logits = jnp.split(
        proj, [POOL_WIDTH, POOL_WIDTH + LRU_WIDTH, POOL_WIDTH + 2 * LRU_WIDTH], axis=-1)

    ext = jnp.concatenate([pool_buf.astype(u.dtype), u], axis=1)
    cs = jnp.cumsum(ext.astype(F32), axis=1)
    cs = jnp.concatenate([jnp.zeros((B, 1, POOL_WIDTH), F32), cs], axis=1)
    end = cs[:, POOL_BUF + 1:]
    means = []
    for g, w in enumerate(POOL_WINDOWS):
        sl = slice(g * POOL_GROUP_DIM, (g + 1) * POOL_GROUP_DIM)
        start = cs[:, POOL_BUF + 1 - w:POOL_BUF + 1 - w + T, sl]
        cnt = jnp.minimum(pos + 1, w).astype(F32)[None, :, None]
        means.append((end[..., sl] - start) / cnt)
    pooled = (jnp.concatenate(means, axis=-1) - u.astype(F32)).astype(h.dtype)
    pooled = pooled.reshape(B, T, POOL_GROUPS, POOL_GROUP_DIM)
    z = jnp.einsum('btgi,gij->btgj', pooled, pool_mix).reshape(B, T, POOL_WIDTH) * pool_scale
    y_a = z @ w_branch_a
    new_pool_buf = ext[:, -POOL_BUF:]

    ext_c = jnp.concatenate([conv_buf.astype(xb.dtype), xb], axis=1)
    xc = conv_b + ext_c[:, 0:T] * conv_w[0]
    for k in range(1, CONV_WIDTH):
        xc = xc + ext_c[:, k:k + T] * conv_w[k]
    new_conv_buf = ext_c[:, -(CONV_WIDTH - 1):]
    xh = xc.reshape(B, T, LRU_HEADS, LRU_HEAD_DIM)
    r = jax.nn.sigmoid((jnp.einsum('bthi,hij->bthj', xh, w_rg).reshape(B, T, LRU_WIDTH) + b_rg).astype(F32))
    i = jax.nn.sigmoid((jnp.einsum('bthi,hij->bthj', xh, w_ig).reshape(B, T, LRU_WIDTH) + b_ig).astype(F32))
    log_a = -LRU_C * r * jax.nn.softplus(-lru_lambda.astype(F32))
    a = jnp.exp(log_a)
    mult = jnp.sqrt(-jnp.expm1(2.0 * log_a))
    mult = jnp.where((pos == 0)[None, :, None], 1.0, mult)
    bx = mult * i * xc.astype(F32)
    hs, h_last = lru_scan(a, bx, lru_h.astype(F32))
    y_b = (hs.astype(h.dtype) * jax.nn.gelu(yb)) @ w_branch_b

    gates = jax.nn.sigmoid((gate_logits + b_gate).astype(F32)).astype(h.dtype)
    g_a, g_b = jnp.split(gates, N_BRANCH, axis=-1)
    out = (g_a * y_a + g_b * y_b) @ w_out
    return out, new_pool_buf, new_conv_buf, h_last

def peer_block(h, w_q, sub_keys, expert_u, expert_v):
    B, T, D = h.shape
    n = B * T
    n_blk = -(-n // PEER_BLOCK)
    flat = jnp.pad(h.reshape(n, D), ((0, n_blk * PEER_BLOCK - n), (0, 0)))
    flat = flat.reshape(n_blk, PEER_BLOCK, D)
    keys = sub_keys.astype(F32)

    def one_block(xb):
        q = (xb @ w_q).reshape(PEER_BLOCK, PEER_HEADS, 2, PEER_DHALF).astype(F32)
        s = jnp.einsum('nhpd,hpkd->nhpk', q, keys)
        top_s, top_i = lax.top_k(s, PEER_TOPK)
        cand = top_s[:, :, 0, :, None] + top_s[:, :, 1, None, :]
        cand_idx = top_i[:, :, 0, :, None] * PEER_NKEYS + top_i[:, :, 1, None, :]
        cand = cand.reshape(PEER_BLOCK, PEER_HEADS, PEER_TOPK * PEER_TOPK)
        cand_idx = cand_idx.reshape(PEER_BLOCK, PEER_HEADS, PEER_TOPK * PEER_TOPK)
        best_s, best_j = lax.top_k(cand, PEER_TOPK)
        idx = jnp.take_along_axis(cand_idx, best_j, axis=-1)
        gsm = jax.nn.softmax(best_s, axis=-1)
        act = jax.nn.gelu(jnp.einsum('nd,nhkd->nhk', xb, expert_u[idx]).astype(F32))
        wts = (gsm * act).astype(xb.dtype)
        return jnp.einsum('nhk,nhkd->nd', wts, expert_v[idx])

    out = lax.map(one_block, flat)
    return out.reshape(n_blk * PEER_BLOCK, D)[:n].reshape(B, T, D)

def run_trunk(x, c, pos, pool_bufs, conv_bufs, lru_hs, norm1, norm2, w_ada, b_ada, w_in, b_gate,
              pool_mix, pool_scale, conv_w, conv_b, w_rg, b_rg, w_ig, b_ig, lru_lambda,
              w_branch_a, w_branch_b, w_out, w_q, sub_keys, expert_u, expert_v, final_norm):
    new_pool, new_conv, new_lru = [], [], []
    for l in range(DEPTH):
        mod = jax.nn.silu(c) @ w_ada[l] + b_ada[l]
        sh1, sc1, g1, sh2, sc2, g2 = jnp.split(mod, 6, axis=-1)
        h = modulate(rmsnorm(x, norm1[l]), sh1, sc1)
        mix, pb, cb, lh = mixer_block(
            h, pos, pool_bufs[l], conv_bufs[l], lru_hs[l], w_in[l], b_gate[l], pool_mix[l],
            pool_scale[l], conv_w[l], conv_b[l], w_rg[l], b_rg[l], w_ig[l], b_ig[l],
            lru_lambda[l], w_branch_a[l], w_branch_b[l], w_out[l])
        x = x + g1[:, None, :] * mix
        h = modulate(rmsnorm(x, norm2[l]), sh2, sc2)
        x = x + g2[:, None, :] * peer_block(h, w_q[l], sub_keys[l], expert_u[l], expert_v[l])
        new_pool.append(pb)
        new_conv.append(cb)
        new_lru.append(lh)
    y = rmsnorm(x, final_norm)
    return y, jnp.stack(new_pool), jnp.stack(new_conv), jnp.stack(new_lru)

def setup_inputs(seed: int = 0) -> dict:
    key = jax.random.key(seed)
    ks = jax.random.split(key, 32)
    nrm = lambda k, shape, s: jax.random.normal(k, shape, F32) * s
    L, D = DEPTH, D_MODEL
    target = jax.random.uniform(ks[20], (L, LRU_WIDTH), F32, 0.9, 0.999)
    a_base = target ** (1.0 / LRU_C)
    lru_lambda = jnp.log(a_base) - jnp.log1p(-a_base)
    return {
        "x_prompt": nrm(ks[0], (BATCH, SEQ, D), 1.0),
        "x_sample": nrm(ks[1], (DEC_BATCH, DEC_SEQ, D), 1.0),
        "c_prompt": nrm(ks[2], (BATCH, D), 1.0),
        "c_sample": nrm(ks[3], (DEC_BATCH, D), 1.0),
        "state_pool": nrm(ks[4], (L, DEC_BATCH, POOL_BUF, POOL_WIDTH), 1.0),
        "state_conv": nrm(ks[5], (L, DEC_BATCH, CONV_WIDTH - 1, LRU_WIDTH), 1.0),
        "state_lru": nrm(ks[6], (L, DEC_BATCH, LRU_WIDTH), 0.5),
        "norm1": 1.0 + nrm(ks[7], (L, D), 0.02),
        "norm2": 1.0 + nrm(ks[8], (L, D), 0.02),
        "w_ada": nrm(ks[9], (L, D, 6 * D), 0.5 * D ** -0.5),
        "b_ada": nrm(ks[10], (L, 6 * D), 0.02),
        "w_in": nrm(ks[11], (L, D, IN_WIDTH), D ** -0.5),
        "b_gate": nrm(ks[12], (L, N_BRANCH * D), 0.02),
        "pool_mix": nrm(ks[13], (L, POOL_GROUPS, POOL_GROUP_DIM, POOL_GROUP_DIM), POOL_GROUP_DIM ** -0.5),
        "pool_scale": 0.5 + nrm(ks[14], (L, POOL_WIDTH), 0.05),
        "conv_w": nrm(ks[15], (L, CONV_WIDTH, LRU_WIDTH), CONV_WIDTH ** -0.5),
        "conv_b": nrm(ks[16], (L, LRU_WIDTH), 0.02),
        "w_rg": nrm(ks[17], (L, LRU_HEADS, LRU_HEAD_DIM, LRU_HEAD_DIM), LRU_HEAD_DIM ** -0.5),
        "b_rg": nrm(ks[18], (L, LRU_WIDTH), 0.02),
        "w_ig": nrm(ks[19], (L, LRU_HEADS, LRU_HEAD_DIM, LRU_HEAD_DIM), LRU_HEAD_DIM ** -0.5),
        "b_ig": nrm(ks[21], (L, LRU_WIDTH), 0.02),
        "lru_lambda": lru_lambda,
        "w_branch_a": nrm(ks[22], (L, POOL_WIDTH, D), POOL_WIDTH ** -0.5),
        "w_branch_b": nrm(ks[23], (L, LRU_WIDTH, D), LRU_WIDTH ** -0.5),
        "w_out": nrm(ks[24], (L, D, D), D ** -0.5),
        "w_q": nrm(ks[25], (L, D, PEER_HEADS * PEER_DKEY), D ** -0.5),
        "sub_keys": nrm(ks[26], (L, PEER_HEADS, 2, PEER_NKEYS, PEER_DHALF), PEER_DHALF ** -0.5),
        "expert_u": nrm(ks[27], (L, PEER_EXPERTS, D), D ** -0.5),
        "expert_v": nrm(ks[28], (L, PEER_EXPERTS, D), 0.3),
        "final_norm": 1.0 + nrm(ks[29], (D,), 0.02),
    }

def reference(x_prompt, x_sample, c_prompt, c_sample, state_pool, state_conv, state_lru,
              norm1, norm2, w_ada, b_ada, w_in, b_gate, pool_mix, pool_scale, conv_w, conv_b,
              w_rg, b_rg, w_ig, b_ig, lru_lambda, w_branch_a, w_branch_b, w_out,
              w_q, sub_keys, expert_u, expert_v, final_norm):
    weights = (norm1, norm2, w_ada, b_ada, w_in, b_gate, pool_mix, pool_scale, conv_w, conv_b,
               w_rg, b_rg, w_ig, b_ig, lru_lambda, w_branch_a, w_branch_b, w_out,
               w_q, sub_keys, expert_u, expert_v, final_norm)
    pos_p = jnp.arange(SEQ, dtype=jnp.int32)
    zp = jnp.zeros((DEPTH, BATCH, POOL_BUF, POOL_WIDTH), x_prompt.dtype)
    zc = jnp.zeros((DEPTH, BATCH, CONV_WIDTH - 1, LRU_WIDTH), x_prompt.dtype)
    zh = jnp.zeros((DEPTH, BATCH, LRU_WIDTH), F32)
    y_prompt, pool_p, conv_p, lru_p = run_trunk(x_prompt, c_prompt, pos_p, zp, zc, zh, *weights)
    pos_s = PAST_LEN + jnp.arange(DEC_SEQ, dtype=jnp.int32)
    y_sample, pool_s, conv_s, lru_s = run_trunk(x_sample, c_sample, pos_s, state_pool, state_conv,
                                                state_lru, *weights)
    lru_p = lru_p.astype(state_lru.dtype)
    lru_s = lru_s.astype(state_lru.dtype)
    return (y_prompt, y_sample, pool_p, conv_p, lru_p, pool_s, conv_s, lru_s)


_drawn_inputs = setup_inputs


def setup_inputs(seed=0):
    import zlib

    import numpy as np

    out = dict(_drawn_inputs(seed))
    spreads = {}
    factors = {'norm1': 2.987,
     'norm2': 7.656,
     'b_gate': 8.0,
     'pool_scale': 6.496,
     'b_rg': 8.0,
     'b_ig': 6.482,
     'final_norm': 2.93}
    for name, (base, spread) in spreads.items():
        noise = np.random.default_rng([zlib.crc32(name.encode()), seed]).standard_normal(out[name].shape)
        drawn = base * np.exp(spread * noise) if base else spread * noise
        out[name] = __import__('jax').numpy.asarray(drawn.astype(out[name].dtype))
    for name, factor in factors.items():
        out[name] = (out[name] * factor).astype(out[name].dtype)
    return out
```

```python
from contextlib import ExitStack

import concourse.bass as bass
from concourse import mybir

P = 128
D = 1024
KT = D // P
SEQ, SB, ST = 512, 8, 8
NS = SB * ST
NR = SB + 1
WINDOWS = (2, 4, 8, 16)
PB = max(WINDOWS) - 1
CW = 4
CB = CW - 1
HEADS, NKEYS, TOPK = 8, 128, 16
SLOTS = HEADS * TOPK
EPS = 1e-6
LOWEST = -3.0e38
GROUP_P = (128, 384)
GROUP_S = (NS, 0)
N_MAX = max(GROUP_P)
TILES = 5
TILE_STEPS = (4, 8, 8, 8, 8)
STEP0 = (0, 4, 12, 20, 28)
WB = 256
NW, NU, NV, ND, NBANK = 3, 4, 8, 4, 6
VEC = ("norm1", "norm2", "pool_scale", "conv_b", "b_rg", "b_ig", "lru_lambda",
       "conv_w0", "conv_w1", "conv_w2", "conv_w3", "b_gate_a", "b_gate_b")

F32, U32 = mybir.dt.float32, mybir.dt.uint32
ALU, ACT, AX = mybir.AluOpType, mybir.ActivationFunctionType, mybir.AxisListType

PER = {"ada": 24, "modT": 1, "ss1": 1, "xb": 8, "rgig": 16, "yb": 8, "u": 8, "mix": 8, "mg": 16, "bb": 8,
       "ba": 8, "out": 8, "ss2": 1, "q": 16, "tok": 4, "score": 4, "g2": 2}
COLS = {"xb": 4, "u": 0, "yb": 8, "mg": 12, "bb": 0, "ba": 0, "out": 0, "q": 0}


def dense_units(g):
    units = [("norm", g, 0)]
    units += [("xb", g, b) for b in range(4)] + [("yb", g, 0), ("rgig", g, 0), ("yb", g, 1), ("yb", g, 2), ("yb", g, 3)]
    units += [("lru", g, 0)] + [("u", g, b) for b in range(4)]
    units += [("mg", g, b) for b in range(2)] + [("mix", g, 0)] + [("mg", g, b) for b in range(2, 8)]
    units += [(k, g, b) for k in ("ba", "bb", "out") for b in range(4)]
    units += [("norm", g, 1)] + [("q", g, b) for b in range(8)]
    return units


def group_tiles(g):
    return (0, 1) if g == 0 else (2, 3, 4)


def schedule():
    s = [("ada", 0, 0)] + dense_units(0)
    s += [("tok", t, 0) for t in group_tiles(0)] + [("topk", t, 0) for t in group_tiles(0)]
    rest = dense_units(1) + [("tok", t, 0) for t in group_tiles(1)]
    steps = [(t, i) for t in group_tiles(0) for i in range(TILE_STEPS[t])]
    for n, (t, i) in enumerate(steps):
        s += [("step", t, i)]
        s += [("final", t, 0)] if i == TILE_STEPS[t] - 1 else []
        s += rest[n * len(rest) // len(steps):(n + 1) * len(rest) // len(steps)]
    for t in group_tiles(1):
        s += [("topk", t, 0), ("steps", t, 0), ("final", t, 0)]
    return s


SCHEDULE = schedule()


def products_of(unit):
    kind, g, b = unit
    if kind == "ada":
        return [("ada", 0, i) for i in range(24)] + [("modT", 0, 0)]
    if kind == "norm":
        return [(("ss1", "ss2")[b], g, 0)]
    if kind in COLS:
        return [(kind, g, 2 * b), (kind, g, 2 * b + 1)]
    if kind in ("rgig", "mix"):
        return [(kind, g, i) for i in range(PER[kind])]
    if kind in ("tok",):
        return [(kind, g, i) for i in range(4)]
    if kind == "topk":
        return [("score", g, i) for i in range(4)]
    if kind == "final":
        return [("g2", g, i) for i in range(2)]
    return []


PRODUCTS = [p for unit in SCHEDULE for p in products_of(unit)]
NUMBER = {p: n for n, p in enumerate(PRODUCTS)}


def nth(product):
    kind, g, i = product
    return g * PER[kind] + i + 1


def weight_blocks():
    blocks = []
    for unit in SCHEDULE:
        kind, g, b = unit
        if kind == "ada":
            blocks += [(("ada", 0, i), ("ada", 0, i)) for i in range(24)]
        elif kind in COLS or kind in ("rgig", "mix"):
            blocks.append((unit, products_of(unit)[-1]))
        elif kind == "topk" and g in (0, 2):
            blocks.append((("keys", int(g > 0), 0), ("score", group_tiles(int(g > 0))[-1], 3)))
    return blocks


BLOCKS = weight_blocks()
BLOCK_NO = {unit: n for n, (unit, _) in enumerate(BLOCKS)}


def trunk(nc, A):
    ctx = ExitStack()
    with ctx:
        def sb(name, shape, dt=F32):
            return ctx.enter_context(nc.sbuf_tensor("t_" + name, shape, dt))

        def sem(name):
            return ctx.enter_context(nc.semaphore(name))

        CEXT = KT * (N_MAX + CB)
        UEXT = KT * (N_MAX + PB)
        NB = KT * N_MAX
        arena = sb("arena", [P, 6 * NB + CEXT + UEXT])
        at, place = 0, {}
        for name, size in (("x", NB), ("h", NB), ("xc", NB), ("gy", NB), ("conv", CEXT), ("i", NB), ("pool", UEXT),
                           ("gb", NB)):
            place[name] = at
            at += size

        def region(name, size):
            return arena[:, place[name]:place[name] + size]

        def cols(name, g):
            n = GROUP_S[g] + GROUP_P[g]
            return region(name, KT * n).rearrange("p (k n) -> p k n", k=KT)

        mod_rows = arena[0:NR, place["xc"]:place["xc"] + 6 * D]
        b_ada = arena[0:NR, place["conv"]:place["conv"] + 6 * D]
        weights = sb("weights", [P, NW, KT * WB])
        u_rows = sb("u_rows", [P, NU, D])
        v_rows = sb("v_rows", [P, NV, D])
        tok0 = sb("tok0", [P, 4, D])
        g2_rows = sb("g2_rows", [NR, D])
        final_norm = sb("final_norm", [P, D])
        vecs = sb("vecs", [P, len(VEC), KT])
        ident = sb("ident", [P, P])
        ident2 = sb("ident2", [P, NS])
        select = sb("select", [NR, 2, P])
        inv_count = sb("inv_count", [P, len(WINDOWS), 16])
        iota16 = sb("iota16", [P, 16])
        ones = sb("ones", [P, P])
        zeros = sb("zeros", [1, P])
        c_t = sb("c_t", [P, KT, NR])
        silu_c = sb("silu_c", [P, KT, NR])
        mod_t = sb("mod_t", [P, 5 * KT, NR])
        coef = sb("coef", [P, 2, KT, NR])
        sp4 = sb("sp4", [P, KT])
        sp_tmp = sb("sp_tmp", [P, 6, KT])
        small = sb("small", [P, NS])
        conv_tail = sb("conv_tail", [P, KT, CB])
        conv_s = sb("conv_s", [P, KT, SB, CB])
        pool_tail = sb("pool_tail", [P, KT, PB])
        lru_tail = sb("lru_tail", [P, KT])
        lru_s = sb("lru_s", [P, KT, SB])
        bx_first = sb("bx_first", [P, KT])
        idx0 = sb("idx0", [P, 2, SLOTS], U32)
        gsm0 = sb("gsm0", [P, 2, SLOTS])
        step_idx = sb("step_idx", [P, 2, TOPK], U32)
        dots = sb("dots", [P, TOPK])
        gelus = sb("gelus", [P, TOPK])
        wts = sb("wts", [P, TOPK])
        diag = sb("diag", [P, ND, P])
        fin = sb("fin", [P, 4])
        banks = [ctx.enter_context(nc.psum_tensor(f"bank{i}", [P, 512], F32)) for i in range(NBANK)]
        v_sum = ctx.enter_context(nc.psum_tensor("v_sum", [P, D], F32))

        state = tok0[:, 0:2, :].rearrange("p a d -> p (a d)")
        state_pool = state[:, 0:KT * SB * PB].rearrange("p (k b t) -> p k b t", k=KT, b=SB)
        s1 = KT * SB * PB
        state_conv = state[:, s1:s1 + KT * SB * CB].rearrange("p (k b t) -> p k b t", k=KT, b=SB)
        s2 = s1 + KT * SB * CB
        state_lru = state[:, s2:s2 + KT * SB].rearrange("p (k b) -> p k b", k=KT)
        pool_s = tok0[:, 2, 0:KT * SB * PB].rearrange("p (k b t) -> p k b t", k=KT, b=SB)

        ms, rstd = (region("gb", 2 * N_MAX)[:, i * N_MAX:(i + 1) * N_MAX] for i in range(2))
        h_twice = region("gb", 2 * N_MAX + KT * P)[:, 2 * N_MAX:].rearrange("p (k n) -> p k n", k=KT)
        choice = region("pool", 12 * SLOTS).rearrange("p (a s) -> p a s", s=SLOTS)
        top_i = choice[:, 0:2, :].bitcast(U32).rearrange("p a (h k) -> p (a h) k", k=TOPK)
        best_j = choice[:, 2, :].bitcast(U32).rearrange("p (h k) -> p h k", k=TOPK)
        part_u = choice[:, 3:5, :].bitcast(U32)
        exps = choice[:, 5, :]

        def idx_of(t):
            return idx0[:, t, :] if t < 2 else choice[:, 4 + t, :].bitcast(U32)

        def gsm_of(t):
            return gsm0[:, t, :] if t < 2 else choice[:, 7 + t, :]

        def vec(name):
            return vecs[:, VEC.index(name), :]

        def h2_rows(t):
            return tok0[:, t, :] if t < 2 else region("conv", NB)[:, (t - 2) * D:(t - 1) * D]

        def x1_rows(t):
            return tok0[:, 2 + t, :] if t < 2 else region("i", NB)[:, (t - 2) * D:(t - 1) * D]

        const_in, c_in, bias_in, norm_in, x_in, state_in = (sem(x) for x in (
            "const_in", "c_in", "bias_in", "norm_in", "x_in", "state_in"))
        weight_in = [sem(f"weight_in{i}") for i in range(NW)]
        ready = {k: sem(f"{k}_ready") for k in PER}
        taken = {k: sem(f"{k}_taken") for k in PER}
        silu_done, zeros_done, square_done, std_done, h_scaled, h_prompt, h_sample = (sem(x) for x in (
            "silu_done", "zeros_done", "square_done", "std_done", "h_scaled", "h_prompt", "h_sample"))
        ms_done, ext_filled, conv_done, tanh_done, sqrt_done, scan_done, gy_done, pooled_done, exp_done, centered = (
            sem(x) for x in ("ms_done", "ext_filled", "conv_done", "tanh_done", "sqrt_done", "scan_done", "gy_done",
                             "pooled_done", "exp_done", "centered"))
        dve_step, coef_done, idx_done = sem("dve_step"), sem("coef_done"), sem("idx_done")
        u_in = [sem(f"u_in{i}") for i in range(NU)]
        v_in = [sem(f"v_in{i}") for i in range(NV)]
        u_free, v_free, idx_copied, dots_done, gelu_done, wts_done, diag_done, v_begun = (sem(x) for x in (
            "u_free", "v_free", "idx_copied", "dots_done", "gelu_done", "wts_done", "diag_done", "v_begun"))
        v_tile, v_read, act_self, yfin, ysq, ymean, ystd, yready, tails, out_done = (sem(x) for x in (
            "v_tile", "v_read", "act_self", "yfin", "ysq", "ymean", "ystd", "yready", "tails", "out_done"))

        N_CONST, N_NORM = 6, 1

        def sizes(g):
            return GROUP_S[g], GROUP_P[g], GROUP_S[g] + GROUP_P[g]

        def conv_ext(g):
            s, p, n = sizes(g)
            w = (s // ST) * (ST + CB) + p + CB
            rows = region("conv", KT * w).rearrange("p (k w) -> p k w", k=KT)
            smp = rows[:, :, 0:w - p - CB].rearrange("p k (b t) -> p k b t", t=ST + CB) if s else None
            return smp, rows[:, :, w - p - CB:w]

        def pool_ext(g):
            s, p, n = sizes(g)
            w = (s // ST) * (ST + PB) + p + PB
            rows = region("pool", KT * w).rearrange("p (k w) -> p k w", k=KT)
            smp = rows[:, :, 0:w - p - PB].rearrange("p k (b t) -> p k b t", t=ST + PB) if s else None
            return rows, smp, rows[:, :, w - p - PB:w]

        def queries(g):
            n = sizes(g)[2] + GROUP_S[g]
            return arena[:, place["xc"]:place["xc"] + 2 * KT * n].rearrange("p (k n) -> p k n", k=2 * KT)

        def by_seq(view):
            return view[:, :, 0:NS].rearrange("p k (b t) -> p k b t", b=SB)

        block = ctx.enter_context(nc.Block())

        @block.sync
        def _(sp):
            sp.dma_start(c_t[:, :, :], A["c_t"]).then_inc(c_in, 16)
            sp.dma_start(b_ada, A["b_ada"].broadcast_to([NR, 6 * D])).then_inc(bias_in, 16)

            def load_weights(n):
                unit, _ = BLOCKS[n]
                kind, g, b = unit
                if n >= NW:
                    last = BLOCKS[n - NW][1]
                    sp.wait_ge(ready[last[0]], nth(last))
                slot = weights[:, n % NW, :]
                if kind == "rgig":
                    dst = slot.rearrange("p (a h n) -> p a h n", a=2, h=HEADS)
                    sp.dma_start(dst[:, 0], A["w_rg"]).then_inc(weight_in[n % NW], 16)
                    sp.dma_start(dst[:, 1], A["w_ig"]).then_inc(weight_in[n % NW], 16)
                    return
                if kind == "keys":
                    src, dst = A["keys_t"], slot
                elif kind == "mix":
                    src = A["pool_mix"]
                    dst = slot.rearrange("p (g k n) -> p g k n", g=4, k=2)
                else:
                    name = {"ada": "w_ada", "bb": "w_branch_b", "ba": "w_branch_a", "out": "w_out", "q": "w_q"}.get(kind, "w_in")
                    c = (COLS.get(kind, 0) + b) * WB
                    src = A[name][:, :, c:c + WB]
                    dst = slot.rearrange("p (k n) -> p k n", k=KT)
                sp.dma_start(dst, src).then_inc(weight_in[n % NW], 16)

            for n in range(len(BLOCKS)):
                load_weights(n)
                if n == 2:
                    sp.dma_start(cols("x", 0), A["x_t0"]).then_inc(x_in, 16)
                    sp.dma_start(state_pool, A["state_pool_t"]).then_inc(state_in, 16)
                    sp.dma_start(state_conv, A["state_conv_t"]).then_inc(state_in, 16)
                    sp.dma_start(state_lru, A["state_lru_t"]).then_inc(state_in, 16)
                if BLOCKS[n][0] == ("xb", 1, 0):
                    sp.wait_ge(ready["tok"], nth(("tok", 1, 3)))
                    sp.dma_start(cols("x", 1), A["x_t1"]).then_inc(x_in, 16)

            sp.wait_ge(tails, 2 * 4)
            sp.dma_start(A["conv_p"], conv_tail[:, :, :]).then_inc(out_done, 16)
            sp.dma_start(A["pool_p"], pool_tail[:, :, :]).then_inc(out_done, 16)
            sp.dma_start(A["lru_p"], lru_tail[:, :]).then_inc(out_done, 16)
            for t in range(1, TILES):
                sp.wait_ge(yready, t + 1)
                sp.dma_start(A["y_prompt"][(t - 1) * P:t * P, :], h2_rows(t)).then_inc(out_done, 16)
            sp.wait_ge(out_done, 16 * (3 + 4 + 4))

        @block.gpsimd
        def _(pool):
            nc.gpsimd.memset(zeros[:, :], 0.0)
            nc.gpsimd.memset(ones[:, :], 1.0).then_inc(zeros_done, 1)
            pool.dma_start(final_norm[:, :], A["final_norm"].broadcast_to([P, D])).then_inc(norm_in, 16)

            def fetch_step(t, i, par, number):
                nc.gpsimd.tensor_copy(step_idx[:, par, :], idx_of(t)[:, bass.ds(i * TOPK, TOPK)]).then_inc(idx_copied, 1)
                pool.wait_ge(idx_copied, number + 1)
                for rows, slots, free, landed, table in ((u_rows, NU, u_free, u_in, A["expert_u"]),
                                                         (v_rows, NV, v_free, v_in, A["expert_v"])):
                    for k in range(TOPK):
                        pool.wait_ge(free, 1)
                        pool.sem_inc(free, -1)
                        pool.indirect_dma_start(
                            out=rows[:, k % slots, :], out_offset=None, in_=table,
                            in_offset=bass.IndirectOffsetOnAxis(ap=step_idx[:, par, k:k + 1], axis=0),
                        ).then_inc(landed[k % slots], 16)

            for kind, t, i in SCHEDULE:
                if kind == "step":
                    if i == 0:
                        pool.wait_ge(idx_done, t + 1)
                    fetch_step(t, i, i % 2, STEP0[t] + i)
                if kind == "steps":
                    pool.wait_ge(idx_done, t + 1)
                    with pool.Fori(0, TILE_STEPS[t] // 2) as pair:
                        for par in range(2):
                            fetch_step(t, pair * 2 + par, par, pair * 2 + (STEP0[t] + par))

        @block.tensor
        def _(pe):
            done = [0]

            def begin(product):
                n = NUMBER[product]
                assert n == done[0]
                done[0] += 1
                if n >= NBANK:
                    old = PRODUCTS[n - NBANK]
                    pe.wait_ge(taken[old[0]], nth(old))
                return banks[n % NBANK]

            def block_of(unit):
                n = BLOCK_NO[unit]
                seen = sum(16 * (1 + (u[0] == "rgig")) for m, (u, _) in enumerate(BLOCKS[:n + 1]) if m % NW == n % NW)
                pe.wait_ge(weight_in[n % NW], seen)
                return weights[:, n % NW, :]

            def finish(ins, product):
                ins.then_inc(ready[product[0]], 1)

            def ada():
                pe.wait_ge(silu_done, 1)
                for i in range(24):
                    w = block_of(("ada", 0, i)).rearrange("p (k n) -> p k n", k=KT)
                    bank = begin(("ada", 0, i))
                    for k in range(KT):
                        ins = nc.tensor.matmul(bank[0:NR, 0:WB], silu_c[:, k, :], w[:, k, :], start=k == 0, stop=k == KT - 1)
                    finish(ins, ("ada", 0, i))
                bank = begin(("modT", 0, 0))
                pe.wait_ge(const_in, 16 * N_CONST)
                pe.wait_ge(taken["ada"], 20)
                for j in range(5 * KT):
                    ins = nc.tensor.transpose(bank[:, j * NR:(j + 1) * NR], mod_rows[:, j * P:(j + 1) * P], ident[0:NR, 0:NR])
                finish(ins, ("modT", 0, 0))

            def norm(g, which):
                n = sizes(g)[2]
                product = (("ss1", "ss2")[which], g, 0)
                sq = cols("pool", g)
                bank = begin(product)
                pe.wait_ge(zeros_done, 1)
                pe.wait_ge(square_done, 2 * g + which + 1)
                for k in range(KT):
                    ins = nc.tensor.matmul(bank[:, 0:n], ones[:, :], sq[:, k, :], start=k == 0, stop=k == KT - 1)
                finish(ins, product)

            def columns(kind, g, b):
                n = sizes(g)[2]
                w = block_of((kind, g, b)).rearrange("p (k n) -> p k n", k=KT)
                src = cols({"bb": "gy", "ba": "pool", "out": "gb"}.get(kind, "h"), g)
                if kind in ("xb", "q") and b == 0:
                    m = 2 * g + (kind == "q") + 1
                    pe.wait_ge(h_prompt, KT * m)
                    pe.wait_ge(h_sample, m)
                if kind == "ba" and b == 0:
                    pe.wait_ge(taken["mix"], nth(("mix", g, 7)))
                if kind == "bb" and b == 0:
                    pe.wait_ge(gy_done, g + 1)
                if kind == "out" and b == 0:
                    pe.wait_ge(taken["bb"], nth(("bb", g, 7)))
                for j in range(2):
                    product = (kind, g, 2 * b + j)
                    bank = begin(product)
                    for k in range(KT):
                        ins = nc.tensor.matmul(bank[:, 0:n], w[:, k, j * P:(j + 1) * P], src[:, k, :], start=k == 0, stop=k == KT - 1)
                    finish(ins, product)

            def lru_gates(g):
                n = sizes(g)[2]
                w = block_of(("rgig", g, 0)).rearrange("p (a h n) -> p a h n", a=2, h=HEADS)
                xc = cols("xc", g)
                for c in range(KT):
                    pe.wait_ge(conv_done, g * KT + c + 1)
                    for a in range(2):
                        product = ("rgig", g, 2 * c + a)
                        bank = begin(product)
                        finish(nc.tensor.matmul(bank[:, 0:n], w[:, a, c, :], xc[:, c, :], start=True, stop=True), product)

            def mix(g):
                n = sizes(g)[2]
                w = block_of(("mix", g, 0)).rearrange("p (g k n) -> p g k n", g=4, k=2)
                pooled = cols("i", g)
                for q in range(4):
                    pe.wait_ge(pooled_done, g * 4 + q + 1)
                    for j in range(2):
                        product = ("mix", g, 2 * q + j)
                        bank = begin(product)
                        for k in range(2):
                            ins = nc.tensor.matmul(bank[:, 0:n], w[:, q, k, j * P:(j + 1) * P], pooled[:, 2 * q + k, :], start=k == 0, stop=k == 1)
                        finish(ins, product)

            def first_col(t, samples):
                return samples if t == 1 else (t - 2) * P

            def token_rows(t):
                g = int(t >= 2)
                for i in range(4):
                    product = ("tok", t, i)
                    src = cols(("h", "x")[i // 2], g)
                    bank = begin(product)
                    if i == 0:
                        m = 2 * g + 2
                        pe.wait_ge(h_prompt, KT * m)
                        pe.wait_ge(h_sample, m)
                    for j in range(4):
                        k = 4 * (i % 2) + j
                        if t:
                            lo = first_col(t, NS)
                            tile = src[:, k, lo:lo + P]
                        else:
                            tile = h_twice[:, k, :] if i < 2 else src[:, k, 0:NS]
                        ins = nc.tensor.transpose(bank[0:tile.shape[1], j * P:(j + 1) * P], tile, ident[:, :])
                    finish(ins, product)

            def scores(t):
                g = int(t >= 2)
                keys = block_of(("keys", g, 0)).rearrange("p (h n) -> p h n", h=2 * HEADS)
                q = queries(g)
                lo = first_col(t, P) if t else 0
                pe.wait_ge(taken["q"], nth(("q", g, 15)))
                for i in range(4):
                    product = ("score", t, i)
                    bank = begin(product)
                    for j in range(4):
                        ins = nc.tensor.matmul(bank[:, j * P:(j + 1) * P], q[:, 4 * i + j, lo:lo + P], keys[:, 4 * i + j, :], start=True, stop=True)
                    finish(ins, product)

            def rows_of(t):
                return NS if t == 0 else P

            def open_sum(t, first):
                m = rows_of(t)
                if first:
                    pe.wait_ge(norm_in, 16)
                    if t:
                        pe.wait_ge(v_read, t)
                for j in range(2):
                    ins = nc.tensor.matmul(v_sum[0:m, j * 512:(j + 1) * 512], zeros[:, 0:m], final_norm[0:1, 0:512], start=first, stop=not first)
                if not first:
                    ins.then_inc(v_tile, 1)

            def sum_step(t, number):
                m = rows_of(t)
                for k in range(TOPK):
                    pe.wait_ge(v_in[k % NV], number * (16 * TOPK // NV) + 16 * (k // NV + 1))
                    pe.wait_ge(diag_done, number * TOPK + (k + 1))
                    nc.tensor.matmul(v_sum[0:m, 0:512], diag[:, k % ND, 0:m], v_rows[:, k % NV, 0:512], start=False, stop=False).then_inc(v_begun, 1)
                    nc.tensor.matmul(v_sum[0:m, 512:D], diag[:, k % ND, 0:m], v_rows[:, k % NV, 512:D], start=False, stop=False).then_inc(v_free, 1)

            for kind, g, b in SCHEDULE:
                if kind == "ada":
                    ada()
                elif kind == "norm":
                    norm(g, b)
                elif kind in COLS:
                    columns(kind, g, b)
                elif kind == "rgig":
                    lru_gates(g)
                elif kind == "mix":
                    mix(g)
                elif kind == "tok":
                    token_rows(g)
                elif kind == "topk":
                    scores(g)
                elif kind == "step":
                    if b == 0:
                        open_sum(g, True)
                    sum_step(g, STEP0[g] + b)
                elif kind == "steps":
                    open_sum(g, True)
                    with pe.Fori(0, TILE_STEPS[g]) as i:
                        sum_step(g, i + STEP0[g])
                elif kind == "final":
                    open_sum(g, False)
                    for i in range(2):
                        bank = begin(("g2", g, i))
                        pe.wait_ge(taken["ada"], 24)
                        finish(nc.tensor.matmul(bank[:, 0:512], select[:, int(g > 0), :], g2_rows[:, i * 512:(i + 1) * 512], start=True, stop=True), ("g2", g, i))

        @block.scalar
        def _(act):
            for dst, name in ((vecs, "vecs"), (ident, "ident"), (ident2, "ident2"), (select, "select"), (inv_count, "inv_count"), (iota16, "iota16")):
                act.dma_start(dst[:], A[name]).then_inc(const_in, 16)
            act.wait_ge(c_in, 16)
            nc.scalar.activation(silu_c[:, :, :], c_t[:, :, :], ACT.Silu).then_inc(silu_done, 1)
            act.wait_ge(centered, 1)
            nc.scalar.activation(sp_tmp[:, 1, :], sp_tmp[:, 0, :], ACT.Exp).then_inc(exp_done, 1)
            selfs = [0]

            def linked(ins):
                ins.then_inc(act_self, 1)
                selfs[0] += 1
                act.wait_ge(act_self, selfs[0])

            def take(product):
                act.wait_ge(ready[product[0]], nth(product))
                return banks[NUMBER[product] % NBANK]

            def norm(g, which):
                s, p, n = sizes(g)
                x, h, sq = cols("x", g), cols("h", g), cols("pool", g)
                if which == 0:
                    act.wait_ge(x_in, 16 * (g + 1))
                    if g:
                        act.wait_ge(idx_done, 2)
                else:
                    act.wait_ge(taken["out"], nth(("out", g, 7)))
                nc.scalar.activation(sq, x, ACT.Square).then_inc(square_done, 1)
                act.wait_ge(ms_done, 2 * g + which + 1)
                nc.scalar.activation(rstd[:, 0:n], ms[:, 0:n], ACT.Sqrt).then_inc(std_done, 1)
                act.wait_ge(coef_done, 1)
                act.wait_ge(h_scaled, 2 * g + which + 1)
                for k in range(KT):
                    nc.scalar.activation(h[:, k, s:n], h[:, k, s:n], ACT.Identity, scale=coef[:, which, k, SB:NR],
                                         bias=mod_t[:, 24 * which + k, SB:NR]).then_inc(h_prompt, 1)

            def columns(kind, g, b):
                s, p, n = sizes(g)
                for c in (2 * b, 2 * b + 1):
                    product = (kind, g, c)
                    if kind in ("bb", "ba", "out"):
                        continue
                    bank = take(product)
                    if kind == "xb":
                        smp, prm = conv_ext(g)
                        if c == 0 and g:
                            act.wait_ge(taken["bb"], nth(("bb", g - 1, 7)))
                        if s:
                            nc.scalar.activation(smp[:, c, :, CB:], bank[:, 0:NS].rearrange("p (b t) -> p b t", b=SB), ACT.Copy)
                        nc.scalar.activation(prm[:, c, CB:], bank[:, s:n], ACT.Copy).then_inc(taken[kind], 1)
                    elif kind == "u":
                        rows, smp, prm = pool_ext(g)
                        if c == 0:
                            act.wait_ge(scan_done, g + 1)
                        if s:
                            nc.scalar.activation(smp[:, c, :, PB:], bank[:, 0:NS].rearrange("p (b t) -> p b t", b=SB), ACT.Copy)
                        nc.scalar.activation(prm[:, c, PB:], bank[:, s:n], ACT.Copy).then_inc(taken[kind], 1)
                    elif kind == "yb":
                        nc.scalar.activation(cols("gy", g)[:, c, :], bank[:, 0:n], ACT.Gelu_apprx_tanh).then_inc(taken[kind], 1)
                    elif kind == "mg":
                        if c == 0:
                            act.wait_ge(scan_done, g + 1)
                        if c == 8:
                            act.wait_ge(pooled_done, 4 * (g + 1))
                        dst = cols(("conv", "gb")[c // 8], g)[:, c % 8, :]
                        nc.scalar.activation(dst, bank[:, 0:n], ACT.Sigmoid, bias=vec(("b_gate_a", "b_gate_b")[c // 8])[:, c % 8:c % 8 + 1]).then_inc(taken[kind], 1)
                    elif kind == "q":
                        q = queries(g)
                        if s:
                            nc.scalar.activation(q[:, c, 0:NS], bank[:, 0:NS], ACT.Copy)
                        at = NS if s else 0
                        nc.scalar.activation(q[:, c, at:], bank[:, 0:n], ACT.Copy).then_inc(taken[kind], 1)

            def lru_gates(g):
                n = sizes(g)[2]
                for c in range(KT):
                    for a, (dst, bias) in enumerate((("conv", "b_rg"), ("i", "b_ig"))):
                        bank = take(("rgig", g, 2 * c + a))
                        nc.scalar.activation(cols(dst, g)[:, c, :], bank[:, 0:n], ACT.Sigmoid, bias=vec(bias)[:, c:c + 1]).then_inc(taken["rgig"], 1)

            def lru(g):
                r = cols("conv", g)
                act.wait_ge(taken["rgig"], nth(("rgig", g, 15)))
                for c in range(KT):
                    nc.scalar.activation(r[:, c, :], r[:, c, :], ACT.Tanh, scale=sp4[:, c:c + 1]).then_inc(tanh_done, 1)
                act.wait_ge(tanh_done, KT * (g + 1))
                nc.scalar.activation(cols("pool", g), r, ACT.Sqrt).then_inc(sqrt_done, 1)

            def mix(g):
                n = sizes(g)[2]
                z = cols("pool", g)
                for c in range(KT):
                    bank = take(("mix", g, c))
                    if c == 0 and g == 0:
                        pass
                    nc.scalar.activation(z[:, c, :], bank[:, 0:n], ACT.Copy, scale=vec("pool_scale")[:, c:c + 1]).then_inc(taken["mix"], 1)

            def token_rows(t):
                for i in range(4):
                    bank = take(("tok", t, i))
                    if i == 0 and t == 0:
                        act.wait_ge(scan_done, 1)
                        act.wait_ge(pooled_done, 4)
                        act.wait_ge(out_done, 16 * 3)
                    if i == 0 and t == 2:
                        act.wait_ge(taken["ba"], nth(("ba", 1, 7)))
                    dst = (h2_rows, x1_rows)[i // 2](t)
                    m = NS if t == 0 and i >= 2 else P
                    nc.scalar.activation(dst[0:m, (i % 2) * 512:(i % 2 + 1) * 512], bank[0:m, :], ACT.Copy).then_inc(taken["tok"], 1)

            def softmax_exp(t):
                act.wait_ge(centered, t + 2)
                nc.scalar.activation(exps, exps, ACT.Exp).then_inc(exp_done, 1)

            def diagonals(t, number, first):
                m = NS if t == 0 else P
                act.wait_ge(dots_done, number + 1)
                nc.scalar.activation(gelus[:, :], dots[:, :], ACT.Gelu_apprx_tanh).then_inc(gelu_done, 1)
                act.wait_ge(wts_done, number + 1)
                for k in range(TOPK):
                    if not (first and k < ND):
                        act.wait_ge(v_begun, number * TOPK + (k + 2 - ND))
                    src = ident2[:, :] if t == 0 else ident[:, :]
                    nc.scalar.activation(diag[:, k % ND, 0:m], src, ACT.Copy, scale=wts[:, k:k + 1]).then_inc(diag_done, 1)

            def final(t):
                m = NS if t == 0 else P
                y = h2_rows(t)[0:m, :]
                act.wait_ge(v_tile, t + 1)
                nc.scalar.activation(y, v_sum[0:m, :], ACT.Copy).then_inc(v_read, 1)
                act.wait_ge(yfin, t + 1)
                nc.scalar.activation(x1_rows(t)[0:m, :], y, ACT.Square, accum_out=fin[0:m, 0:1]).then_inc(ysq, 1)
                act.wait_ge(ymean, t + 1)
                nc.scalar.activation(fin[0:m, 2:3], fin[0:m, 1:2], ACT.Sqrt).then_inc(ystd, 1)

            for kind, g, b in SCHEDULE:
                if kind == "ada":
                    bank = take(("modT", 0, 0))
                    nc.scalar.activation(mod_t[:, :, :].rearrange("p a r -> p (a r)"), bank[:, 0:5 * KT * NR], ACT.Copy).then_inc(taken["modT"], 1)
                elif kind == "norm":
                    norm(g, b)
                elif kind in COLS:
                    columns(kind, g, b)
                    if kind == "xb" and (g, b) == (0, 3):
                        act.wait_ge(tails, 1)
                        act.dma_start(A["conv_s"], conv_s[:, :, :, :]).then_inc(out_done, 16)
                    if kind == "mg" and (g, b) == (0, 7):
                        act.wait_ge(tails, 4)
                        act.dma_start(A["lru_s"], lru_s[:, :, :]).then_inc(out_done, 16)
                        act.dma_start(A["pool_s"], pool_s).then_inc(out_done, 16)
                elif kind == "rgig":
                    lru_gates(g)
                elif kind == "lru":
                    lru(g)
                elif kind == "mix":
                    mix(g)
                elif kind == "tok":
                    token_rows(g)
                elif kind == "topk":
                    softmax_exp(g)
                elif kind == "step":
                    diagonals(g, STEP0[g] + b, STEP0[g] + b == 0)
                elif kind == "steps":
                    with act.Fori(0, TILE_STEPS[g]) as i:
                        diagonals(g, i + STEP0[g], False)
                elif kind == "final":
                    final(g)
                    if g == 0:
                        act.wait_ge(yready, 1)
                        act.dma_start(A["y_sample"], h2_rows(0)[0:NS, :]).then_inc(out_done, 16)

        @block.vector
        def _(dve):
            V = nc.vector
            steps = [0]
            counts = {}

            def link(ins):
                steps[0] += 1
                ins.then_inc(dve_step, 1)
                dve.wait_ge(dve_step, steps[0])

            def mark(ins, s, n):
                ins.then_inc(s, 1)
                dve.wait_ge(s, n)

            def take(product):
                dve.wait_ge(ready[product[0]], nth(product))
                return banks[NUMBER[product] % NBANK]

            def softplus():
                z, s, q, r = (sp_tmp[:, i, :] for i in range(1, 5))
                dve.wait_ge(exp_done, 1)
                link(V.tensor_scalar_add(s, z, 2.0))
                link(V.reciprocal(q, s))
                link(V.tensor_tensor(s, z, q, ALU.mult))
                link(V.tensor_tensor(q, s, s, ALU.mult))
                link(V.tensor_scalar(r, q, 1.0 / 17, None, ALU.mult))
                for odd in (15, 13, 11, 9, 7, 5, 3):
                    link(V.scalar_tensor_tensor(out=r, in0=r, scalar=1.0 / odd, in1=q, op0=ALU.add, op1=ALU.mult))
                link(V.scalar_tensor_tensor(out=r, in0=r, scalar=1.0, in1=s, op0=ALU.add, op1=ALU.mult))
                link(V.tensor_scalar(z, vec("lru_lambda"), -1.0, 0.0, ALU.mult, ALU.max))
                link(V.scalar_tensor_tensor(out=z, in0=r, scalar=2.0, in1=z, op0=ALU.mult, op1=ALU.add))
                V.tensor_scalar(sp4[:, :], z, 4.0, None, ALU.mult).then_inc(coef_done, 1)

            def ada():
                dve.wait_ge(const_in, 16 * N_CONST)
                lam = vec("lru_lambda")
                link(V.tensor_scalar(sp_tmp[:, 0, :], lam, -1.0, None, ALU.mult))
                V.tensor_tensor(sp_tmp[:, 0, :], sp_tmp[:, 0, :], lam, ALU.min).then_inc(centered, 1)
                V.memset(dots[:, :], 0.0).then_inc(u_free, NU)
                V.memset(gelus[:, :], 0.0).then_inc(v_free, NV)
                dve.wait_ge(bias_in, 16)
                for i in range(24):
                    bank = take(("ada", 0, i))
                    dst = mod_rows[:, i * WB:(i + 1) * WB] if i < 20 else g2_rows[:, (i - 20) * WB:(i - 19) * WB]
                    V.tensor_tensor(dst, bank[0:NR, 0:WB], b_ada[:, i * WB:(i + 1) * WB], ALU.add).then_inc(taken["ada"], 1)
                softplus()
                dve.wait_ge(taken["modT"], 1)
                for which in range(2):
                    scale = mod_t[:, 8 + 24 * which:16 + 24 * which, :]
                    link(V.tensor_scalar_add(coef[:, which, :, :], scale, 1.0))
                    norm_w = vec(("norm1", "norm2")[which]).rearrange("p (k o) -> p k o", o=1).broadcast_to([P, KT, NR])
                    ins = V.tensor_tensor(coef[:, which, :, :], coef[:, which, :, :], norm_w, ALU.mult)
                    mark(ins, coef_done, 2 + which)

            def over_time(view):
                return view.rearrange("p k (b o) -> p k b o", o=1).broadcast_to([P, view.shape[1], SB, ST])

            def norm(g, which):
                s, p, n = sizes(g)
                m = 2 * g + which
                x, h = cols("x", g), cols("h", g)
                bank = take((("ss1", "ss2")[which], g, 0))
                V.tensor_scalar(ms[:, 0:n], bank[:, 0:n], 1.0 / D, EPS, ALU.mult, ALU.add).then_inc(taken[("ss1", "ss2")[which]], 1)
                dve.wait_ge(taken[("ss1", "ss2")[which]], g + 1)
                dve.sem_inc(ms_done, 1)
                dve.wait_ge(std_done, m + 1)
                link(V.reciprocal(rstd[:, 0:n], rstd[:, 0:n]))
                r = rstd[:, 0:n].rearrange("p (o n) -> p o n", o=1).broadcast_to([P, KT, n])
                dve.wait_ge(x_in, 16 * (g + 1))
                mark(V.tensor_tensor(h, x, r, ALU.mult), h_scaled, m + 1)
                if s:
                    hs = by_seq(h)
                    link(V.tensor_tensor(hs, hs, over_time(coef[:, which, :, 0:SB]), ALU.mult))
                    link(V.tensor_tensor(hs, hs, over_time(mod_t[:, 24 * which:24 * which + 8, 0:SB]), ALU.add))
                    if which:
                        twice = h[:, :, 0:NS].rearrange("p k (o n) -> p k o n", o=1).broadcast_to([P, KT, 2, NS])
                        link(V.tensor_copy(h_twice.rearrange("p k (o n) -> p k o n", o=2), twice))
                    dve.sem_inc(h_sample, 1)
                else:
                    dve.sem_inc(h_sample, 1)
                if which == 0:
                    smp, prm = conv_ext(g)
                    rows, psmp, pprm = pool_ext(g)
                    if g == 0:
                        dve.wait_ge(state_in, 48)
                        dve.wait_ge(ready["modT"], 1)
                        link(V.tensor_copy(smp[:, :, :, 0:CB], state_conv))
                        link(V.memset(prm[:, :, 0:CB], 0.0))

            def conv(g, b):
                s, p, n = sizes(g)
                smp, prm = conv_ext(g)
                xc = cols("xc", g)
                if g and b == 0:
                    link(V.tensor_copy(prm[:, :, 0:CB], conv_tail[:, :, :]))
                for c in (2 * b, 2 * b + 1):
                    dve.wait_ge(taken["xb"], nth(("xb", g, c)))
                    parts = [(xc[:, c, s:n], lambda t: prm[:, c, t:t + p])]
                    if s:
                        parts.append((by_seq(xc)[:, c], lambda t: smp[:, c, :, t:t + ST]))
                    for out, tap in parts:
                        V.tensor_scalar(out, tap(0), vec("conv_w0")[:, c:c + 1], vec("conv_b")[:, c:c + 1], ALU.mult, ALU.add).then_inc(dve_step, 1)
                        steps[0] += 1
                    for t in range(1, CW):
                        dve.wait_ge(dve_step, steps[0])
                        for out, tap in parts:
                            V.scalar_tensor_tensor(out=out, in0=tap(t), scalar=vec(f"conv_w{t}")[:, c:c + 1], in1=out, op0=ALU.mult, op1=ALU.add).then_inc(dve_step, 1)
                            steps[0] += 1
                    dve.wait_ge(dve_step, steps[0])
                    if s:
                        link(V.tensor_copy(conv_s[:, c, :, :], smp[:, c, :, ST:]))
                    V.tensor_copy(conv_tail[:, c, :], prm[:, c, p:]).then_inc(conv_done, 1)
                if b == 3:
                    dve.wait_ge(conv_done, KT * (g + 1))
                    dve.sem_inc(tails, 1)

            def lru(g):
                s, p, n = sizes(g)
                a, bx, xc, root, rc = cols("conv", g), cols("i", g), cols("xc", g), cols("pool", g), cols("gb", g)
                dve.wait_ge(taken["rgig"], nth(("rgig", g, 15)))
                link(V.tensor_tensor(bx, bx, xc, ALU.mult))
                if g == 0:
                    link(V.tensor_copy(bx_first[:, :], bx[:, :, s]))
                dve.wait_ge(sqrt_done, g + 1)
                link(V.tensor_scalar_add(rc, a, 1.0))
                link(V.reciprocal(rc, rc))
                link(V.scalar_tensor_tensor(out=bx, in0=bx, scalar=2.0, in1=root, op0=ALU.mult, op1=ALU.mult))
                link(V.tensor_tensor(bx, bx, rc, ALU.mult))
                link(V.tensor_scalar(a, rc, 2.0, -1.0, ALU.mult, ALU.add))
                if g == 0:
                    link(V.tensor_copy(bx[:, :, s], bx_first[:, :]))
                    a0, b0 = by_seq(a)[:, :, :, 0], by_seq(bx)[:, :, :, 0]
                    link(V.tensor_tensor(lru_s[:, :, :], a0, state_lru, ALU.mult))
                    link(V.tensor_tensor(b0, b0, lru_s[:, :, :], ALU.add))
                    link(V.memset(a0, 0.0))
                else:
                    link(V.tensor_tensor(lru_tail[:, :], lru_tail[:, :], a[:, :, 0], ALU.mult))
                    link(V.tensor_tensor(bx[:, :, 0], bx[:, :, 0], lru_tail[:, :], ALU.add))
                link(V.memset(a[:, :, s], 0.0))
                flat = [arena[:, place[x]:place[x] + KT * n] for x in ("xc", "conv", "i")]
                link(V.tensor_tensor_scan(out=flat[0], data0=flat[1], data1=flat[2], initial=0.0, op0=ALU.mult, op1=ALU.add))
                if s:
                    link(V.tensor_copy(lru_s[:, :, :], by_seq(xc)[:, :, :, ST - 1]))
                link(V.tensor_copy(lru_tail[:, :], xc[:, :, n - 1]))
                dve.sem_inc(tails, 1)
                dve.sem_inc(scan_done, 1)
                dve.wait_ge(taken["yb"], nth(("yb", g, 7)))
                V.tensor_tensor(cols("gy", g), cols("gy", g), xc, ALU.mult).then_inc(gy_done, 1)
                rows, smp, prm = pool_ext(g)
                if g == 0:
                    link(V.tensor_copy(smp[:, :, :, 0:PB], state_pool))
                    link(V.memset(prm[:, :, 0:PB], 0.0))
                else:
                    link(V.tensor_copy(prm[:, :, 0:PB], pool_tail[:, :, :]))

            def pooling(g, q):
                s, p, n = sizes(g)
                rows, smp, prm = pool_ext(g)
                w = rows.shape[2]
                pooled = cols("i", g)
                two = slice(2 * q, 2 * q + 2)
                dve.wait_ge(taken["u"], nth(("u", g, 2 * q + 1)))
                half = 2 * w
                sums = [region("gb", NB)[:, i * half:(i + 1) * half].rearrange("p (k w) -> p k w", k=2) for i in range(2)]
                src, lag = rows[:, two, :], 1
                for level in range(q + 1):
                    dst = sums[level % 2]
                    lo = 2 * lag - 1
                    link(V.tensor_tensor(dst[:, :, lo:w], src[:, :, lo:w], src[:, :, lo - lag:w - lag], ALU.add))
                    src, lag = dst, 2 * lag
                base = w - p - PB
                window = float(WINDOWS[q])
                V.scalar_tensor_tensor(out=pooled[:, two, s:n], in0=src[:, :, base + PB:w], scalar=1.0 / window,
                                       in1=prm[:, two, PB:], op0=ALU.mult, op1=ALU.subtract).then_inc(dve_step, 1)
                steps[0] += 1
                if s:
                    for c in range(2):
                        in0 = src[:, c, 0:base].rearrange("p (b t) -> p b t", b=SB)[:, :, PB:]
                        link(V.scalar_tensor_tensor(out=by_seq(pooled)[:, 2 * q + c], in0=in0, scalar=1.0 / window,
                                                    in1=smp[:, 2 * q + c, :, PB:], op0=ALU.mult, op1=ALU.subtract))
                    tmp = small[:, 0:32].rearrange("p (k t) -> p k t", k=2)
                    inv = inv_count[:, q:q + 1, :].broadcast_to([P, 2, 16])
                    link(V.tensor_tensor(tmp, src[:, :, base + PB:base + PB + 16], inv, ALU.mult))
                    link(V.tensor_tensor(pooled[:, two, s:s + 16], tmp, prm[:, two, PB:PB + 16], ALU.subtract))
                    link(V.tensor_copy(pool_s[:, two, :, :], smp[:, two, :, ST:]))
                link(V.tensor_copy(pool_tail[:, two, :], prm[:, two, p:]))
                dve.sem_inc(pooled_done, 1)
                if q == 3:
                    dve.sem_inc(tails, 2)

            def gated(kind, g, b):
                s, p, n = sizes(g)
                ga, gb, x = cols("conv", g), cols("gb", g), cols("x", g)
                for c in (2 * b, 2 * b + 1):
                    if kind == "ba" and c == 0:
                        dve.wait_ge(taken["mg"], nth(("mg", g, 15)))
                    bank = take((kind, g, c))
                    if kind == "ba":
                        V.tensor_tensor(ga[:, c, :], ga[:, c, :], bank[:, 0:n], ALU.mult).then_inc(taken[kind], 1)
                    elif kind == "bb":
                        link(V.tensor_tensor(gb[:, c, :], gb[:, c, :], bank[:, 0:n], ALU.mult))
                        dve.wait_ge(taken["ba"], nth(("ba", g, c)))
                        V.tensor_tensor(gb[:, c, :], gb[:, c, :], ga[:, c, :], ALU.add).then_inc(taken[kind], 1)
                    else:
                        if s:
                            gate = over_time(mod_t[:, 16 + c:17 + c, 0:SB])
                            tmp = small[:, 0:NS].rearrange("p (o b t) -> p o b t", o=1, b=SB)
                            link(V.tensor_tensor(tmp, bank[:, 0:NS].rearrange("p (o b t) -> p o b t", o=1, b=SB), gate, ALU.mult))
                            link(V.tensor_tensor(x[:, c, 0:NS], x[:, c, 0:NS], small[:, 0:NS], ALU.add))
                        V.scalar_tensor_tensor(out=x[:, c, s:n], in0=bank[:, s:n], scalar=mod_t[:, 16 + c, SB:NR], in1=x[:, c, s:n],
                                               op0=ALU.mult, op1=ALU.add).then_inc(taken[kind], 1)

            scratch_h, scratch_gb = region("h", NB), region("gb", NB)
            cand = scratch_h[:, 0:2048]
            less = scratch_gb[:, 0:2048]
            less4 = scratch_h[:, 2048:2560].rearrange("p (i n) -> p i n", i=4)
            top_v = scratch_h[:, 2560:2816].rearrange("p (h k) -> p h k", h=16)
            top_f = scratch_h[:, 2816:3072].rearrange("p (h k) -> p h k", h=16)
            best_v = scratch_gb[:, 2048:2176].rearrange("p (h k) -> p h k", h=8)
            part_f = [scratch_gb[:, 2176 + 128 * i:2304 + 128 * i] for i in range(2)]
            chosen = [scratch_gb[:, 2432 + 128 * i:2560 + 128 * i] for i in range(2)]
            sums8 = scratch_gb[:, 2688:2696]

            def batch(instructions):
                for ins in instructions:
                    ins.then_inc(dve_step, 1)
                    steps[0] += 1
                dve.wait_ge(dve_step, steps[0])

            def topk(t):
                if t == 0:
                    dve.wait_ge(ready["tok"], nth(("tok", 1, 3)))
                if t == 2:
                    dve.wait_ge(ready["tok"], nth(("tok", 4, 3)))
                for i in range(4):
                    bank = take(("score", t, i))
                    s = [bank[:, j * P:(j + 1) * P] for j in range(4)]
                    hp = range(4 * i, 4 * i + 4)
                    batch(V.max(top_v[:, h, 0:8], s[j]) for j, h in enumerate(hp))
                    batch(V.max_index(top_i[:, h, 0:8], top_v[:, h, 0:8], s[j]) for j, h in enumerate(hp))
                    batch(V.match_replace(less4[:, j, :], top_v[:, h, 0:8], s[j], LOWEST) for j, h in enumerate(hp))
                    dve.sem_inc(taken["score"], 1)
                    batch(V.max(top_v[:, h, 8:16], less4[:, j, :]) for j, h in enumerate(hp))
                    batch(V.max_index(top_i[:, h, 8:16], top_v[:, h, 8:16], less4[:, j, :]) for j, h in enumerate(hp))
                halves = top_v.rearrange("p (h a) k -> p h a k", a=2)
                first = halves[:, :, 0, :].rearrange("p h (k o) -> p h k o", o=1).broadcast_to([P, 8, 16, 16])
                second = halves[:, :, 1, :].rearrange("p h (o k) -> p h o k", o=1).broadcast_to([P, 8, 16, 16])
                grid = cand.rearrange("p (h k m) -> p h k m", h=8, k=16)
                grid2 = less.rearrange("p (h k m) -> p h k m", h=8, k=16)
                link(V.tensor_tensor(grid, first, second, ALU.add))
                c = [cand[:, 256 * h:256 * h + 256] for h in range(8)]
                l = [less[:, 256 * h:256 * h + 256] for h in range(8)]
                batch(V.max(best_v[:, h, 0:8], c[h]) for h in range(8))
                batch(V.max_index(best_j[:, h, 0:8], best_v[:, h, 0:8], c[h]) for h in range(8))
                batch(V.match_replace(l[h], best_v[:, h, 0:8], c[h], LOWEST) for h in range(8))
                batch(V.max(best_v[:, h, 8:16], l[h]) for h in range(8))
                batch(V.max_index(best_j[:, h, 8:16], best_v[:, h, 8:16], l[h]) for h in range(8))
                top = best_v[:, :, 0:1].broadcast_to([P, 8, 16])
                e3 = exps.rearrange("p (h k) -> p h k", h=8)
                if t:
                    dve.wait_ge(idx_done, t)
                V.tensor_tensor(e3, best_v, top, ALU.subtract).then_inc(centered, 1)
                bj = choice[:, 2, :].bitcast(U32)
                batch([V.tensor_scalar(part_u[:, 0, :], bj, 4, None, ALU.logical_shift_right),
                       V.tensor_scalar(part_u[:, 1, :], bj, 15, None, ALU.bitwise_and),
                       V.tensor_copy(top_f, top_i[:, :, :])])
                batch([V.tensor_copy(part_f[a], part_u[:, a, :]) for a in range(2)])
                tops = top_f.rearrange("p (h a) k -> p h a k", a=2)
                for a in range(2):
                    want = part_f[a].rearrange("p (h k o) -> p h k o", h=8, o=1).broadcast_to([P, 8, 16, 16])
                    numbers = iota16[:, :].rearrange("p (h k m) -> p h k m", h=1, k=1).broadcast_to([P, 8, 16, 16])
                    values = tops[:, :, a, :].rearrange("p h (o k) -> p h o k", o=1).broadcast_to([P, 8, 16, 16])
                    link(V.tensor_tensor(grid, numbers, want, ALU.is_equal))
                    link(V.tensor_tensor(grid2, grid, values, ALU.mult))
                    link(V.reduce_sum(chosen[a].rearrange("p (h k) -> p h k", h=8), grid2, axis=AX.X))
                link(V.scalar_tensor_tensor(out=chosen[0], in0=chosen[0], scalar=float(NKEYS), in1=chosen[1], op0=ALU.mult, op1=ALU.add))
                link(V.tensor_copy(idx_of(t), chosen[0]))
                dve.wait_ge(exp_done, t + 2)
                link(V.reduce_sum(sums8, e3, axis=AX.X))
                link(V.reciprocal(sums8, sums8))
                inv = sums8.rearrange("p (h o) -> p h o", o=1).broadcast_to([P, 8, 16])
                link(V.tensor_tensor(gsm_of(t).rearrange("p (h k) -> p h k", h=8), e3, inv, ALU.mult))
                if t == 0:
                    batch([V.tensor_copy(idx0[NS:P, 0, 0:64], idx0[NS:P, 0, 64:128]),
                           V.tensor_copy(gsm0[NS:P, 0, 0:64], gsm0[NS:P, 0, 64:128])])
                dve.sem_inc(idx_done, 1)

            def dot_step(t, i, number):
                h2 = h2_rows(t)
                for k in range(TOPK):
                    row = u_rows[:, k % NU, :]
                    dve.wait_ge(u_in[k % NU], number * (16 * TOPK // NU) + 16 * (k // NU + 1))
                    ins = V.tensor_tensor_reduce(out=row, in0=row, in1=h2, scale=1.0, scalar=0.0, op0=ALU.mult, op1=ALU.add,
                                                 accum_out=dots[:, k:k + 1])
                    ins.then_inc(u_free if k < TOPK - 1 else dots_done, 1)
                dve.wait_ge(dots_done, number + 1)
                dve.sem_inc(u_free, 1)
                dve.wait_ge(gelu_done, number + 1)
                V.tensor_tensor(wts[:, :], gelus[:, :], gsm_of(t)[:, bass.ds(i * TOPK, TOPK)], ALU.mult).then_inc(wts_done, 1)

            def final(t):
                m = NS if t == 0 else P
                y, x1 = h2_rows(t)[0:m, :], x1_rows(t)[0:m, :]
                dve.wait_ge(v_read, t + 1)
                for i in range(2):
                    bank = take(("g2", t, i))
                    half = slice(i * 512, (i + 1) * 512)
                    mark(V.tensor_tensor(y[:, half], y[:, half], bank[0:m, :], ALU.mult), taken["g2"], nth(("g2", t, i)))
                mark(V.tensor_tensor(y, y, x1, ALU.add), yfin, t + 1)
                dve.wait_ge(ysq, t + 1)
                link(V.tensor_scalar(fin[0:m, 1:2], fin[0:m, 0:1], 1.0 / D, EPS, ALU.mult, ALU.add))
                dve.sem_inc(ymean, 1)
                dve.wait_ge(ystd, t + 1)
                link(V.reciprocal(fin[0:m, 3:4], fin[0:m, 2:3]))
                if t == 0:
                    dve.wait_ge(norm_in, 16)
                V.scalar_tensor_tensor(out=y, in0=y, scalar=fin[0:m, 3:4], in1=final_norm[0:m, :], op0=ALU.mult, op1=ALU.mult).then_inc(yready, 1)

            for kind, g, b in SCHEDULE:
                if kind == "ada":
                    ada()
                elif kind == "norm":
                    norm(g, b)
                elif kind == "xb":
                    conv(g, b)
                elif kind == "lru":
                    lru(g)
                elif kind == "u":
                    pooling(g, b)
                elif kind in ("ba", "bb", "out"):
                    gated(kind, g, b)
                elif kind == "topk":
                    topk(g)
                elif kind == "step":
                    dot_step(g, b, STEP0[g] + b)
                elif kind == "steps":
                    with dve.Fori(0, TILE_STEPS[g]) as i:
                        dot_step(g, i, i + STEP0[g])
                elif kind == "final":
                    final(g)


OUTPUTS = {"y_prompt": (SEQ, D), "y_sample": (NS, D), "pool_p": (P, KT, PB), "conv_p": (P, KT, CB), "lru_p": (P, KT),
           "pool_s": (P, KT, SB, PB), "conv_s": (P, KT, SB, CB), "lru_s": (P, KT, SB)}


def kernel(x_prompt, x_sample, c_prompt, c_sample, state_pool, state_conv, state_lru, norm1, norm2, w_ada, b_ada,
           w_in, b_gate, pool_mix, pool_scale, conv_w, conv_b, w_rg, b_rg, w_ig, b_ig, lru_lambda, w_branch_a,
           w_branch_b, w_out, w_q, sub_keys, expert_u, expert_v, final_norm):
    import numpy as np
    import concourse.bacc as bacc
    from concourse.bass_utils import run_bass_kernel_spmd

    def features_first(a):
        a = np.asarray(a)
        return np.ascontiguousarray(np.moveaxis(a.reshape(a.shape[:-1] + (KT, P)), (-1, -2), (0, 1)))

    def rows(a):
        return np.asarray(a)[0]

    xs, xp = np.asarray(x_sample).reshape(NS, D), np.asarray(x_prompt)[0]
    vectors = [rows(norm1), rows(norm2), rows(pool_scale), rows(conv_b), rows(b_rg), rows(b_ig), rows(lru_lambda),
               *rows(conv_w), rows(b_gate)[:D], rows(b_gate)[D:]]
    n = np.arange(P)
    select = np.zeros((NR, 2, P), np.float32)
    select[n % NS // ST, 0, n] = 1.0
    select[SB, 1, :] = 1.0
    counts = np.minimum(np.arange(16)[None, :] + 1, np.array(WINDOWS)[:, None])
    arrays = {
        "x_t0": features_first(np.concatenate([xs, xp[:GROUP_P[0]]])),
        "x_t1": features_first(xp[GROUP_P[0]:]),
        "c_t": features_first(np.concatenate([np.asarray(c_sample), np.asarray(c_prompt)])),
        "state_pool_t": features_first(rows(state_pool)),
        "state_conv_t": features_first(rows(state_conv)),
        "state_lru_t": features_first(rows(state_lru)),
        "vecs": np.ascontiguousarray(np.stack([features_first(v) for v in vectors], axis=1)),
        "keys_t": np.ascontiguousarray(rows(sub_keys).reshape(2 * HEADS, NKEYS, P).transpose(2, 0, 1).reshape(P, -1)),
        "ident": np.eye(P, dtype=np.float32),
        "ident2": np.concatenate([np.eye(NS, dtype=np.float32)] * 2),
        "select": select,
        "inv_count": np.ascontiguousarray(np.broadcast_to((1.0 / counts).astype(np.float32), (P, len(WINDOWS), 16))),
        "iota16": np.ascontiguousarray(np.broadcast_to(np.arange(16, dtype=np.float32), (P, 16))),
        "b_ada": np.asarray(b_ada), "final_norm": np.asarray(final_norm).reshape(1, D),
        "w_ada": rows(w_ada), "w_in": rows(w_in), "w_branch_a": rows(w_branch_a), "w_branch_b": rows(w_branch_b),
        "w_out": rows(w_out), "w_q": rows(w_q), "pool_mix": rows(pool_mix), "w_rg": rows(w_rg), "w_ig": rows(w_ig),
        "expert_u": rows(expert_u), "expert_v": rows(expert_v),
    }
    nc = bacc.Bacc("TRN2", target_bir_lowering=False, num_devices=1)
    A, launched = {}, {}
    for name, a in arrays.items():
        a = np.ascontiguousarray(a)
        launched["in_" + name] = a
        A[name] = nc.dram_tensor("in_" + name, a.shape, mybir.dt.from_np(a.dtype), kind="ExternalInput").ap()
    for name, shape in OUTPUTS.items():
        A[name] = nc.dram_tensor("out_" + name, shape, F32, kind="ExternalOutput").ap()
    for name in ("w_ada", "w_in", "w_branch_a", "w_branch_b", "w_out", "w_q"):
        A[name] = A[name].rearrange("(k p) n -> p k n", p=P)
    A["pool_mix"] = A["pool_mix"].rearrange("g (k p) n -> p g k n", p=P)
    A["w_rg"], A["w_ig"] = (A[x].rearrange("h p n -> p h n") for x in ("w_rg", "w_ig"))
    trunk(nc, A)
    r = run_bass_kernel_spmd(nc, [launched], core_ids=[0]).results[0]

    def features_last(name):
        a = np.moveaxis(r["out_" + name], (0, 1), (-1, -2))
        return np.ascontiguousarray(a.reshape(a.shape[:-2] + (D,)))

    return (r["out_y_prompt"].reshape(1, SEQ, D), r["out_y_sample"].reshape(SB, ST, D),
            features_last("pool_p")[None, None], features_last("conv_p")[None, None], features_last("lru_p")[None, None],
            features_last("pool_s")[None], features_last("conv_s")[None], features_last("lru_s")[None])
```

```python
from contextlib import ExitStack

import concourse.bass as bass
from concourse import mybir

P = 128
D = 1024
KT = D // P
SEQ, SB, ST = 512, 8, 8
NS = SB * ST
NR = SB + 1
WINDOWS = (2, 4, 8, 16)
PB = max(WINDOWS) - 1
CW = 4
CB = CW - 1
HEADS, NKEYS, TOPK = 8, 128, 16
SLOTS = HEADS * TOPK
EPS = 1e-6
LOWEST = -3.0e38
GROUP_P = (128, 384)
GROUP_S = (NS, 0)
N_MAX = max(GROUP_P)
TILES = 5
TILE_STEPS = (4, 8, 8, 8, 8)
STEP0 = (0, 4, 12, 20, 28)
WB = 256
NW, NU, NV, NBANK = 3, 4, 8, 6
PAIRS = TOPK // 2
PEELED = 5
CHOICE_PLACES, DENSE_PLACES, TOK_PLACES = 26, 80, 84
VEC = ("norm1", "norm2", "pool_scale", "conv_b", "b_rg", "b_ig", "lru_lambda",
       "conv_w0", "conv_w1", "conv_w2", "conv_w3", "b_gate_a", "b_gate_b")

F32, U32 = mybir.dt.float32, mybir.dt.uint32
ALU, ACT, AX = mybir.AluOpType, mybir.ActivationFunctionType, mybir.AxisListType

PER = {"ada": 24, "modT": 1, "ss1": 1, "xb": 8, "rgig": 16, "yb": 8, "u": 8, "mix": 8, "mg": 16, "bb": 8,
       "ba": 8, "out": 8, "ss2": 1, "q": 16, "tok": 4, "score": 4, "g2": 2}
COLS = {"xb": 4, "u": 0, "yb": 8, "mg": 12, "bb": 0, "ba": 0, "out": 0, "q": 0}
GROUPED = {"rgig": ("rgig", 4), "mix": ("mix", 2), "tok": ("tok", 4), "keytop": ("score", 2), "final": ("g2", 2)}


def products_of(unit):
    kind, g, b = unit
    if kind == "norm":
        return [(("ss1", "ss2")[b], g, 0)]
    if kind in GROUPED:
        name, count = GROUPED[kind]
        return [(name, g, b * count + i) for i in range(count)]
    return [unit] if kind in PER else []


def group_tiles(g):
    return (0, 1) if g == 0 else (2, 3, 4)


def mixer_units(g):
    units = [("square", g, 0), ("norm", g, 0)] + [("xb", g, c) for c in range(8)] + [("yb", g, 0), ("yb", g, 1)]
    units += [("rgig", g, q) for q in range(4)]
    for q in range(4):
        units += [("yb", g, c) for c in range(2 + 2 * q, 4 + 2 * q) if c < 8] + [("lru", g, q)]
    units += [("u", g, c) for c in range(8)] + [("mg", g, c) for c in range(8)]
    units += [("mix", g, q) for q in range(4)] + [("mg", g, c) for c in range(8, 16)]
    units += [(k, g, c) for k in ("ba", "bb") for c in range(8)]
    for c in range(8):
        units += [("out", g, c), ("square", g, 1 + c)]
    return units + [("norm", g, 1)] + [("q", g, c) for c in range(16)]


def choice_units(t, z):
    return [("keytop", t, z), ("pairtop", t, z), ("number", t, z)]


def weight_of(unit):
    return {"ada": 0.5, "tok": 0.5, "keytop": 0.5, "rgig": 0.8, "mix": 0.8}.get(unit[0], float(len(products_of(unit))))


def spread(units, places, first, last):
    total, before, place = sum(max(weight_of(u), 0.01) for u in units), 0.0, first
    for unit in units:
        place = max(place, first + int(before * (last - first) / total))
        if sum(len(products_of(u)) for u in places[place] + [unit]) > NBANK:
            place += 1
        places[place].append(unit)
        before += max(weight_of(unit), 0.01)


def deal(units, places, first, last):
    for n, unit in enumerate(units):
        places[first + n * (last - first) // len(units)].append(unit)


def staggered(places, between):
    s, before = [], []
    for n, units in enumerate(places):
        assert sum(len(products_of(u)) for u in units) <= NBANK
        s += between(n, 0) + [("read",) + u for u in before] + [("make",) + u for u in units] + between(n, 1)
        before = units
    return s + [("read",) + u for u in before]


def schedule():
    start = [[("ada", 0, i)] for i in range(20)] + [[("modT", 0, 0)]] + [[u] for u in mixer_units(0)]
    start += [[("tok", t, 0)] for t in group_tiles(0)] + [[u] for u in choice_units(0, 0)]
    s = staggered(start, lambda n, after: []) + [("both", "dots", 0, 0)]
    steps = [(t, i) for t in group_tiles(0) for i in range(TILE_STEPS[t])]
    places = [[] for _ in range(PAIRS * len(steps))]
    deal(choice_units(0, 1) + choice_units(1, 0) + choice_units(1, 1), places, 0, CHOICE_PLACES)
    for i in range(4):
        places[2 * i + 1].append(("ada", 0, 20 + i))
    spread(mixer_units(1), places, CHOICE_PLACES, DENSE_PLACES)
    deal([("tok", t, 0) for t in group_tiles(1)], places, DENSE_PLACES, TOK_PLACES)
    deal(choice_units(2, 0), places, TOK_PLACES, PAIRS * (len(steps) - 1))
    deal(choice_units(2, 1), places, PAIRS * (len(steps) - 1), len(places))

    def pair_entries(steps):
        def between(n, after):
            t, i = steps[n // PAIRS]
            out = [(("pair", "sum")[after], "pair", t, (i, n % PAIRS))]
            if after and n % PAIRS == PAIRS - 1 and i == TILE_STEPS[t] - 1:
                out += [("both", "final", t, 0)]
            return out
        return between

    s += staggered(places, pair_entries(steps))
    for t in group_tiles(1):
        last = TILE_STEPS[t] - 1
        if t + 1 < TILES:
            steps = [(t, i) for i in range(PEELED)]
            places = [[] for _ in range(PAIRS * PEELED)]
            deal(choice_units(t + 1, 0) + choice_units(t + 1, 1), places, 0, len(places))
            s += staggered(places, pair_entries(steps)) + [("both", "loop", t, (PEELED, last))]
        else:
            s += [("both", "loop", t, (0, last))]
        s += staggered([[] for _ in range(PAIRS)], pair_entries([(t, last)]))
    return s


SCHEDULE = schedule()


PRODUCTS = [p for role, *unit in SCHEDULE if role in ("make", "both") for p in products_of(tuple(unit))]
NUMBER = {p: n for n, p in enumerate(PRODUCTS)}


def nth(product):
    kind, g, i = product
    return g * PER[kind] + i + 1


def weight_blocks():
    blocks = {}
    for role, *unit in SCHEDULE:
        kind, g, b = unit
        if role == "make" and (kind in COLS or kind in ("ada", "rgig", "mix", "keytop")):
            if kind in COLS:
                b = b // 2
            if kind in ("rgig", "mix"):
                b = 0
            blocks[kind, g, b] = products_of(tuple(unit))[-1]
    return list(blocks.items())


BLOCKS = weight_blocks()
BLOCK_NO = {unit: n for n, (unit, _) in enumerate(BLOCKS)}


def trunk(nc, A):
    ctx = ExitStack()
    with ctx:
        def sb(name, shape, dt=F32):
            return ctx.enter_context(nc.sbuf_tensor("t_" + name, shape, dt))

        def sem(name):
            return ctx.enter_context(nc.semaphore(name))

        CEXT = KT * (N_MAX + CB)
        UEXT = KT * (N_MAX + PB)
        NB = KT * N_MAX
        arena = sb("arena", [P, 6 * NB + CEXT + UEXT])
        at, place = 0, {}
        for name, size in (("x", NB), ("h", NB), ("xc", NB), ("gy", NB), ("conv", CEXT), ("i", NB), ("pool", UEXT),
                           ("gb", NB)):
            place[name] = at
            at += size

        def region(name, size):
            return arena[:, place[name]:place[name] + size]

        def cols(name, g):
            n = GROUP_S[g] + GROUP_P[g]
            return region(name, KT * n).rearrange("p (k n) -> p k n", k=KT)

        mod_rows = arena[0:NR, place["xc"]:place["xc"] + 5 * D]
        b_ada = arena[0:NR, place["conv"]:place["conv"] + 5 * D]
        weights = sb("weights", [P, NW, KT * WB])
        u_rows = sb("u_rows", [P, NU, D])
        v_rows = sb("v_rows", [P, NV, D])
        tok0 = sb("tok0", [P, 4, D])
        g2_rows = sb("g2_rows", [NR, D])
        final_norm = sb("final_norm", [P, D])
        vecs = sb("vecs", [P, len(VEC), KT])
        ident = sb("ident", [P, P])
        ident2 = sb("ident2", [P, NS])
        select = sb("select", [NR, 2, P])
        inv_count = sb("inv_count", [P, len(WINDOWS), 16])
        iota16 = sb("iota16", [P, 16])
        ones = sb("ones", [P, P])
        zeros = sb("zeros", [1, P])
        c_t = sb("c_t", [P, KT, NR])
        silu_c = sb("silu_c", [P, KT, NR])
        mod_t = sb("mod_t", [P, 5 * KT, NR])
        coef = sb("coef", [P, 2, KT, NR])
        sp4 = sb("sp4", [P, KT])
        minus_sp8 = sb("minus_sp8", [P, KT])
        sp_tmp = sb("sp_tmp", [P, 6, KT])
        small = sb("small", [P, NS])
        conv_tail = sb("conv_tail", [P, KT, CB])
        conv_s = sb("conv_s", [P, KT, SB, CB])
        pool_tail = sb("pool_tail", [P, KT, PB])
        lru_tail = sb("lru_tail", [P, KT])
        lru_s = sb("lru_s", [P, KT, SB])
        bx_first = sb("bx_first", [P, KT])
        idx0 = sb("idx0", [P, 2, SLOTS], U32)
        gsm0 = sb("gsm0", [P, 2, SLOTS])
        step_idx = sb("step_idx", [P, 2, 2, TOPK], U32)
        dots = sb("dots", [P, TOPK])
        gelus = sb("gelus", [P, TOPK])
        wts = sb("wts", [P, TOPK])
        fin = sb("fin", [P, 4])
        banks = [ctx.enter_context(nc.psum_tensor(f"bank{i}", [P, 512], F32)) for i in range(NBANK)]
        v_sum = ctx.enter_context(nc.psum_tensor("v_sum", [P, D], F32))

        state = tok0[:, 0:2, :].rearrange("p a d -> p (a d)")
        state_pool = state[:, 0:KT * SB * PB].rearrange("p (k b t) -> p k b t", k=KT, b=SB)
        s1 = KT * SB * PB
        state_conv = state[:, s1:s1 + KT * SB * CB].rearrange("p (k b t) -> p k b t", k=KT, b=SB)
        s2 = s1 + KT * SB * CB
        state_lru = state[:, s2:s2 + KT * SB].rearrange("p (k b) -> p k b", k=KT)
        pool_s = tok0[:, 2, 0:KT * SB * PB].rearrange("p (k b t) -> p k b t", k=KT, b=SB)

        ms, rstd = (region("gb", 2 * N_MAX)[:, i * N_MAX:(i + 1) * N_MAX] for i in range(2))
        h_twice = region("gb", 2 * N_MAX + KT * P)[:, 2 * N_MAX:].rearrange("p (k n) -> p k n", k=KT)
        choice = region("pool", 12 * SLOTS).rearrange("p (a s) -> p a s", s=SLOTS)
        top_i = choice[:, 0:2, :].bitcast(U32).rearrange("p a (h k) -> p (a h) k", k=TOPK)
        best_j = choice[:, 2, :].bitcast(U32).rearrange("p (h k) -> p h k", k=TOPK)
        part_u = choice[:, 3:5, :].bitcast(U32)
        exps = choice[:, 5, :]

        def idx_of(t):
            return idx0[:, t, :] if t < 2 else choice[:, 4 + t, :].bitcast(U32)

        def gsm_of(t):
            return gsm0[:, t, :] if t < 2 else choice[:, 7 + t, :]

        def vec(name):
            return vecs[:, VEC.index(name), :]

        def h2_rows(t):
            return tok0[:, t, :] if t < 2 else region("conv", NB)[:, (t - 2) * D:(t - 1) * D]

        def x1_rows(t):
            return tok0[:, 2 + t, :] if t < 2 else region("i", NB)[:, (t - 2) * D:(t - 1) * D]

        const_in, c_in, bias_in, norm_in, x_in, state_in = (sem(x) for x in (
            "const_in", "c_in", "bias_in", "norm_in", "x_in", "state_in"))
        weight_in = [sem(f"weight_in{i}") for i in range(NW)]
        ready = {k: sem(f"{k}_ready") for k in PER}
        taken = {k: sem(f"{k}_taken") for k in PER}
        silu_done, zeros_done, square_done, std_done, h_scaled, h_prompt, h_sample = (sem(x) for x in (
            "silu_done", "zeros_done", "square_done", "std_done", "h_scaled", "h_prompt", "h_sample"))
        ms_done, conv_done, sqrt_done, scan_done, gy_done, pooled_done, exp_done, centered = (
            sem(x) for x in ("ms_done", "conv_done", "sqrt_done", "scan_done", "gy_done",
                             "pooled_done", "exp_done", "centered"))
        dve_step, coef_done, idx_done, rates_done = (sem(x) for x in ("dve_step", "coef_done", "idx_done", "rates_done"))
        u_in = [sem(f"u_in{i}") for i in range(NU)]
        v_in = [sem(f"v_in{i}") for i in range(NV)]
        u_free, v_free, idx_copied, dots_done, gelu_done, wts_done, scaled_done, paired_done = (sem(x) for x in (
            "u_free", "v_free", "idx_copied", "dots_done", "gelu_done", "wts_done", "scaled_done", "paired_done"))
        v_tile, v_read, yfin, ysq, ymean, ystd, yready, tails, out_done = (sem(x) for x in (
            "v_tile", "v_read", "yfin", "ysq", "ymean", "ystd", "yready", "tails", "out_done"))

        N_CONST, N_NORM = 6, 1

        def sizes(g):
            return GROUP_S[g], GROUP_P[g], GROUP_S[g] + GROUP_P[g]

        def conv_ext(g):
            s, p, n = sizes(g)
            w = (s // ST) * (ST + CB) + p + CB
            rows = region("conv", KT * w).rearrange("p (k w) -> p k w", k=KT)
            smp = rows[:, :, 0:w - p - CB].rearrange("p k (b t) -> p k b t", t=ST + CB) if s else None
            return smp, rows[:, :, w - p - CB:w]

        def pool_ext(g):
            s, p, n = sizes(g)
            w = (s // ST) * (ST + PB) + p + PB
            rows = region("pool", KT * w).rearrange("p (k w) -> p k w", k=KT)
            smp = rows[:, :, 0:w - p - PB].rearrange("p k (b t) -> p k b t", t=ST + PB) if s else None
            return rows, smp, rows[:, :, w - p - PB:w]

        def queries(g):
            n = sizes(g)[2] + GROUP_S[g]
            return arena[:, place["xc"]:place["xc"] + 2 * KT * n].rearrange("p (k n) -> p k n", k=2 * KT)

        def by_seq(view):
            return view[:, :, 0:NS].rearrange("p k (b t) -> p k b t", b=SB)

        block = ctx.enter_context(nc.Block())

        @block.sync
        def _(sp):
            sp.dma_start(c_t[:, :, :], A["c_t"]).then_inc(c_in, 16)
            sp.dma_start(b_ada, A["b_ada"][:, 0:5 * D].broadcast_to([NR, 5 * D])).then_inc(bias_in, 16)
            sp.dma_start(g2_rows[:, :], A["b_ada"][:, 5 * D:].broadcast_to([NR, D])).then_inc(bias_in, 16)

            def load_weights(n):
                unit, _ = BLOCKS[n]
                kind, g, b = unit
                if n >= NW:
                    last = BLOCKS[n - NW][1]
                    sp.wait_ge(ready[last[0]], nth(last))
                slot = weights[:, n % NW, :]
                if kind == "rgig":
                    dst = slot.rearrange("p (a h n) -> p a h n", a=2, h=HEADS)
                    sp.dma_start(dst[:, 0], A["w_rg"]).then_inc(weight_in[n % NW], 16)
                    sp.dma_start(dst[:, 1], A["w_ig"]).then_inc(weight_in[n % NW], 16)
                    return
                if kind == "keytop":
                    half = HEADS * NKEYS
                    src, dst = A["keys_t"][:, b * half:(b + 1) * half], slot[:, 0:half]
                elif kind == "mix":
                    src = A["pool_mix"]
                    dst = slot.rearrange("p (g k n) -> p g k n", g=4, k=2)
                else:
                    name = {"ada": "w_ada", "bb": "w_branch_b", "ba": "w_branch_a", "out": "w_out", "q": "w_q"}.get(kind, "w_in")
                    c = (COLS.get(kind, 0) + b) * WB
                    src = A[name][:, :, c:c + WB]
                    dst = slot.rearrange("p (k n) -> p k n", k=KT)
                sp.dma_start(dst, src).then_inc(weight_in[n % NW], 16)

            for n in range(len(BLOCKS)):
                load_weights(n)
                if n == 2:
                    sp.dma_start(cols("x", 0), A["x_t0"]).then_inc(x_in, 16)
                    sp.dma_start(state_pool, A["state_pool_t"]).then_inc(state_in, 16)
                    sp.dma_start(state_conv, A["state_conv_t"]).then_inc(state_in, 16)
                    sp.dma_start(state_lru, A["state_lru_t"]).then_inc(state_in, 16)
                if BLOCKS[n][0] == ("xb", 1, 0):
                    sp.wait_ge(ready["tok"], nth(("tok", 1, 3)))
                    sp.dma_start(cols("x", 1), A["x_t1"]).then_inc(x_in, 16)

            sp.wait_ge(tails, 2 * 4)
            sp.dma_start(A["conv_p"], conv_tail[:, :, :]).then_inc(out_done, 16)
            sp.dma_start(A["pool_p"], pool_tail[:, :, :]).then_inc(out_done, 16)
            sp.dma_start(A["lru_p"], lru_tail[:, :]).then_inc(out_done, 16)
            for t in range(1, TILES):
                sp.wait_ge(yready, t + 1)
                sp.dma_start(A["y_prompt"][(t - 1) * P:t * P, :], h2_rows(t)).then_inc(out_done, 16)
            sp.wait_ge(out_done, 16 * (3 + 4 + 4))

        @block.gpsimd
        def _(pool):
            nc.gpsimd.memset(zeros[:, :], 0.0)
            nc.gpsimd.memset(ones[:, :], 1.0).then_inc(zeros_done, 1)
            pool.dma_start(final_norm[:, :], A["final_norm"].broadcast_to([P, D])).then_inc(norm_in, 16)

            def take_indices(t, i, table, par):
                nc.gpsimd.tensor_copy(step_idx[:, table, par, :], idx_of(t)[:, bass.ds(i * TOPK, TOPK)]).then_inc(idx_copied, 1)

            def fetch(table, par, k):
                rows, slots, free, landed, source = ((u_rows, NU, u_free, u_in, A["expert_u"]),
                                                     (v_rows, NV, v_free, v_in, A["expert_v"]))[table]
                pool.wait_ge(free, 1)
                pool.sem_inc(free, -1)
                pool.indirect_dma_start(
                    out=rows[:, k % slots, :], out_offset=None, in_=source,
                    in_offset=bass.IndirectOffsetOnAxis(ap=step_idx[:, table, par, k:k + 1], axis=0),
                ).then_inc(landed[k % slots], 16)

            def fetch_step(u_step, v_step, odd, number):
                if u_step:
                    take_indices(*u_step, 0, 1 - odd)
                take_indices(*v_step, 1, odd)
                pool.wait_ge(idx_copied, number * 2 + (3 if u_step else 2))
                for k in range(0, TOPK, 2):
                    if u_step:
                        fetch(0, 1 - odd, k)
                        fetch(0, 1 - odd, k + 1)
                    fetch(1, odd, k)
                    fetch(1, odd, k + 1)

            def following(t, i):
                return (t, i + 1) if i + 1 < TILE_STEPS[t] else (t + 1, 0) if t + 1 < TILES else None

            for role, kind, t, i in SCHEDULE:
                if kind == "dots":
                    pool.wait_ge(idx_done, 1)
                    take_indices(0, 0, 0, 0)
                    pool.wait_ge(idx_copied, 1)
                    for k in range(TOPK):
                        fetch(0, 0, k)
                if role == "pair" and i[1] == 0:
                    i = i[0]
                    number = STEP0[t] + i
                    after = following(t, i)
                    if after and after[1] % (TILE_STEPS[after[0]] // 2) == 0:
                        pool.wait_ge(idx_done, 2 * after[0] + 1 + 2 * after[1] // TILE_STEPS[after[0]])
                    fetch_step(after, (t, i), number % 2, number)
                if kind == "loop":
                    first, end = i
                    pool.wait_ge(idx_done, 2 * t + 2)
                    with pool.Fori(0, (end - first) // 2) as two:
                        for j in range(2):
                            i = two * 2 + (first + j)
                            fetch_step((t, i + 1), (t, i), (STEP0[t] + first + j) % 2, two * 2 + (STEP0[t] + first + j))
                    if (end - first) % 2:
                        fetch_step((t, end), (t, end - 1), (STEP0[t] + end - 1) % 2, STEP0[t] + end - 1)

        @block.tensor
        def _(pe):
            done = [0]

            def begin(product):
                n = NUMBER[product]
                assert n == done[0]
                done[0] += 1
                if n >= NBANK:
                    old = PRODUCTS[n - NBANK]
                    pe.wait_ge(taken[old[0]], nth(old))
                return banks[n % NBANK]

            def block_of(unit):
                n = BLOCK_NO[unit]
                seen = sum(16 * (1 + (u[0] == "rgig")) for m, (u, _) in enumerate(BLOCKS[:n + 1]) if m % NW == n % NW)
                pe.wait_ge(weight_in[n % NW], seen)
                return weights[:, n % NW, :]

            def finish(ins, product):
                ins.then_inc(ready[product[0]], 1)

            def ada(i):
                if i == 0:
                    pe.wait_ge(silu_done, 1)
                w = block_of(("ada", 0, i)).rearrange("p (k n) -> p k n", k=KT)
                bank = begin(("ada", 0, i))
                for k in range(KT):
                    ins = nc.tensor.matmul(bank[0:NR, 0:WB], silu_c[:, k, :], w[:, k, :], start=k == 0, stop=k == KT - 1)
                finish(ins, ("ada", 0, i))

            def turn_modulation():
                bank = begin(("modT", 0, 0))
                pe.wait_ge(const_in, 16 * N_CONST)
                pe.wait_ge(taken["ada"], 20)
                for j in range(5 * KT):
                    ins = nc.tensor.transpose(bank[:, j * NR:(j + 1) * NR], mod_rows[:, j * P:(j + 1) * P], ident[0:NR, 0:NR])
                finish(ins, ("modT", 0, 0))

            def norm(g, which):
                n = sizes(g)[2]
                product = (("ss1", "ss2")[which], g, 0)
                sq = cols("pool", g)
                bank = begin(product)
                pe.wait_ge(zeros_done, 1)
                pe.wait_ge(square_done, KT * (2 * g + which + 1))
                for k in range(KT):
                    ins = nc.tensor.matmul(bank[:, 0:n], ones[:, :], sq[:, k, :], start=k == 0, stop=k == KT - 1)
                finish(ins, product)

            def columns(kind, g, c):
                n = sizes(g)[2]
                w = block_of((kind, g, c // 2)).rearrange("p (k n) -> p k n", k=KT)
                src = cols({"bb": "gy", "ba": "pool", "out": "gb"}.get(kind, "h"), g)
                if kind in ("xb", "q") and c == 0:
                    m = 2 * g + (kind == "q") + 1
                    pe.wait_ge(h_prompt, KT * m)
                    pe.wait_ge(h_sample, m)
                if kind == "ba" and c == 0:
                    pe.wait_ge(taken["mix"], nth(("mix", g, 7)))
                if kind == "bb" and c == 0:
                    pe.wait_ge(gy_done, 4 * (g + 1))
                if kind == "out" and c == 0:
                    pe.wait_ge(taken["bb"], nth(("bb", g, 7)))
                product = (kind, g, c)
                bank = begin(product)
                j = c % 2
                for k in range(KT):
                    ins = nc.tensor.matmul(bank[:, 0:n], w[:, k, j * P:(j + 1) * P], src[:, k, :], start=k == 0, stop=k == KT - 1)
                finish(ins, product)

            def lru_gates(g, q):
                n = sizes(g)[2]
                w = block_of(("rgig", g, 0)).rearrange("p (a h n) -> p a h n", a=2, h=HEADS)
                xc = cols("xc", g)
                for c in (2 * q, 2 * q + 1):
                    pe.wait_ge(conv_done, g * KT + c + 1)
                    for a in range(2):
                        product = ("rgig", g, 2 * c + a)
                        bank = begin(product)
                        finish(nc.tensor.matmul(bank[:, 0:n], w[:, a, c, :], xc[:, c, :], start=True, stop=True), product)

            def mix(g, q):
                n = sizes(g)[2]
                w = block_of(("mix", g, 0)).rearrange("p (g k n) -> p g k n", g=4, k=2)
                pooled = cols("i", g)
                pe.wait_ge(pooled_done, g * 4 + q + 1)
                for j in range(2):
                    product = ("mix", g, 2 * q + j)
                    bank = begin(product)
                    for k in range(2):
                        ins = nc.tensor.matmul(bank[:, 0:n], w[:, q, k, j * P:(j + 1) * P], pooled[:, 2 * q + k, :], start=k == 0, stop=k == 1)
                    finish(ins, product)

            def first_col(t, samples):
                return samples if t == 1 else (t - 2) * P

            def token_rows(t):
                g = int(t >= 2)
                for i in range(4):
                    product = ("tok", t, i)
                    src = cols(("h", "x")[i // 2], g)
                    bank = begin(product)
                    if i == 0:
                        m = 2 * g + 2
                        pe.wait_ge(h_prompt, KT * m)
                        pe.wait_ge(h_sample, m)
                    for j in range(4):
                        k = 4 * (i % 2) + j
                        if t:
                            lo = first_col(t, NS)
                            tile = src[:, k, lo:lo + P]
                        else:
                            tile = h_twice[:, k, :] if i < 2 else src[:, k, 0:NS]
                        ins = nc.tensor.transpose(bank[0:tile.shape[1], j * P:(j + 1) * P], tile, ident[:, :])
                    finish(ins, product)

            def scores(t, z):
                g = int(t >= 2)
                keys = block_of(("keytop", t, z)).rearrange("p (h n) -> p h n", h=2 * HEADS)
                q = queries(g)
                lo = first_col(t, P) if t else 0
                pe.wait_ge(taken["q"], nth(("q", g, 15)))
                for i in (2 * z, 2 * z + 1):
                    product = ("score", t, i)
                    bank = begin(product)
                    for j in range(4):
                        ins = nc.tensor.matmul(bank[:, j * P:(j + 1) * P], q[:, 4 * i + j, lo:lo + P], keys[:, 4 * (i - 2 * z) + j, :], start=True, stop=True)
                    finish(ins, product)

            def rows_of(t):
                return NS if t == 0 else P

            def open_sum(t, first):
                m = rows_of(t)
                if first:
                    pe.wait_ge(norm_in, 16)
                    if t:
                        pe.wait_ge(v_read, t)
                for j in range(2):
                    ins = nc.tensor.matmul(v_sum[0:m, j * 512:(j + 1) * 512], zeros[:, 0:m], final_norm[0:1, 0:512], start=first, stop=not first)
                if not first:
                    ins.then_inc(v_tile, 1)

            def sum_pairs(t, number, pairs):
                m = rows_of(t)
                add = ident2[:, :] if t == 0 else ident[:, :]
                for j in pairs:
                    pe.wait_ge(paired_done, number * PAIRS + (j + 1))
                    row = v_rows[:, (2 * j + 1) % NV, :]
                    for half in (slice(0, 512), slice(512, D)):
                        nc.tensor.matmul(v_sum[0:m, half], add, row[:, half], start=False, stop=False).then_inc(v_free, 1)

            for role, kind, g, b in SCHEDULE:
                if kind == "loop":
                    first, end = b
                    if first == 0:
                        open_sum(g, True)
                    with pe.Fori(0, end - first) as i:
                        sum_pairs(g, i + (STEP0[g] + first), range(PAIRS))
                elif kind == "final":
                    open_sum(g, False)
                    for i in range(2):
                        bank = begin(("g2", g, i))
                        pe.wait_ge(taken["ada"], 24)
                        finish(nc.tensor.matmul(bank[:, 0:512], select[:, int(g > 0), :], g2_rows[:, i * 512:(i + 1) * 512], start=True, stop=True), ("g2", g, i))
                elif role == "sum":
                    if b == (0, 0):
                        open_sum(g, True)
                    sum_pairs(g, STEP0[g] + b[0], [b[1]])
                elif role != "make":
                    continue
                elif kind == "ada":
                    ada(b)
                elif kind == "modT":
                    turn_modulation()
                elif kind == "norm":
                    norm(g, b)
                elif kind in COLS:
                    columns(kind, g, b)
                elif kind == "rgig":
                    lru_gates(g, b)
                elif kind == "mix":
                    mix(g, b)
                elif kind == "tok":
                    token_rows(g)
                elif kind == "keytop":
                    scores(g, b)

        @block.scalar
        def _(act):
            for dst, name in ((vecs, "vecs"), (ident, "ident"), (ident2, "ident2"), (select, "select"), (inv_count, "inv_count"), (iota16, "iota16")):
                act.dma_start(dst[:], A[name]).then_inc(const_in, 16)
            act.wait_ge(c_in, 16)
            nc.scalar.activation(silu_c[:, :, :], c_t[:, :, :], ACT.Silu).then_inc(silu_done, 1)
            act.wait_ge(centered, 1)
            nc.scalar.activation(sp_tmp[:, 1, :], sp_tmp[:, 0, :], ACT.Exp).then_inc(exp_done, 1)
            def take(product):
                act.wait_ge(ready[product[0]], nth(product))
                return banks[NUMBER[product] % NBANK]

            def square(g, b):
                x, sq = cols("x", g), cols("pool", g)
                if b == 0:
                    act.wait_ge(x_in, 16 * (g + 1))
                    if g:
                        act.wait_ge(idx_done, 4)
                else:
                    act.wait_ge(taken["out"], nth(("out", g, b - 1)))
                for k in range(KT) if b == 0 else (b - 1,):
                    nc.scalar.activation(sq[:, k, :], x[:, k, :], ACT.Square).then_inc(square_done, 1)

            def norm(g, which):
                s, p, n = sizes(g)
                h = cols("h", g)
                act.wait_ge(ms_done, 2 * g + which + 1)
                nc.scalar.activation(rstd[:, 0:n], ms[:, 0:n], ACT.Sqrt).then_inc(std_done, 1)
                act.wait_ge(coef_done, 3)
                act.wait_ge(h_scaled, 2 * g + which + 1)
                for k in range(KT):
                    nc.scalar.activation(h[:, k, s:n], h[:, k, s:n], ACT.Identity, scale=coef[:, which, k, SB:NR],
                                         bias=mod_t[:, 24 * which + k, SB:NR]).then_inc(h_prompt, 1)

            def columns(kind, g, c):
                s, p, n = sizes(g)
                if kind not in ("bb", "ba", "out"):
                    bank = take((kind, g, c))
                    if kind == "xb":
                        smp, prm = conv_ext(g)
                        if c == 0 and g:
                            act.wait_ge(taken["bb"], nth(("bb", g - 1, 7)))
                        if s:
                            nc.scalar.activation(smp[:, c, :, CB:], bank[:, 0:NS].rearrange("p (b t) -> p b t", b=SB), ACT.Copy)
                        nc.scalar.activation(prm[:, c, CB:], bank[:, s:n], ACT.Copy).then_inc(taken[kind], 1)
                    elif kind == "u":
                        rows, smp, prm = pool_ext(g)
                        if s:
                            nc.scalar.activation(smp[:, c, :, PB:], bank[:, 0:NS].rearrange("p (b t) -> p b t", b=SB), ACT.Copy)
                        nc.scalar.activation(prm[:, c, PB:], bank[:, s:n], ACT.Copy).then_inc(taken[kind], 1)
                    elif kind == "yb":
                        nc.scalar.activation(cols("gy", g)[:, c, :], bank[:, 0:n], ACT.Gelu_apprx_tanh).then_inc(taken[kind], 1)
                    elif kind == "mg":
                        if c == 0:
                            act.wait_ge(scan_done, 4 * (g + 1))
                        if c == 8:
                            act.wait_ge(pooled_done, 4 * (g + 1))
                        dst = cols(("conv", "gb")[c // 8], g)[:, c % 8, :]
                        nc.scalar.activation(dst, bank[:, 0:n], ACT.Sigmoid, bias=vec(("b_gate_a", "b_gate_b")[c // 8])[:, c % 8:c % 8 + 1]).then_inc(taken[kind], 1)
                    elif kind == "q":
                        q = queries(g)
                        if s:
                            nc.scalar.activation(q[:, c, 0:NS], bank[:, 0:NS], ACT.Copy)
                        at = NS if s else 0
                        nc.scalar.activation(q[:, c, at:], bank[:, 0:n], ACT.Copy).then_inc(taken[kind], 1)

            def lru_gates(g, q):
                n = sizes(g)[2]
                for c in (2 * q, 2 * q + 1):
                    for a, (dst, bias) in enumerate((("conv", "b_rg"), ("i", "b_ig"))):
                        bank = take(("rgig", g, 2 * c + a))
                        nc.scalar.activation(cols(dst, g)[:, c, :], bank[:, 0:n], ACT.Sigmoid, bias=vec(bias)[:, c:c + 1]).then_inc(taken["rgig"], 1)

            def lru(g, q):
                r, root = cols("conv", g), cols("gb", g)
                act.wait_ge(taken["rgig"], nth(("rgig", g, 4 * q + 3)))
                for c in (2 * q, 2 * q + 1):
                    nc.scalar.activation(root[:, c, :], r[:, c, :], ACT.Tanh, scale=sp4[:, c:c + 1])
                for c in (2 * q, 2 * q + 1):
                    nc.scalar.activation(r[:, c, :], r[:, c, :], ACT.Exp, scale=minus_sp8[:, c:c + 1]).then_inc(rates_done, 1)
                act.wait_ge(rates_done, 2 * (4 * g + q + 1))
                two = root[:, 2 * q:2 * q + 2, :]
                nc.scalar.activation(two, two, ACT.Sqrt).then_inc(sqrt_done, 1)

            def mix(g, q):
                n = sizes(g)[2]
                z = cols("pool", g)
                for c in (2 * q, 2 * q + 1):
                    bank = take(("mix", g, c))
                    if c == 0:
                        act.wait_ge(pooled_done, 4 * (g + 1))
                    nc.scalar.activation(z[:, c, :], bank[:, 0:n], ACT.Copy, scale=vec("pool_scale")[:, c:c + 1]).then_inc(taken["mix"], 1)

            def token_rows(t):
                for i in range(4):
                    bank = take(("tok", t, i))
                    if i == 0 and t == 0:
                        act.wait_ge(scan_done, 4)
                        act.wait_ge(pooled_done, 4)
                        act.wait_ge(out_done, 16 * 3)
                    if i == 0 and t == 2:
                        act.wait_ge(taken["ba"], nth(("ba", 1, 7)))
                    dst = (h2_rows, x1_rows)[i // 2](t)
                    m = NS if t == 0 and i >= 2 else P
                    nc.scalar.activation(dst[0:m, (i % 2) * 512:(i % 2 + 1) * 512], bank[0:m, :], ACT.Copy).then_inc(taken["tok"], 1)

            def softmax_exp(t, z):
                act.wait_ge(centered, 2 * t + z + 2)
                half = exps[:, z * SLOTS // 2:(z + 1) * SLOTS // 2]
                nc.scalar.activation(half, half, ACT.Exp).then_inc(exp_done, 1)

            def gelu(number):
                act.wait_ge(dots_done, number + 1)
                nc.scalar.activation(gelus[:, :], dots[:, :], ACT.Gelu_apprx_tanh).then_inc(gelu_done, 1)
                act.wait_ge(wts_done, number + 1)

            def scale_pair(number, j):
                k = 2 * j + 1
                row = v_rows[:, k % NV, :]
                act.wait_ge(v_in[k % NV], number * (16 * TOPK // NV) + 16 * (k // NV + 1))
                nc.scalar.activation(row, row, ACT.Copy, scale=wts[:, k:k + 1]).then_inc(scaled_done, 1)

            def final(t):
                m = NS if t == 0 else P
                y = h2_rows(t)[0:m, :]
                act.wait_ge(v_tile, t + 1)
                nc.scalar.activation(y, v_sum[0:m, :], ACT.Copy).then_inc(v_read, 1)
                act.wait_ge(yfin, t + 1)
                nc.scalar.activation(x1_rows(t)[0:m, :], y, ACT.Square, accum_out=fin[0:m, 0:1]).then_inc(ysq, 1)
                act.wait_ge(ymean, t + 1)
                nc.scalar.activation(fin[0:m, 2:3], fin[0:m, 1:2], ACT.Sqrt).then_inc(ystd, 1)

            for role, kind, g, b in SCHEDULE:
                if kind == "loop":
                    first, end = b
                    with act.Fori(0, end - first) as i:
                        for j in range(PAIRS):
                            if j == 0:
                                gelu(i + (STEP0[g] + first))
                            scale_pair(i + (STEP0[g] + first), j)
                elif role == "pair":
                    if b[1] == 0:
                        gelu(STEP0[g] + b[0])
                    scale_pair(STEP0[g] + b[0], b[1])
                elif role in ("make", "sum"):
                    continue
                elif kind == "modT":
                    bank = take(("modT", 0, 0))
                    nc.scalar.activation(mod_t[:, :, :].rearrange("p a r -> p (a r)"), bank[:, 0:5 * KT * NR], ACT.Copy).then_inc(taken["modT"], 1)
                elif kind == "square":
                    square(g, b)
                elif kind == "norm":
                    norm(g, b)
                elif kind in COLS:
                    columns(kind, g, b)
                    if kind == "yb" and (g, b) == (0, 0):
                        act.wait_ge(tails, 1)
                        act.dma_start(A["conv_s"], conv_s[:, :, :, :]).then_inc(out_done, 16)
                    if kind == "mg" and (g, b) == (0, 15):
                        act.wait_ge(tails, 4)
                        act.dma_start(A["lru_s"], lru_s[:, :, :]).then_inc(out_done, 16)
                        act.dma_start(A["pool_s"], pool_s).then_inc(out_done, 16)
                elif kind == "rgig":
                    lru_gates(g, b)
                elif kind == "lru":
                    lru(g, b)
                elif kind == "mix":
                    mix(g, b)
                elif kind == "tok":
                    token_rows(g)
                elif kind == "number":
                    softmax_exp(g, b)
                elif kind == "final":
                    final(g)
                    if g == 0:
                        act.wait_ge(yready, 1)
                        act.dma_start(A["y_sample"], h2_rows(0)[0:NS, :]).then_inc(out_done, 16)

        @block.vector
        def _(dve):
            V = nc.vector
            steps = [0]
            counts = {}

            def link(ins):
                steps[0] += 1
                ins.then_inc(dve_step, 1)
                dve.wait_ge(dve_step, steps[0])

            def mark(ins, s, n):
                ins.then_inc(s, 1)
                dve.wait_ge(s, n)

            def take(product):
                dve.wait_ge(ready[product[0]], nth(product))
                return banks[NUMBER[product] % NBANK]

            def softplus():
                z, s, q, r = (sp_tmp[:, i, :] for i in range(1, 5))
                dve.wait_ge(exp_done, 1)
                link(V.tensor_scalar_add(s, z, 2.0))
                link(V.reciprocal(q, s))
                link(V.tensor_tensor(s, z, q, ALU.mult))
                link(V.tensor_tensor(q, s, s, ALU.mult))
                link(V.tensor_scalar(r, q, 1.0 / 17, None, ALU.mult))
                for odd in (15, 13, 11, 9, 7, 5, 3):
                    link(V.scalar_tensor_tensor(out=r, in0=r, scalar=1.0 / odd, in1=q, op0=ALU.add, op1=ALU.mult))
                link(V.scalar_tensor_tensor(out=r, in0=r, scalar=1.0, in1=s, op0=ALU.add, op1=ALU.mult))
                link(V.tensor_scalar(z, vec("lru_lambda"), -1.0, 0.0, ALU.mult, ALU.max))
                link(V.scalar_tensor_tensor(out=z, in0=r, scalar=2.0, in1=z, op0=ALU.mult, op1=ALU.add))
                link(V.tensor_scalar(minus_sp8[:, :], z, -8.0, None, ALU.mult))
                V.tensor_scalar(sp4[:, :], z, 4.0, None, ALU.mult).then_inc(coef_done, 1)

            def begin():
                dve.wait_ge(const_in, 16 * N_CONST)
                lam = vec("lru_lambda")
                link(V.tensor_scalar(sp_tmp[:, 0, :], lam, -1.0, None, ALU.mult))
                V.tensor_tensor(sp_tmp[:, 0, :], sp_tmp[:, 0, :], lam, ALU.min).then_inc(centered, 1)
                V.memset(dots[:, :], 0.0).then_inc(u_free, NU)
                V.memset(gelus[:, :], 0.0).then_inc(v_free, NV)
                dve.wait_ge(bias_in, 32)
                softplus()

            def ada(i):
                bank = take(("ada", 0, i))
                if i < 20:
                    dst = mod_rows[:, i * WB:(i + 1) * WB]
                    bias = b_ada[:, i * WB:(i + 1) * WB]
                else:
                    dst = bias = g2_rows[:, (i - 20) * WB:(i - 19) * WB]
                V.tensor_tensor(dst, bank[0:NR, 0:WB], bias, ALU.add).then_inc(taken["ada"], 1)

            def coefficients():
                dve.wait_ge(taken["modT"], 1)
                for which in range(2):
                    scale = mod_t[:, 8 + 24 * which:16 + 24 * which, :]
                    link(V.tensor_scalar_add(coef[:, which, :, :], scale, 1.0))
                    norm_w = vec(("norm1", "norm2")[which]).rearrange("p (k o) -> p k o", o=1).broadcast_to([P, KT, NR])
                    ins = V.tensor_tensor(coef[:, which, :, :], coef[:, which, :, :], norm_w, ALU.mult)
                    mark(ins, coef_done, 2 + which)

            def over_time(view):
                return view.rearrange("p k (b o) -> p k b o", o=1).broadcast_to([P, view.shape[1], SB, ST])

            def norm(g, which):
                s, p, n = sizes(g)
                m = 2 * g + which
                x, h = cols("x", g), cols("h", g)
                bank = take((("ss1", "ss2")[which], g, 0))
                V.tensor_scalar(ms[:, 0:n], bank[:, 0:n], 1.0 / D, EPS, ALU.mult, ALU.add).then_inc(taken[("ss1", "ss2")[which]], 1)
                dve.wait_ge(taken[("ss1", "ss2")[which]], g + 1)
                dve.sem_inc(ms_done, 1)
                dve.wait_ge(std_done, m + 1)
                link(V.reciprocal(rstd[:, 0:n], rstd[:, 0:n]))
                r = rstd[:, 0:n].rearrange("p (o n) -> p o n", o=1).broadcast_to([P, KT, n])
                dve.wait_ge(x_in, 16 * (g + 1))
                mark(V.tensor_tensor(h, x, r, ALU.mult), h_scaled, m + 1)
                if s:
                    hs = by_seq(h)
                    link(V.tensor_tensor(hs, hs, over_time(coef[:, which, :, 0:SB]), ALU.mult))
                    link(V.tensor_tensor(hs, hs, over_time(mod_t[:, 24 * which:24 * which + 8, 0:SB]), ALU.add))
                    if which:
                        twice = h[:, :, 0:NS].rearrange("p k (o n) -> p k o n", o=1).broadcast_to([P, KT, 2, NS])
                        link(V.tensor_copy(h_twice.rearrange("p k (o n) -> p k o n", o=2), twice))
                    dve.sem_inc(h_sample, 1)
                else:
                    dve.sem_inc(h_sample, 1)
                if which == 0:
                    smp, prm = conv_ext(g)
                    rows, psmp, pprm = pool_ext(g)
                    if g:
                        link(V.tensor_copy(pprm[:, :, 0:PB], pool_tail[:, :, :]))
                    else:
                        dve.wait_ge(state_in, 48)
                        dve.wait_ge(ready["modT"], 1)
                        link(V.tensor_copy(smp[:, :, :, 0:CB], state_conv))
                        link(V.memset(prm[:, :, 0:CB], 0.0))
                        link(V.tensor_copy(psmp[:, :, :, 0:PB], state_pool))
                        link(V.memset(pprm[:, :, 0:PB], 0.0))

            def conv(g, c):
                s, p, n = sizes(g)
                smp, prm = conv_ext(g)
                xc = cols("xc", g)
                if g and c == 0:
                    link(V.tensor_copy(prm[:, :, 0:CB], conv_tail[:, :, :]))
                dve.wait_ge(taken["xb"], nth(("xb", g, c)))
                parts = [(xc[:, c, s:n], lambda t: prm[:, c, t:t + p])]
                if s:
                    parts.append((by_seq(xc)[:, c], lambda t: smp[:, c, :, t:t + ST]))
                for out, tap in parts:
                    V.tensor_scalar(out, tap(0), vec("conv_w0")[:, c:c + 1], vec("conv_b")[:, c:c + 1], ALU.mult, ALU.add).then_inc(dve_step, 1)
                    steps[0] += 1
                for t in range(1, CW):
                    dve.wait_ge(dve_step, steps[0])
                    for out, tap in parts:
                        V.scalar_tensor_tensor(out=out, in0=tap(t), scalar=vec(f"conv_w{t}")[:, c:c + 1], in1=out, op0=ALU.mult, op1=ALU.add).then_inc(dve_step, 1)
                        steps[0] += 1
                dve.wait_ge(dve_step, steps[0])
                if s:
                    link(V.tensor_copy(conv_s[:, c, :, :], smp[:, c, :, ST:]))
                V.tensor_copy(conv_tail[:, c, :], prm[:, c, p:]).then_inc(conv_done, 1)
                if c == KT - 1:
                    dve.wait_ge(conv_done, KT * (g + 1))
                    dve.sem_inc(tails, 1)

            def lru(g, q):
                s, p, n = sizes(g)
                two = slice(2 * q, 2 * q + 2)
                a, bx, xc, root = (cols(x, g)[:, two, :] for x in ("conv", "i", "xc", "gb"))
                dve.wait_ge(taken["rgig"], nth(("rgig", g, 4 * q + 3)))
                link(V.tensor_tensor(bx, bx, xc, ALU.mult))
                if g == 0:
                    link(V.tensor_copy(bx_first[:, two], bx[:, :, s]))
                dve.wait_ge(sqrt_done, 4 * g + q + 1)
                link(V.tensor_tensor(bx, bx, root, ALU.mult))
                link(V.scalar_tensor_tensor(out=bx, in0=a, scalar=1.0, in1=bx, op0=ALU.add, op1=ALU.mult))
                if g == 0:
                    link(V.tensor_copy(bx[:, :, s], bx_first[:, two]))
                    a0, b0 = by_seq(a)[:, :, :, 0], by_seq(bx)[:, :, :, 0]
                    link(V.tensor_tensor(lru_s[:, two, :], a0, state_lru[:, two, :], ALU.mult))
                    link(V.tensor_tensor(b0, b0, lru_s[:, two, :], ALU.add))
                    link(V.memset(a0, 0.0))
                else:
                    link(V.tensor_tensor(lru_tail[:, two], lru_tail[:, two], a[:, :, 0], ALU.mult))
                    link(V.tensor_tensor(bx[:, :, 0], bx[:, :, 0], lru_tail[:, two], ALU.add))
                link(V.memset(a[:, :, s], 0.0))
                flat = [arena[:, place[x] + 2 * q * n:place[x] + (2 * q + 2) * n] for x in ("xc", "conv", "i")]
                link(V.tensor_tensor_scan(out=flat[0], data0=flat[1], data1=flat[2], initial=0.0, op0=ALU.mult, op1=ALU.add))
                if s:
                    link(V.tensor_copy(lru_s[:, two, :], by_seq(xc)[:, :, :, ST - 1]))
                link(V.tensor_copy(lru_tail[:, two], xc[:, :, n - 1]))
                if q == 3:
                    dve.sem_inc(tails, 1)
                dve.sem_inc(scan_done, 1)
                dve.wait_ge(taken["yb"], nth(("yb", g, 2 * q + 1)))
                gy = cols("gy", g)[:, two, :]
                V.tensor_tensor(gy, gy, xc, ALU.mult).then_inc(gy_done, 1)

            def pooling(g, q):
                s, p, n = sizes(g)
                rows, smp, prm = pool_ext(g)
                w = rows.shape[2]
                pooled = cols("i", g)
                two = slice(2 * q, 2 * q + 2)
                dve.wait_ge(taken["u"], nth(("u", g, 2 * q + 1)))
                half = 2 * w
                sums = [region("gb", NB)[:, i * half:(i + 1) * half].rearrange("p (k w) -> p k w", k=2) for i in range(2)]
                src, lag = rows[:, two, :], 1
                for level in range(q + 1):
                    dst = sums[level % 2]
                    lo = 2 * lag - 1
                    link(V.tensor_tensor(dst[:, :, lo:w], src[:, :, lo:w], src[:, :, lo - lag:w - lag], ALU.add))
                    src, lag = dst, 2 * lag
                base = w - p - PB
                window = float(WINDOWS[q])
                V.scalar_tensor_tensor(out=pooled[:, two, s:n], in0=src[:, :, base + PB:w], scalar=1.0 / window,
                                       in1=prm[:, two, PB:], op0=ALU.mult, op1=ALU.subtract).then_inc(dve_step, 1)
                steps[0] += 1
                if s:
                    for c in range(2):
                        in0 = src[:, c, 0:base].rearrange("p (b t) -> p b t", b=SB)[:, :, PB:]
                        link(V.scalar_tensor_tensor(out=by_seq(pooled)[:, 2 * q + c], in0=in0, scalar=1.0 / window,
                                                    in1=smp[:, 2 * q + c, :, PB:], op0=ALU.mult, op1=ALU.subtract))
                    tmp = small[:, 0:32].rearrange("p (k t) -> p k t", k=2)
                    inv = inv_count[:, q:q + 1, :].broadcast_to([P, 2, 16])
                    link(V.tensor_tensor(tmp, src[:, :, base + PB:base + PB + 16], inv, ALU.mult))
                    link(V.tensor_tensor(pooled[:, two, s:s + 16], tmp, prm[:, two, PB:PB + 16], ALU.subtract))
                    link(V.tensor_copy(pool_s[:, two, :, :], smp[:, two, :, ST:]))
                link(V.tensor_copy(pool_tail[:, two, :], prm[:, two, p:]))
                dve.sem_inc(pooled_done, 1)
                if q == 3:
                    dve.sem_inc(tails, 2)

            def gated(kind, g, c):
                s, p, n = sizes(g)
                ga, gb, x = cols("conv", g), cols("gb", g), cols("x", g)
                if kind == "ba" and c == 0:
                    dve.wait_ge(taken["mg"], nth(("mg", g, 15)))
                bank = take((kind, g, c))
                if kind == "ba":
                    V.tensor_tensor(ga[:, c, :], ga[:, c, :], bank[:, 0:n], ALU.mult).then_inc(taken[kind], 1)
                elif kind == "bb":
                    link(V.tensor_tensor(gb[:, c, :], gb[:, c, :], bank[:, 0:n], ALU.mult))
                    dve.wait_ge(taken["ba"], nth(("ba", g, c)))
                    V.tensor_tensor(gb[:, c, :], gb[:, c, :], ga[:, c, :], ALU.add).then_inc(taken[kind], 1)
                else:
                    if s:
                        gate = over_time(mod_t[:, 16 + c:17 + c, 0:SB])
                        tmp = small[:, 0:NS].rearrange("p (o b t) -> p o b t", o=1, b=SB)
                        link(V.tensor_tensor(tmp, bank[:, 0:NS].rearrange("p (o b t) -> p o b t", o=1, b=SB), gate, ALU.mult))
                        link(V.tensor_tensor(x[:, c, 0:NS], x[:, c, 0:NS], small[:, 0:NS], ALU.add))
                    V.scalar_tensor_tensor(out=x[:, c, s:n], in0=bank[:, s:n], scalar=mod_t[:, 16 + c, SB:NR], in1=x[:, c, s:n],
                                           op0=ALU.mult, op1=ALU.add).then_inc(taken[kind], 1)

            scratch_h, scratch_gb = region("h", NB), region("gb", NB)
            cand = scratch_h[:, 0:2048]
            less = scratch_gb[:, 0:2048]
            less4 = scratch_h[:, 2048:2560].rearrange("p (i n) -> p i n", i=4)
            top_v = scratch_h[:, 2560:2816].rearrange("p (h k) -> p h k", h=16)
            top_f = scratch_h[:, 2816:3072].rearrange("p (h k) -> p h k", h=16)
            best_v = scratch_gb[:, 2048:2176].rearrange("p (h k) -> p h k", h=8)
            part_f = [scratch_gb[:, 2176 + 128 * i:2304 + 128 * i] for i in range(2)]
            chosen = [scratch_gb[:, 2432 + 128 * i:2560 + 128 * i] for i in range(2)]
            sums8 = scratch_gb[:, 2688:2696]

            def batch(instructions):
                for ins in instructions:
                    ins.then_inc(dve_step, 1)
                    steps[0] += 1
                dve.wait_ge(dve_step, steps[0])

            def key_tops(t, z):
                if z == 0 and t in (0, 2):
                    dve.wait_ge(ready["tok"], nth(("tok", 1 if t == 0 else 4, 3)))
                for i in (2 * z, 2 * z + 1):
                    bank = take(("score", t, i))
                    s = [bank[:, j * P:(j + 1) * P] for j in range(4)]
                    hp = range(4 * i, 4 * i + 4)
                    batch(V.max(top_v[:, h, 0:8], s[j]) for j, h in enumerate(hp))
                    batch(V.max_index(top_i[:, h, 0:8], top_v[:, h, 0:8], s[j]) for j, h in enumerate(hp))
                    batch(V.match_replace(less4[:, j, :], top_v[:, h, 0:8], s[j], LOWEST) for j, h in enumerate(hp))
                    dve.sem_inc(taken["score"], 1)
                    batch(V.max(top_v[:, h, 8:16], less4[:, j, :]) for j, h in enumerate(hp))
                    batch(V.max_index(top_i[:, h, 8:16], top_v[:, h, 8:16], less4[:, j, :]) for j, h in enumerate(hp))

            H4 = HEADS // 2

            def grid_of(x):
                return x[:, 0:H4 * TOPK * TOPK].rearrange("p (h k m) -> p h k m", h=H4, k=TOPK)

            def down(x):
                return x.rearrange("p h (k o) -> p h k o", o=1).broadcast_to([P, H4, TOPK, TOPK])

            def across(x):
                return x.rearrange("p h (o k) -> p h o k", o=1).broadcast_to([P, H4, TOPK, TOPK])

            def pair_tops(t, z):
                halves = top_v.rearrange("p (h a) k -> p h a k", a=2)[:, z * H4:(z + 1) * H4]
                link(V.tensor_tensor(grid_of(cand), down(halves[:, :, 0, :]), across(halves[:, :, 1, :]), ALU.add))
                c = [cand[:, 256 * h:256 * h + 256] for h in range(H4)]
                l = [less[:, 256 * h:256 * h + 256] for h in range(H4)]
                v = [best_v[:, z * H4 + h, :] for h in range(H4)]
                j = [best_j[:, z * H4 + h, :] for h in range(H4)]
                batch(V.max(v[h][:, 0:8], c[h]) for h in range(H4))
                batch(V.max_index(j[h][:, 0:8], v[h][:, 0:8], c[h]) for h in range(H4))
                batch(V.match_replace(l[h], v[h][:, 0:8], c[h], LOWEST) for h in range(H4))
                batch(V.max(v[h][:, 8:16], l[h]) for h in range(H4))
                batch(V.max_index(j[h][:, 8:16], v[h][:, 8:16], l[h]) for h in range(H4))

            def numbers(t, z):
                mine = slice(z * H4 * TOPK, (z + 1) * H4 * TOPK)
                heads = slice(z * H4, (z + 1) * H4)
                top = best_v[:, heads, 0:1].broadcast_to([P, H4, TOPK])
                e3 = exps[:, mine].rearrange("p (h k) -> p h k", h=H4)
                V.tensor_tensor(e3, best_v[:, heads, :], top, ALU.subtract).then_inc(centered, 1)
                bj = choice[:, 2, mine].bitcast(U32)
                tops = top_f.rearrange("p (h a) k -> p h a k", a=2)[:, heads]
                batch([V.tensor_scalar(part_u[:, 0, mine], bj, 4, None, ALU.logical_shift_right),
                       V.tensor_scalar(part_u[:, 1, mine], bj, 15, None, ALU.bitwise_and),
                       V.tensor_copy(top_f[:, 2 * z * H4:2 * (z + 1) * H4, :], top_i[:, 2 * z * H4:2 * (z + 1) * H4, :])])
                batch([V.tensor_copy(part_f[a][:, mine], part_u[:, a, mine]) for a in range(2)])
                count = iota16[:, :].rearrange("p (h k m) -> p h k m", h=1, k=1).broadcast_to([P, H4, TOPK, TOPK])
                for a in range(2):
                    want = down(part_f[a][:, mine].rearrange("p (h k) -> p h k", h=H4))
                    link(V.tensor_tensor(grid_of(cand), count, want, ALU.is_equal))
                    link(V.tensor_tensor(grid_of(less), grid_of(cand), across(tops[:, :, a, :]), ALU.mult))
                    link(V.reduce_sum(chosen[a][:, mine].rearrange("p (h k) -> p h k", h=H4), grid_of(less), axis=AX.X))
                first, second = (chosen[a][:, mine] for a in range(2))
                link(V.scalar_tensor_tensor(out=first, in0=first, scalar=float(NKEYS), in1=second, op0=ALU.mult, op1=ALU.add))
                dve.wait_ge(exp_done, 2 * t + z + 2)
                link(V.reduce_sum(sums8[:, heads], e3, axis=AX.X))
                link(V.reciprocal(sums8[:, heads], sums8[:, heads]))
                inv = sums8[:, heads].rearrange("p (h o) -> p h o", o=1).broadcast_to([P, H4, TOPK])
                if t:
                    batch([V.tensor_copy(idx_of(t)[:, mine], first),
                           V.tensor_tensor(gsm_of(t)[:, mine].rearrange("p (h k) -> p h k", h=H4), e3, inv, ALU.mult)])
                else:
                    link(V.tensor_tensor(e3, e3, inv, ALU.mult))
                    steps2 = slice(z * 2 * TOPK, (z + 1) * 2 * TOPK)
                    for odd, rows in ((0, slice(0, NS)), (1, slice(NS, P))):
                        batch([V.tensor_copy(dst[rows, 0, steps2].rearrange("p (h k) -> p h k", h=2),
                                             src.rearrange("p (h a k) -> p h a k", a=2, k=TOPK)[rows, :, odd, :])
                               for dst, src in ((idx0, first), (gsm0, exps[:, mine]))])
                dve.sem_inc(idx_done, 1)

            def dot(t, number, k):
                row = u_rows[:, k % NU, :]
                dve.wait_ge(u_in[k % NU], number * (16 * TOPK // NU) + 16 * (k // NU + 1))
                ins = V.tensor_tensor_reduce(out=row, in0=row, in1=h2_rows(t), scale=1.0, scalar=0.0, op0=ALU.mult, op1=ALU.add,
                                             accum_out=dots[:, k:k + 1])
                ins.then_inc(u_free if k < TOPK - 1 else dots_done, 1)
                if k == TOPK - 1:
                    dve.wait_ge(dots_done, number + 1)
                    dve.sem_inc(u_free, 1)

            def weigh(t, i, number):
                if t or i:
                    dve.wait_ge(paired_done, number * PAIRS)
                dve.wait_ge(gelu_done, number + 1)
                mark(V.tensor_tensor(wts[:, :], gelus[:, :], gsm_of(t)[:, bass.ds(i * TOPK, TOPK)], ALU.mult), wts_done, number + 1)

            def pair(t, i, number, j, dots_tile):
                if j == 0:
                    weigh(t, i, number)
                if dots_tile is not None:
                    dot(dots_tile, number + 1, 2 * j)
                    dot(dots_tile, number + 1, 2 * j + 1)
                k = 2 * j
                one, two = v_rows[:, k % NV, :], v_rows[:, (k + 1) % NV, :]
                dve.wait_ge(v_in[k % NV], number * (16 * TOPK // NV) + 16 * (k // NV + 1))
                dve.wait_ge(scaled_done, number * PAIRS + (j + 1))
                V.scalar_tensor_tensor(out=two, in0=one, scalar=wts[:, k:k + 1], in1=two, op0=ALU.mult, op1=ALU.add).then_inc(paired_done, 1)

            def final(t):
                m = NS if t == 0 else P
                y, x1 = h2_rows(t)[0:m, :], x1_rows(t)[0:m, :]
                dve.wait_ge(v_read, t + 1)
                for i in range(2):
                    bank = take(("g2", t, i))
                    half = slice(i * 512, (i + 1) * 512)
                    mark(V.tensor_tensor(y[:, half], y[:, half], bank[0:m, :], ALU.mult), taken["g2"], nth(("g2", t, i)))
                mark(V.tensor_tensor(y, y, x1, ALU.add), yfin, t + 1)
                dve.wait_ge(ysq, t + 1)
                link(V.tensor_scalar(fin[0:m, 1:2], fin[0:m, 0:1], 1.0 / D, EPS, ALU.mult, ALU.add))
                dve.sem_inc(ymean, 1)
                dve.wait_ge(ystd, t + 1)
                link(V.reciprocal(fin[0:m, 3:4], fin[0:m, 2:3]))
                if t == 0:
                    dve.wait_ge(norm_in, 16)
                V.scalar_tensor_tensor(out=y, in0=y, scalar=fin[0:m, 3:4], in1=final_norm[0:m, :], op0=ALU.mult, op1=ALU.mult).then_inc(yready, 1)

            begin()
            for role, kind, g, b in SCHEDULE:
                if kind == "loop":
                    first, end = b
                    with dve.Fori(0, end - first) as i:
                        for j in range(PAIRS):
                            pair(g, i + first, i + (STEP0[g] + first), j, g)
                elif role == "pair":
                    i, j = b
                    next_tile = g if i + 1 < TILE_STEPS[g] else g + 1 if g + 1 < TILES else None
                    pair(g, i, STEP0[g] + i, j, next_tile)
                elif role in ("make", "sum"):
                    continue
                elif kind == "dots":
                    for k in range(TOPK):
                        dot(0, 0, k)
                elif kind == "ada":
                    ada(b)
                elif kind == "modT":
                    coefficients()
                elif kind == "norm":
                    norm(g, b)
                elif kind == "xb":
                    conv(g, b)
                elif kind == "lru":
                    lru(g, b)
                elif kind == "u":
                    if b % 2:
                        pooling(g, b // 2)
                elif kind in ("ba", "bb", "out"):
                    gated(kind, g, b)
                elif kind == "keytop":
                    key_tops(g, b)
                elif kind == "pairtop":
                    pair_tops(g, b)
                elif kind == "number":
                    numbers(g, b)
                elif kind == "final":
                    final(g)


OUTPUTS = {"y_prompt": (SEQ, D), "y_sample": (NS, D), "pool_p": (P, KT, PB), "conv_p": (P, KT, CB), "lru_p": (P, KT),
           "pool_s": (P, KT, SB, PB), "conv_s": (P, KT, SB, CB), "lru_s": (P, KT, SB)}


def kernel(x_prompt, x_sample, c_prompt, c_sample, state_pool, state_conv, state_lru, norm1, norm2, w_ada, b_ada,
           w_in, b_gate, pool_mix, pool_scale, conv_w, conv_b, w_rg, b_rg, w_ig, b_ig, lru_lambda, w_branch_a,
           w_branch_b, w_out, w_q, sub_keys, expert_u, expert_v, final_norm):
    import numpy as np
    import concourse.bacc as bacc
    from concourse.bass_utils import run_bass_kernel_spmd

    def features_first(a):
        a = np.asarray(a)
        return np.ascontiguousarray(np.moveaxis(a.reshape(a.shape[:-1] + (KT, P)), (-1, -2), (0, 1)))

    def rows(a):
        return np.asarray(a)[0]

    xs, xp = np.asarray(x_sample).reshape(NS, D), np.asarray(x_prompt)[0]
    vectors = [rows(norm1), rows(norm2), rows(pool_scale), rows(conv_b), rows(b_rg), rows(b_ig), rows(lru_lambda),
               *rows(conv_w), rows(b_gate)[:D], rows(b_gate)[D:]]
    n = np.arange(P)
    select = np.zeros((NR, 2, P), np.float32)
    select[n % NS // ST, 0, n] = 1.0
    select[SB, 1, :] = 1.0
    counts = np.minimum(np.arange(16)[None, :] + 1, np.array(WINDOWS)[:, None])
    arrays = {
        "x_t0": features_first(np.concatenate([xs, xp[:GROUP_P[0]]])),
        "x_t1": features_first(xp[GROUP_P[0]:]),
        "c_t": features_first(np.concatenate([np.asarray(c_sample), np.asarray(c_prompt)])),
        "state_pool_t": features_first(rows(state_pool)),
        "state_conv_t": features_first(rows(state_conv)),
        "state_lru_t": features_first(rows(state_lru)),
        "vecs": np.ascontiguousarray(np.stack([features_first(v) for v in vectors], axis=1)),
        "keys_t": np.ascontiguousarray(rows(sub_keys).reshape(2 * HEADS, NKEYS, P).transpose(2, 0, 1).reshape(P, -1)),
        "ident": np.eye(P, dtype=np.float32),
        "ident2": np.concatenate([np.eye(NS, dtype=np.float32)] * 2),
        "select": select,
        "inv_count": np.ascontiguousarray(np.broadcast_to((1.0 / counts).astype(np.float32), (P, len(WINDOWS), 16))),
        "iota16": np.ascontiguousarray(np.broadcast_to(np.arange(16, dtype=np.float32), (P, 16))),
        "b_ada": np.asarray(b_ada), "final_norm": np.asarray(final_norm).reshape(1, D),
        "w_ada": rows(w_ada), "w_in": rows(w_in), "w_branch_a": rows(w_branch_a), "w_branch_b": rows(w_branch_b),
        "w_out": rows(w_out), "w_q": rows(w_q), "pool_mix": rows(pool_mix), "w_rg": rows(w_rg), "w_ig": rows(w_ig),
        "expert_u": rows(expert_u), "expert_v": rows(expert_v),
    }
    nc = bacc.Bacc("TRN2", target_bir_lowering=False, num_devices=1)
    A, launched = {}, {}
    for name, a in arrays.items():
        a = np.ascontiguousarray(a)
        launched["in_" + name] = a
        A[name] = nc.dram_tensor("in_" + name, a.shape, mybir.dt.from_np(a.dtype), kind="ExternalInput").ap()
    for name, shape in OUTPUTS.items():
        A[name] = nc.dram_tensor("out_" + name, shape, F32, kind="ExternalOutput").ap()
    for name in ("w_ada", "w_in", "w_branch_a", "w_branch_b", "w_out", "w_q"):
        A[name] = A[name].rearrange("(k p) n -> p k n", p=P)
    A["pool_mix"] = A["pool_mix"].rearrange("g (k p) n -> p g k n", p=P)
    A["w_rg"], A["w_ig"] = (A[x].rearrange("h p n -> p h n") for x in ("w_rg", "w_ig"))
    trunk(nc, A)
    r = run_bass_kernel_spmd(nc, [launched], core_ids=[0]).results[0]

    def features_last(name):
        a = np.moveaxis(r["out_" + name], (0, 1), (-1, -2))
        return np.ascontiguousarray(a.reshape(a.shape[:-2] + (D,)))

    return (r["out_y_prompt"].reshape(1, SEQ, D), r["out_y_sample"].reshape(SB, ST, D),
            features_last("pool_p")[None, None], features_last("conv_p")[None, None], features_last("lru_p")[None, None],
            features_last("pool_s")[None], features_last("conv_s")[None], features_last("lru_s")[None])
```

```python
from contextlib import ExitStack

import concourse.bass as bass
from concourse import mybir

P = 128
D = 1024
KT = D // P
SEQ, SB, ST = 512, 8, 8
NS = SB * ST
NR = SB + 1
WINDOWS = (2, 4, 8, 16)
PB = max(WINDOWS) - 1
CW = 4
CB = CW - 1
HEADS, NKEYS, TOPK = 8, 128, 16
SLOTS = HEADS * TOPK
EPS = 1e-6
LOWEST = -3.0e38
GROUP_P = (128, 384)
GROUP_S = (NS, 0)
N_MAX = max(GROUP_P)
TILES = 5
TILE_STEPS = (4, 8, 8, 8, 8)
STEP0 = (0, 4, 12, 20, 28)
WB = 256
NW, NU, NV, NBANK = 3, 4, 8, 6
PAIRS = TOPK // 2
PEELED = {2: 7, 3: 5, 4: 1}
CHOICE_PLACES, DENSE_PLACES = 24, 87
VEC = ("norm1", "norm2", "pool_scale", "conv_b", "b_rg", "b_ig", "lru_lambda",
       "conv_w0", "conv_w1", "conv_w2", "conv_w3", "b_gate_a", "b_gate_b")

F32, U32 = mybir.dt.float32, mybir.dt.uint32
ALU, ACT, AX = mybir.AluOpType, mybir.ActivationFunctionType, mybir.AxisListType

PER = {"ada": 24, "modT": 2, "ss1": 1, "xb": 8, "rgig": 16, "yb": 8, "u": 8, "mix": 8, "mg": 16, "bb": 8,
       "ba": 8, "out": 8, "ss2": 1, "q": 16, "tok": 4, "score": 4, "g2": 2}
COLS = {"xb": 4, "u": 0, "yb": 8, "mg": 12, "bb": 0, "ba": 0, "out": 0, "q": 0}
GROUPED = {"rgig": ("rgig", 4), "mix": ("mix", 2), "tok": ("tok", 4), "keytop": ("score", 1), "final": ("g2", 2)}


def products_of(unit):
    kind, g, b = unit
    if kind == "norm":
        return [(("ss1", "ss2")[b], g, 0)]
    if kind == "final" and b:
        return []
    if kind in GROUPED:
        name, count = GROUPED[kind]
        return [(name, g, b * count + i) for i in range(count)]
    return [unit] if kind in PER else []


def group_tiles(g):
    return (0, 1) if g == 0 else (2, 3, 4)


def first_units(g):
    units = [("square", g, 0), ("norm", g, 0)]
    if g == 1:
        return units + [("xb", g, c) for c in range(8)] + [("u", g, c) for c in range(8)] + [("yb", g, c) for c in range(4, 8)]
    for c in range(8):
        units += [("xb", g, c), ("conv", g, c)]
    return units


def mixer_units(g):
    units = []
    if g == 0:
        units += [("yb", g, 0), ("yb", g, 1)] + [("rgig", g, q) for q in range(4)]
        for q in range(4):
            units += [("yb", g, c) for c in range(2 + 2 * q, 4 + 2 * q) if c < 8] + [("lru", g, q)]
        for q in range(4):
            units += [("u", g, 2 * q), ("u", g, 2 * q + 1), ("pool", g, q)]
        units += [("mg", g, c) for c in range(8)]
    else:
        for q in range(4):
            units += [("conv", g, 2 * q), ("conv", g, 2 * q + 1), ("yb", g, q)]
        units += [("rgig", g, 0), ("rgig", g, 1), ("lru", g, 0), ("rgig", g, 2), ("lru", g, 1), ("mg", g, 0), ("mg", g, 1),
                  ("rgig", g, 3), ("lru", g, 2), ("mg", g, 2), ("mg", g, 3), ("lru", g, 3)]
        for q in range(4):
            units += [("mg", g, 4 + q), ("pool", g, q)]
    units += [("mix", g, q) for q in range(4)] + [("mg", g, c) for c in range(8, 16)]
    units += [(k, g, c) for k in ("ba", "bb") for c in range(8)]
    for c in range(8):
        units += [("out", g, c), ("square", g, 1 + c)]
    return units + [("norm", g, 1)]


def query_units(g):
    return [("q", g, c) for c in range(16)]


def choice_units(t, y):
    return [("keytop", t, y), ("pairtop", t, y), ("number", t, y)]


def weight_of(unit):
    return {"ada": 0.5, "tok": 0.5, "keytop": 0.3, "rgig": 0.8, "mix": 0.8}.get(unit[0], float(len(products_of(unit))))


def spread(units, places, first, last):
    total, before, place = sum(max(weight_of(u), 0.01) for u in units), 0.0, first
    for unit in units:
        place = max(place, first + int(before * (last - first) / total))
        if sum(len(products_of(u)) for u in places[place] + [unit]) > NBANK:
            place += 1
        places[place].append(unit)
        before += max(weight_of(unit), 0.01)


def deal(units, places, first, last):
    for n, unit in enumerate(units):
        places[first + n * (last - first) // len(units)].append(unit)


def staggered(places, between):
    s, before = [], []
    for n, units in enumerate(places):
        assert sum(len(products_of(u)) for u in units) <= NBANK
        s += between(n, 0) + [("read",) + u for u in before] + [("make",) + u for u in units] + between(n, 1)
        before = units
    return s + [("read",) + u for u in before]


def schedule():
    square, norm, *inputs = first_units(0)
    start = [[("ada", 0, i)] for i in range(8)] + [[("modT", 0, 0)], [("ada", 0, 8), square], [norm], [("ada", 0, 9)]]
    start += [[("ada", 0, i)] for i in range(10, 20)] + [[("modT", 0, 1)]] + [[u] for u in inputs + mixer_units(0)]
    start += [[("ada", 0, 20)], [("ada", 0, 21)], [("tok", 0, 0)]]
    queries = query_units(0)
    (key, pair, number), (key1, pair1, number1), (key2, pair2, number2) = (choice_units(0, y) for y in range(3))
    dot = [("dots", 0, n) for n in range(4)]
    square, norm, *copied = first_units(1)
    start += [[u] for u in queries[:5] + [key, queries[5], pair] + queries[6:8] + [number] + queries[8:10]
              + [key1, queries[10], dot[0], queries[11], pair1, queries[12], queries[13], queries[14], queries[15],
                 ("tok", 1, 0), square, dot[1], number1, norm, ("ada", 0, 22), dot[2], key2, ("ada", 0, 23), dot[3], pair2]]
    s = staggered(start, lambda n, after: [])
    steps = [(t, i) for t in group_tiles(0) for i in range(TILE_STEPS[t])]
    places = [[] for _ in range(PAIRS * len(steps))]
    later = [number2] + [u for t, y in ((0, 3), (1, 0), (1, 1), (1, 2), (1, 3)) for u in choice_units(t, y)]
    deal(later, places, 0, CHOICE_PLACES)
    spread(copied, places, 0, CHOICE_PLACES)
    queries, (key, pair, number) = query_units(1), choice_units(2, 0)
    tail = [("tok", 2, 0)] + queries[:4] + [("tok", 3, 0), key, queries[4], pair, ("tok", 4, 0), queries[5], number, queries[6], queries[7]]
    spread(mixer_units(1) + tail, places, CHOICE_PLACES, DENSE_PLACES)
    deal(choice_units(2, 1), places, DENSE_PLACES - 2, len(places))

    def pair_entries(steps):
        def between(n, after):
            t, i = steps[n // PAIRS]
            j = n % PAIRS
            if after:
                close = j == PAIRS - 1 and i == TILE_STEPS[t] - 1
                return [("sum", "pair", t, (i, j))] + [("both", "final", t, 0)] * close
            return [("pair", "pair", t, (i, j))] + [("both", "final", t - 1, j + 1)] * (t > 0 and i == 0 and j < 3)
        return between

    s += staggered(places, pair_entries(steps))
    for t in group_tiles(1):
        last = TILE_STEPS[t] - 1
        if PEELED[t]:
            steps = [(t, i) for i in range(PEELED[t])]
            places = [[] for _ in range(PAIRS * PEELED[t])]
            chosen = [(2, 2), (2, 3)] * (t == 2) + [(t + 1, y) for y in range(4) if t + 1 < TILES]
            deal([u for n, y in chosen for u in choice_units(n, y)], places, 5 * (t == 2), len(places))
            if t == 2:
                for n, unit in enumerate(query_units(1)[8:]):
                    places[n // 4 * 8 + n % 4 - (0 if n < 4 else 2)].insert(0, unit)
            s += staggered(places, pair_entries(steps))
        if PEELED[t] < last:
            s += [("both", "loop", t, (PEELED[t], last))]
        s += staggered([[] for _ in range(PAIRS)], pair_entries([(t, last)]))
    s += [("both", "final", t, stage) for stage in (1, 2, 3)]
    return s


SCHEDULE = schedule()
PRODUCTS = [p for role, *unit in SCHEDULE if role in ("make", "both") for p in products_of(tuple(unit))]
NUMBER = {p: n for n, p in enumerate(PRODUCTS)}


NTH = {p: sum(q[0] == p[0] for q in PRODUCTS[:n + 1]) for n, p in enumerate(PRODUCTS)}


def nth(product):
    return NTH[product]


def weight_blocks():
    blocks = {}
    for role, *unit in SCHEDULE:
        kind, g, b = unit
        if role == "make" and (kind in COLS or kind in ("ada", "rgig", "mix", "keytop")):
            if kind in COLS:
                b = b // 2
            if kind in ("rgig", "mix"):
                b = 0
            blocks[kind, g, b] = products_of(tuple(unit))[-1]
    return list(blocks.items())


BLOCKS = weight_blocks()
BLOCK_NO = {unit: n for n, (unit, _) in enumerate(BLOCKS)}


def trunk(nc, A):
    ctx = ExitStack()
    with ctx:
        def sb(name, shape, dt=F32):
            return ctx.enter_context(nc.sbuf_tensor("t_" + name, shape, dt))

        def sem(name):
            return ctx.enter_context(nc.semaphore(name))

        CEXT = KT * (N_MAX + CB)
        UEXT = KT * (N_MAX + PB)
        NB = KT * N_MAX
        arena = sb("arena", [P, 6 * NB + CEXT + UEXT])
        at, place = 0, {}
        for name, size in (("x", NB), ("h", NB), ("xc", NB), ("gy", NB), ("conv", CEXT), ("i", NB), ("pool", UEXT),
                           ("gb", NB)):
            place[name] = at
            at += size

        def region(name, size):
            return arena[:, place[name]:place[name] + size]

        def cols(name, g):
            n = GROUP_S[g] + GROUP_P[g]
            return region(name, KT * n).rearrange("p (k n) -> p k n", k=KT)

        mod_rows = arena[0:NR, place["xc"]:place["xc"] + 5 * D]
        b_ada = arena[0:NR, place["conv"]:place["conv"] + 5 * D]
        weights = sb("weights", [P, NW, KT * WB])
        u_rows = sb("u_rows", [P, NU, D])
        v_rows = sb("v_rows", [P, NV, D])
        tok0 = sb("tok0", [P, 4, D])
        g2_rows = sb("g2_rows", [NR, D])
        final_norm = sb("final_norm", [P, D])
        vecs = sb("vecs", [P, len(VEC), KT])
        ident = sb("ident", [P, P])
        ident2 = sb("ident2", [P, NS])
        select = sb("select", [NR, 2, P])
        inv_count = sb("inv_count", [P, len(WINDOWS), 16])
        iota16 = sb("iota16", [P, 16])
        ones = sb("ones", [P, P])
        zeros = sb("zeros", [1, P])
        c_t = sb("c_t", [P, KT, NR])
        silu_c = sb("silu_c", [P, KT, NR])
        mod_t = sb("mod_t", [P, 5 * KT, NR])
        coef = sb("coef", [P, 2, KT, NR])
        sp4 = sb("sp4", [P, KT])
        minus_sp8 = sb("minus_sp8", [P, KT])
        sp_tmp = sb("sp_tmp", [P, 6, KT])
        small = sb("small", [P, NS])
        conv_tail = sb("conv_tail", [P, KT, CB])
        conv_s = sb("conv_s", [P, KT, SB, CB])
        pool_tail = sb("pool_tail", [P, KT, PB])
        lru_tail = sb("lru_tail", [P, KT])
        lru_s = sb("lru_s", [P, KT, SB])
        bx_first = sb("bx_first", [P, KT])
        idx0 = sb("idx0", [P, 2, SLOTS], U32)
        gsm0 = sb("gsm0", [P, 2, SLOTS])
        step_idx = sb("step_idx", [P, 2, 2, TOPK], U32)
        dots = sb("dots", [P, TOPK])
        gelus = sb("gelus", [P, TOPK])
        wts = sb("wts", [P, TOPK])
        fin = sb("fin", [P, 4])
        banks = [ctx.enter_context(nc.psum_tensor(f"bank{i}", [P, 512], F32)) for i in range(NBANK)]
        v_sum = ctx.enter_context(nc.psum_tensor("v_sum", [P, D], F32))

        state = tok0[:, 0:2, :].rearrange("p a d -> p (a d)")
        state_pool = state[:, 0:KT * SB * PB].rearrange("p (k b t) -> p k b t", k=KT, b=SB)
        s1 = KT * SB * PB
        state_conv = state[:, s1:s1 + KT * SB * CB].rearrange("p (k b t) -> p k b t", k=KT, b=SB)
        s2 = s1 + KT * SB * CB
        state_lru = state[:, s2:s2 + KT * SB].rearrange("p (k b) -> p k b", k=KT)
        pool_s = tok0[:, 2, 0:KT * SB * PB].rearrange("p (k b t) -> p k b t", k=KT, b=SB)

        ms, rstd = (region("gb", 2 * N_MAX)[:, i * N_MAX:(i + 1) * N_MAX] for i in range(2))
        h_twice = region("gb", 2 * N_MAX + KT * P)[:, 2 * N_MAX:].rearrange("p (k n) -> p k n", k=KT)
        kept = region("pool", 12 * SLOTS).rearrange("p (a s) -> p a s", s=SLOTS)
        rows_g0 = region("i", 6 * SLOTS).rearrange("p (a s) -> p a s", s=SLOTS)

        def idx_of(t):
            return idx0[:, t, :] if t < 2 else kept[:, 4 + t, :].bitcast(U32)

        def gsm_of(t):
            return gsm0[:, t, :] if t < 2 else kept[:, 7 + t, :]

        def exps_of(t):
            return (rows_g0 if t < 2 else kept)[:, 5, :]

        def vec(name):
            return vecs[:, VEC.index(name), :]

        def h2_rows(t):
            return tok0[:, t, :] if t < 2 else region("conv", NB)[:, (t - 2) * D:(t - 1) * D]

        def x1_rows(t):
            return tok0[:, 2 + t, :] if t < 2 else region("i", NB)[:, (t - 2) * D:(t - 1) * D]

        const_in, c_in, bias_in, norm_in, x_in, state_in = (sem(x) for x in (
            "const_in", "c_in", "bias_in", "norm_in", "x_in", "state_in"))
        weight_in = [sem(f"weight_in{i}") for i in range(NW)]
        ready = {k: sem(f"{k}_ready") for k in PER}
        taken = {k: sem(f"{k}_taken") for k in PER}
        silu_done, zeros_done, square_done, std_done, h_scaled, h_prompt, h_sample = (sem(x) for x in (
            "silu_done", "zeros_done", "square_done", "std_done", "h_scaled", "h_prompt", "h_sample"))
        ms_done, conv_done, sqrt_done, scan_done, gy_done, pooled_done, exp_done, centered = (
            sem(x) for x in ("ms_done", "conv_done", "sqrt_done", "scan_done", "gy_done",
                             "pooled_done", "exp_done", "centered"))
        dve_step, coef_done, idx_done, rates_done = (sem(x) for x in ("dve_step", "coef_done", "idx_done", "rates_done"))
        u_in = [sem(f"u_in{i}") for i in range(NU)]
        v_in = [sem(f"v_in{i}") for i in range(NV)]
        u_free, v_free, idx_copied, dots_done, gelu_done, wts_done, scaled_done, paired_done = (sem(x) for x in (
            "u_free", "v_free", "idx_copied", "dots_done", "gelu_done", "wts_done", "scaled_done", "paired_done"))
        v_tile, v_read, yfin, ysq, ymean, ystd, yready, tails, out_done = (sem(x) for x in (
            "v_tile", "v_read", "yfin", "ysq", "ymean", "ystd", "yready", "tails", "out_done"))

        N_CONST = 6

        def sizes(g):
            return GROUP_S[g], GROUP_P[g], GROUP_S[g] + GROUP_P[g]

        def conv_ext(g):
            s, p, n = sizes(g)
            w = (s // ST) * (ST + CB) + p + CB
            rows = region("conv", KT * w).rearrange("p (k w) -> p k w", k=KT)
            smp = rows[:, :, 0:w - p - CB].rearrange("p k (b t) -> p k b t", t=ST + CB) if s else None
            return smp, rows[:, :, w - p - CB:w]

        def pool_ext(g):
            s, p, n = sizes(g)
            w = (s // ST) * (ST + PB) + p + PB
            rows = region("pool", KT * w).rearrange("p (k w) -> p k w", k=KT)
            smp = rows[:, :, 0:w - p - PB].rearrange("p k (b t) -> p k b t", t=ST + PB) if s else None
            return rows, smp, rows[:, :, w - p - PB:w]

        def queries(g):
            n = sizes(g)[2] + GROUP_S[g]
            return arena[:, place["xc"]:place["xc"] + 2 * KT * n].rearrange("p (k n) -> p k n", k=2 * KT)

        def by_seq(view):
            return view[:, :, 0:NS].rearrange("p k (b t) -> p k b t", b=SB)

        def quarter(n):
            return range(n * TOPK // 4, (n + 1) * TOPK // 4)

        block = ctx.enter_context(nc.Block())

        @block.sync
        def _(sp):
            sp.dma_start(c_t[:, :, :], A["c_t"]).then_inc(c_in, 16)
            sp.dma_start(b_ada, A["b_ada"][:, 0:5 * D].broadcast_to([NR, 5 * D])).then_inc(bias_in, 16)
            sp.dma_start(g2_rows[:, :], A["b_ada"][:, 5 * D:].broadcast_to([NR, D])).then_inc(bias_in, 16)

            def load_weights(n):
                unit, _ = BLOCKS[n]
                kind, g, b = unit
                if n >= NW:
                    last = BLOCKS[n - NW][1]
                    sp.wait_ge(ready[last[0]], nth(last))
                slot = weights[:, n % NW, :]
                if kind == "rgig":
                    dst = slot.rearrange("p (a h n) -> p a h n", a=2, h=HEADS)
                    sp.dma_start(dst[:, 0], A["w_rg"]).then_inc(weight_in[n % NW], 16)
                    sp.dma_start(dst[:, 1], A["w_ig"]).then_inc(weight_in[n % NW], 16)
                    return
                if kind == "keytop":
                    n_cols = 4 * NKEYS
                    src, dst = A["keys_t"][:, b * n_cols:(b + 1) * n_cols], slot[:, 0:n_cols]
                elif kind == "mix":
                    src = A["pool_mix"]
                    dst = slot.rearrange("p (g k n) -> p g k n", g=4, k=2)
                else:
                    name = {"ada": "w_ada", "bb": "w_branch_b", "ba": "w_branch_a", "out": "w_out", "q": "w_q"}.get(kind, "w_in")
                    c = (COLS.get(kind, 0) + b) * WB
                    src = A[name][:, :, c:c + WB]
                    dst = slot.rearrange("p (k n) -> p k n", k=KT)
                sp.dma_start(dst, src).then_inc(weight_in[n % NW], 16)

            for n in range(len(BLOCKS)):
                load_weights(n)
                if n == 2:
                    sp.dma_start(cols("x", 0), A["x_t0"]).then_inc(x_in, 16)
                    sp.dma_start(state_pool, A["state_pool_t"]).then_inc(state_in, 16)
                    sp.dma_start(state_conv, A["state_conv_t"]).then_inc(state_in, 16)
                    sp.dma_start(state_lru, A["state_lru_t"]).then_inc(state_in, 16)
                if BLOCKS[n][0] == ("keytop", 0, 2):
                    sp.wait_ge(ready["tok"], nth(("tok", 1, 3)))
                    sp.dma_start(cols("x", 1), A["x_t1"]).then_inc(x_in, 16)

            sp.wait_ge(tails, 2 * 4)
            sp.dma_start(A["conv_p"], conv_tail[:, :, :]).then_inc(out_done, 16)
            sp.dma_start(A["pool_p"], pool_tail[:, :, :]).then_inc(out_done, 16)
            sp.dma_start(A["lru_p"], lru_tail[:, :]).then_inc(out_done, 16)
            for t in range(1, TILES):
                sp.wait_ge(yready, t + 1)
                sp.dma_start(A["y_prompt"][(t - 1) * P:t * P, :], h2_rows(t)).then_inc(out_done, 16)
            sp.wait_ge(out_done, 16 * (3 + 4 + 4))

        @block.gpsimd
        def _(pool):
            nc.gpsimd.memset(zeros[:, :], 0.0)
            nc.gpsimd.memset(ones[:, :], 1.0).then_inc(zeros_done, 1)
            pool.dma_start(final_norm[:, :], A["final_norm"].broadcast_to([P, D])).then_inc(norm_in, 16)

            def take_indices(t, i, table, par):
                nc.gpsimd.tensor_copy(step_idx[:, table, par, :], idx_of(t)[:, bass.ds(i * TOPK, TOPK)]).then_inc(idx_copied, 1)

            def fetch(table, par, k):
                rows, slots, free, landed, source = ((u_rows, NU, u_free, u_in, A["expert_u"]),
                                                     (v_rows, NV, v_free, v_in, A["expert_v"]))[table]
                pool.wait_ge(free, 1)
                pool.sem_inc(free, -1)
                pool.indirect_dma_start(
                    out=rows[:, k % slots, :], out_offset=None, in_=source,
                    in_offset=bass.IndirectOffsetOnAxis(ap=step_idx[:, table, par, k:k + 1], axis=0),
                ).then_inc(landed[k % slots], 16)

            def fetch_step(u_step, v_step, odd, number):
                if u_step:
                    take_indices(*u_step, 0, 1 - odd)
                take_indices(*v_step, 1, odd)
                pool.wait_ge(idx_copied, number * 2 + (3 if u_step else 2))
                for k in range(0, TOPK, 2):
                    if u_step:
                        fetch(0, 1 - odd, k)
                        fetch(0, 1 - odd, k + 1)
                    fetch(1, odd, k)
                    fetch(1, odd, k + 1)

            def following(t, i):
                return (t, i + 1) if i + 1 < TILE_STEPS[t] else (t + 1, 0) if t + 1 < TILES else None

            for role, kind, t, i in SCHEDULE:
                if role == "read" and kind == "dots":
                    if i == 0:
                        pool.wait_ge(idx_done, 1)
                        take_indices(0, 0, 0, 0)
                        pool.wait_ge(idx_copied, 1)
                    for k in quarter(i):
                        fetch(0, 0, k)
                if role == "pair" and i[1] == 0:
                    i = i[0]
                    number = STEP0[t] + i
                    after = following(t, i)
                    if after and after[1] % (TILE_STEPS[after[0]] // 4) == 0:
                        pool.wait_ge(idx_done, 4 * after[0] + 1 + 4 * after[1] // TILE_STEPS[after[0]])
                    fetch_step(after, (t, i), number % 2, number)
                if kind == "loop":
                    first, end = i
                    pool.wait_ge(idx_done, 4 * t + 4)
                    with pool.Fori(0, (end - first) // 2) as two:
                        for j in range(2):
                            i = two * 2 + (first + j)
                            fetch_step((t, i + 1), (t, i), (STEP0[t] + first + j) % 2, two * 2 + (STEP0[t] + first + j))
                    if (end - first) % 2:
                        fetch_step((t, end), (t, end - 1), (STEP0[t] + end - 1) % 2, STEP0[t] + end - 1)

        @block.tensor
        def _(pe):
            done = [0]

            def begin(product):
                n = NUMBER[product]
                assert n == done[0]
                done[0] += 1
                if n >= NBANK:
                    old = PRODUCTS[n - NBANK]
                    pe.wait_ge(taken[old[0]], nth(old))
                return banks[n % NBANK]

            def block_of(unit):
                n = BLOCK_NO[unit]
                seen = sum(16 * (1 + (u[0] == "rgig")) for m, (u, _) in enumerate(BLOCKS[:n + 1]) if m % NW == n % NW)
                pe.wait_ge(weight_in[n % NW], seen)
                return weights[:, n % NW, :]

            def finish(ins, product):
                ins.then_inc(ready[product[0]], 1)

            def ada(i):
                if i == 0:
                    pe.wait_ge(silu_done, 1)
                w = block_of(("ada", 0, i)).rearrange("p (k n) -> p k n", k=KT)
                bank = begin(("ada", 0, i))
                for k in range(KT):
                    ins = nc.tensor.matmul(bank[0:NR, 0:WB], silu_c[:, k, :], w[:, k, :], start=k == 0, stop=k == KT - 1)
                finish(ins, ("ada", 0, i))

            def turn_modulation(part):
                first, end = (0, 2 * KT) if part == 0 else (2 * KT, 5 * KT)
                bank = begin(("modT", 0, part))
                pe.wait_ge(const_in, 16 * N_CONST)
                pe.wait_ge(taken["ada"], end * P // WB)
                for j in range(first, end):
                    ins = nc.tensor.transpose(bank[:, (j - first) * NR:(j - first + 1) * NR], mod_rows[:, j * P:(j + 1) * P], ident[0:NR, 0:NR])
                finish(ins, ("modT", 0, part))

            def norm(g, which):
                n = sizes(g)[2]
                product = (("ss1", "ss2")[which], g, 0)
                sq = cols("pool", g)
                bank = begin(product)
                pe.wait_ge(zeros_done, 1)
                for k in range(KT):
                    pe.wait_ge(square_done, KT * (2 * g + which) + k + 1)
                    ins = nc.tensor.matmul(bank[:, 0:n], ones[:, :], sq[:, k, :], start=k == 0, stop=k == KT - 1)
                finish(ins, product)

            def columns(kind, g, c):
                n = sizes(g)[2]
                w = block_of((kind, g, c // 2)).rearrange("p (k n) -> p k n", k=KT)
                src = cols({"bb": "gy", "ba": "pool", "out": "gb"}.get(kind, "h"), g)
                if kind in ("xb", "q") and c == 0:
                    m = 2 * g + (kind == "q") + 1
                    pe.wait_ge(h_prompt, KT * m)
                    pe.wait_ge(h_sample, m)
                if kind == "ba" and c == 0:
                    pe.wait_ge(taken["mix"], nth(("mix", g, 7)))
                if kind == "bb" and c == 0:
                    pe.wait_ge(gy_done, 4 * (g + 1))
                if kind == "out" and c == 0:
                    pe.wait_ge(taken["bb"], nth(("bb", g, 7)))
                product = (kind, g, c)
                bank = begin(product)
                j = c % 2
                for k in range(KT):
                    ins = nc.tensor.matmul(bank[:, 0:n], w[:, k, j * P:(j + 1) * P], src[:, k, :], start=k == 0, stop=k == KT - 1)
                finish(ins, product)

            def lru_gates(g, q):
                n = sizes(g)[2]
                w = block_of(("rgig", g, 0)).rearrange("p (a h n) -> p a h n", a=2, h=HEADS)
                xc = cols("xc", g)
                for c in (2 * q, 2 * q + 1):
                    pe.wait_ge(conv_done, g * KT + c + 1)
                    for a in range(2):
                        product = ("rgig", g, 2 * c + a)
                        bank = begin(product)
                        finish(nc.tensor.matmul(bank[:, 0:n], w[:, a, c, :], xc[:, c, :], start=True, stop=True), product)

            def mix(g, q):
                n = sizes(g)[2]
                w = block_of(("mix", g, 0)).rearrange("p (g k n) -> p g k n", g=4, k=2)
                pooled = cols("i", g)
                pe.wait_ge(pooled_done, g * 4 + q + 1)
                for j in range(2):
                    product = ("mix", g, 2 * q + j)
                    bank = begin(product)
                    for k in range(2):
                        ins = nc.tensor.matmul(bank[:, 0:n], w[:, q, k, j * P:(j + 1) * P], pooled[:, 2 * q + k, :], start=k == 0, stop=k == 1)
                    finish(ins, product)

            def first_col(t, samples):
                return samples if t == 1 else (t - 2) * P

            def token_rows(t):
                g = int(t >= 2)
                for i in range(4):
                    product = ("tok", t, i)
                    src = cols(("h", "x")[i // 2], g)
                    bank = begin(product)
                    if i == 0:
                        m = 2 * g + 2
                        pe.wait_ge(h_prompt, KT * m)
                        pe.wait_ge(h_sample, m)
                    for j in range(4):
                        k = 4 * (i % 2) + j
                        if t:
                            lo = first_col(t, NS)
                            tile = src[:, k, lo:lo + P]
                        else:
                            tile = h_twice[:, k, :] if i < 2 else src[:, k, 0:NS]
                        ins = nc.tensor.transpose(bank[0:tile.shape[1], j * P:(j + 1) * P], tile, ident[:, :])
                    finish(ins, product)

            def scores(t, y):
                g = int(t >= 2)
                keys = block_of(("keytop", t, y))[:, 0:4 * NKEYS].rearrange("p (h n) -> p h n", h=4)
                q = queries(g)
                lo = first_col(t, P) if t else 0
                pe.wait_ge(taken["q"], nth(("q", g, 4 * y + 3)))
                bank = begin(("score", t, y))
                for j in range(4):
                    ins = nc.tensor.matmul(bank[:, j * P:(j + 1) * P], q[:, 4 * y + j, lo:lo + P], keys[:, j, :], start=True, stop=True)
                finish(ins, ("score", t, y))

            def rows_of(t):
                return NS if t == 0 else P

            def open_sum(t, first):
                m = rows_of(t)
                if first:
                    pe.wait_ge(norm_in, 16)
                    if t:
                        pe.wait_ge(v_read, t)
                for j in range(2):
                    ins = nc.tensor.matmul(v_sum[0:m, j * 512:(j + 1) * 512], zeros[:, 0:m], final_norm[0:1, 0:512], start=first, stop=not first)
                if not first:
                    ins.then_inc(v_tile, 1)

            def sum_pairs(t, number, pairs):
                m = rows_of(t)
                add = ident2[:, :] if t == 0 else ident[:, :]
                for j in pairs:
                    pe.wait_ge(paired_done, number * PAIRS + (j + 1))
                    row = v_rows[:, (2 * j + 1) % NV, :]
                    for half in (slice(0, 512), slice(512, D)):
                        nc.tensor.matmul(v_sum[0:m, half], add, row[:, half], start=False, stop=False).then_inc(v_free, 1)

            for role, kind, g, b in SCHEDULE:
                if kind == "loop":
                    first, end = b
                    with pe.Fori(0, end - first) as i:
                        sum_pairs(g, i + (STEP0[g] + first), range(PAIRS))
                elif kind == "final":
                    if b:
                        continue
                    open_sum(g, False)
                    for i in range(2):
                        bank = begin(("g2", g, i))
                        pe.wait_ge(taken["ada"], 24)
                        finish(nc.tensor.matmul(bank[:, 0:512], select[:, int(g > 0), :], g2_rows[:, i * 512:(i + 1) * 512], start=True, stop=True), ("g2", g, i))
                elif role == "sum":
                    if b == (0, 0):
                        open_sum(g, True)
                    sum_pairs(g, STEP0[g] + b[0], [b[1]])
                elif role != "make":
                    continue
                elif kind == "ada":
                    ada(b)
                elif kind == "modT":
                    turn_modulation(b)
                elif kind == "norm":
                    norm(g, b)
                elif kind in COLS:
                    columns(kind, g, b)
                elif kind == "rgig":
                    lru_gates(g, b)
                elif kind == "mix":
                    mix(g, b)
                elif kind == "tok":
                    token_rows(g)
                elif kind == "keytop":
                    scores(g, b)

        @block.scalar
        def _(act):
            for dst, name in ((vecs, "vecs"), (ident, "ident"), (ident2, "ident2"), (select, "select"), (inv_count, "inv_count"), (iota16, "iota16")):
                act.dma_start(dst[:], A[name]).then_inc(const_in, 16)
            act.wait_ge(c_in, 16)
            nc.scalar.activation(silu_c[:, :, :], c_t[:, :, :], ACT.Silu).then_inc(silu_done, 1)
            act.wait_ge(centered, 1)
            nc.scalar.activation(sp_tmp[:, 1, :], sp_tmp[:, 0, :], ACT.Exp).then_inc(exp_done, 1)
            def take(product):
                act.wait_ge(ready[product[0]], nth(product))
                return banks[NUMBER[product] % NBANK]

            def square(g, b):
                x, sq = cols("x", g), cols("pool", g)
                if b == 0:
                    act.wait_ge(x_in, 16 * (g + 1))
                else:
                    act.wait_ge(taken["out"], nth(("out", g, b - 1)))
                for k in range(KT) if b == 0 else (b - 1,):
                    nc.scalar.activation(sq[:, k, :], x[:, k, :], ACT.Square).then_inc(square_done, 1)

            def norm(g, which):
                s, p, n = sizes(g)
                h = cols("h", g)
                act.wait_ge(ms_done, 2 * g + which + 1)
                nc.scalar.activation(rstd[:, 0:n], ms[:, 0:n], ACT.Sqrt).then_inc(std_done, 1)
                act.wait_ge(coef_done, 2 + which)
                act.wait_ge(h_scaled, 2 * g + which + 1)
                for k in range(KT):
                    nc.scalar.activation(h[:, k, s:n], h[:, k, s:n], ACT.Identity, scale=coef[:, which, k, SB:NR],
                                         bias=mod_t[:, 24 * which + k, SB:NR]).then_inc(h_prompt, 1)

            def columns(kind, g, c):
                s, p, n = sizes(g)
                if kind not in ("bb", "ba", "out"):
                    bank = take((kind, g, c))
                    if kind == "xb":
                        smp, prm = conv_ext(g)
                        if c == 0 and g:
                            act.wait_ge(taken["bb"], nth(("bb", g - 1, 7)))
                        if s:
                            nc.scalar.activation(smp[:, c, :, CB:], bank[:, 0:NS].rearrange("p (b t) -> p b t", b=SB), ACT.Copy)
                        nc.scalar.activation(prm[:, c, CB:], bank[:, s:n], ACT.Copy).then_inc(taken[kind], 1)
                    elif kind == "u":
                        rows, smp, prm = pool_ext(g)
                        if s:
                            nc.scalar.activation(smp[:, c, :, PB:], bank[:, 0:NS].rearrange("p (b t) -> p b t", b=SB), ACT.Copy)
                        nc.scalar.activation(prm[:, c, PB:], bank[:, s:n], ACT.Copy).then_inc(taken[kind], 1)
                    elif kind == "yb":
                        if g and c == 0:
                            act.wait_ge(idx_done, 8)
                        nc.scalar.activation(cols("gy", g)[:, c, :], bank[:, 0:n], ACT.Gelu_apprx_tanh).then_inc(taken[kind], 1)
                    elif kind == "mg":
                        if c < 8:
                            act.wait_ge(scan_done, 4 * g + c // 2 + 1)
                        if c == 8:
                            act.wait_ge(pooled_done, 4 * (g + 1))
                        dst = cols(("conv", "gb")[c // 8], g)[:, c % 8, :]
                        nc.scalar.activation(dst, bank[:, 0:n], ACT.Sigmoid, bias=vec(("b_gate_a", "b_gate_b")[c // 8])[:, c % 8:c % 8 + 1]).then_inc(taken[kind], 1)
                    elif kind == "q":
                        q = queries(g)
                        if s:
                            nc.scalar.activation(q[:, c, 0:NS], bank[:, 0:NS], ACT.Copy)
                        at = NS if s else 0
                        nc.scalar.activation(q[:, c, at:], bank[:, 0:n], ACT.Copy).then_inc(taken[kind], 1)

            def lru_gates(g, q):
                n = sizes(g)[2]
                for c in (2 * q, 2 * q + 1):
                    for a, (dst, bias) in enumerate((("conv", "b_rg"), ("i", "b_ig"))):
                        bank = take(("rgig", g, 2 * c + a))
                        nc.scalar.activation(cols(dst, g)[:, c, :], bank[:, 0:n], ACT.Sigmoid, bias=vec(bias)[:, c:c + 1]).then_inc(taken["rgig"], 1)

            def lru(g, q):
                r, root = cols("conv", g), cols("gb", g)
                act.wait_ge(taken["rgig"], nth(("rgig", g, 4 * q + 3)))
                for c in (2 * q, 2 * q + 1):
                    nc.scalar.activation(root[:, c, :], r[:, c, :], ACT.Tanh, scale=sp4[:, c:c + 1])
                for c in (2 * q, 2 * q + 1):
                    nc.scalar.activation(r[:, c, :], r[:, c, :], ACT.Exp, scale=minus_sp8[:, c:c + 1]).then_inc(rates_done, 1)
                act.wait_ge(rates_done, 2 * (4 * g + q + 1))
                two = root[:, 2 * q:2 * q + 2, :]
                nc.scalar.activation(two, two, ACT.Sqrt).then_inc(sqrt_done, 1)

            def mix(g, q):
                n = sizes(g)[2]
                z = cols("pool", g)
                for c in (2 * q, 2 * q + 1):
                    bank = take(("mix", g, c))
                    if c == 0:
                        act.wait_ge(pooled_done, 4 * (g + 1))
                    nc.scalar.activation(z[:, c, :], bank[:, 0:n], ACT.Copy, scale=vec("pool_scale")[:, c:c + 1]).then_inc(taken["mix"], 1)

            def token_rows(t):
                for i in range(4):
                    bank = take(("tok", t, i))
                    if i == 0 and t == 0:
                        act.wait_ge(scan_done, 4)
                        act.wait_ge(pooled_done, 4)
                        act.wait_ge(out_done, 16 * 3)
                    if i == 0 and t == 2:
                        act.wait_ge(taken["ba"], nth(("ba", 1, 7)))
                    dst = (h2_rows, x1_rows)[i // 2](t)
                    m = NS if t == 0 and i >= 2 else P
                    nc.scalar.activation(dst[0:m, (i % 2) * 512:(i % 2 + 1) * 512], bank[0:m, :], ACT.Copy).then_inc(taken["tok"], 1)

            def softmax_exp(t, y):
                act.wait_ge(centered, 4 * t + y + 2)
                part = exps_of(t)[:, y * 2 * TOPK:(y + 1) * 2 * TOPK]
                nc.scalar.activation(part, part, ACT.Exp).then_inc(exp_done, 1)

            def gelu(number):
                act.wait_ge(dots_done, number + 1)
                nc.scalar.activation(gelus[:, :], dots[:, :], ACT.Gelu_apprx_tanh).then_inc(gelu_done, 1)
                act.wait_ge(wts_done, number + 1)

            def scale_pair(number, j):
                k = 2 * j + 1
                row = v_rows[:, k % NV, :]
                act.wait_ge(v_in[k % NV], number * (16 * TOPK // NV) + 16 * (k // NV + 1))
                nc.scalar.activation(row, row, ACT.Copy, scale=wts[:, k:k + 1]).then_inc(scaled_done, 1)

            def final(t, stage):
                m = NS if t == 0 else P
                y = h2_rows(t)[0:m, :]
                if stage == 0:
                    act.wait_ge(v_tile, t + 1)
                    nc.scalar.activation(y, v_sum[0:m, :], ACT.Copy).then_inc(v_read, 1)
                if stage == 1:
                    act.wait_ge(yfin, t + 1)
                    nc.scalar.activation(x1_rows(t)[0:m, :], y, ACT.Square, accum_out=fin[0:m, 0:1]).then_inc(ysq, 1)
                if stage == 2:
                    act.wait_ge(ymean, t + 1)
                    nc.scalar.activation(fin[0:m, 2:3], fin[0:m, 1:2], ACT.Sqrt).then_inc(ystd, 1)
                if stage == 3 and t == 0:
                    act.wait_ge(yready, 1)
                    act.dma_start(A["y_sample"], y).then_inc(out_done, 16)

            for role, kind, g, b in SCHEDULE:
                if kind == "loop":
                    first, end = b
                    with act.Fori(0, end - first) as i:
                        for j in range(PAIRS):
                            if j == 0:
                                gelu(i + (STEP0[g] + first))
                            scale_pair(i + (STEP0[g] + first), j)
                elif role == "pair":
                    if b[1] == 0:
                        gelu(STEP0[g] + b[0])
                    scale_pair(STEP0[g] + b[0], b[1])
                elif role in ("make", "sum"):
                    continue
                elif kind == "modT":
                    bank = take(("modT", 0, b))
                    rows = mod_t[:, 2 * KT * b:(2, 5)[b] * KT, :].rearrange("p a r -> p (a r)")
                    nc.scalar.activation(rows, bank[:, 0:(2, 3)[b] * KT * NR], ACT.Copy).then_inc(taken["modT"], 1)
                elif kind == "square":
                    square(g, b)
                elif kind == "norm":
                    norm(g, b)
                elif kind in COLS:
                    columns(kind, g, b)
                    if kind == "yb" and (g, b) == (0, 3):
                        act.wait_ge(tails, 1)
                        act.dma_start(A["conv_s"], conv_s[:, :, :, :]).then_inc(out_done, 16)
                    if kind == "mg" and (g, b) == (0, 15):
                        act.wait_ge(tails, 4)
                        act.dma_start(A["lru_s"], lru_s[:, :, :]).then_inc(out_done, 16)
                        act.dma_start(A["pool_s"], pool_s).then_inc(out_done, 16)
                elif kind == "rgig":
                    lru_gates(g, b)
                elif kind == "lru":
                    lru(g, b)
                elif kind == "mix":
                    mix(g, b)
                elif kind == "tok":
                    token_rows(g)
                elif kind == "number":
                    softmax_exp(g, b)
                elif kind == "final":
                    final(g, b)

        @block.vector
        def _(dve):
            V = nc.vector
            steps = [0]
            counts = {}

            def link(ins):
                steps[0] += 1
                ins.then_inc(dve_step, 1)
                dve.wait_ge(dve_step, steps[0])

            def mark(ins, s, n):
                ins.then_inc(s, 1)
                dve.wait_ge(s, n)

            def take(product):
                dve.wait_ge(ready[product[0]], nth(product))
                return banks[NUMBER[product] % NBANK]

            def softplus():
                z, s, q, r = (sp_tmp[:, i, :] for i in range(1, 5))
                dve.wait_ge(exp_done, 1)
                link(V.tensor_scalar_add(s, z, 2.0))
                link(V.reciprocal(q, s))
                link(V.tensor_tensor(s, z, q, ALU.mult))
                link(V.tensor_tensor(q, s, s, ALU.mult))
                link(V.tensor_scalar(r, q, 1.0 / 17, None, ALU.mult))
                for odd in (15, 13, 11, 9, 7, 5, 3):
                    link(V.scalar_tensor_tensor(out=r, in0=r, scalar=1.0 / odd, in1=q, op0=ALU.add, op1=ALU.mult))
                link(V.scalar_tensor_tensor(out=r, in0=r, scalar=1.0, in1=s, op0=ALU.add, op1=ALU.mult))
                link(V.tensor_scalar(z, vec("lru_lambda"), -1.0, 0.0, ALU.mult, ALU.max))
                link(V.scalar_tensor_tensor(out=z, in0=r, scalar=2.0, in1=z, op0=ALU.mult, op1=ALU.add))
                link(V.tensor_scalar(minus_sp8[:, :], z, -8.0, None, ALU.mult))
                V.tensor_scalar(sp4[:, :], z, 4.0, None, ALU.mult).then_inc(coef_done, 1)

            def begin():
                dve.wait_ge(const_in, 16 * N_CONST)
                lam = vec("lru_lambda")
                link(V.tensor_scalar(sp_tmp[:, 0, :], lam, -1.0, None, ALU.mult))
                V.tensor_tensor(sp_tmp[:, 0, :], sp_tmp[:, 0, :], lam, ALU.min).then_inc(centered, 1)
                V.memset(dots[:, :], 0.0).then_inc(u_free, NU)
                V.memset(gelus[:, :], 0.0).then_inc(v_free, NV)
                dve.wait_ge(bias_in, 32)
                softplus()

            def ada(i):
                bank = take(("ada", 0, i))
                if i < 20:
                    dst = mod_rows[:, i * WB:(i + 1) * WB]
                    bias = b_ada[:, i * WB:(i + 1) * WB]
                else:
                    dst = bias = g2_rows[:, (i - 20) * WB:(i - 19) * WB]
                V.tensor_tensor(dst, bank[0:NR, 0:WB], bias, ALU.add).then_inc(taken["ada"], 1)

            def coefficients(which):
                dve.wait_ge(taken["modT"], which + 1)
                scale = mod_t[:, 8 + 24 * which:16 + 24 * which, :]
                link(V.tensor_scalar_add(coef[:, which, :, :], scale, 1.0))
                norm_w = vec(("norm1", "norm2")[which]).rearrange("p (k o) -> p k o", o=1).broadcast_to([P, KT, NR])
                mark(V.tensor_tensor(coef[:, which, :, :], coef[:, which, :, :], norm_w, ALU.mult), coef_done, 2 + which)

            def conv_histories():
                smp, prm = conv_ext(0)
                dve.wait_ge(state_in, 48)
                link(V.tensor_copy(smp[:, :, :, 0:CB], state_conv))
                link(V.memset(prm[:, :, 0:CB], 0.0))

            def over_time(view):
                return view.rearrange("p k (b o) -> p k b o", o=1).broadcast_to([P, view.shape[1], SB, ST])

            def norm(g, which):
                s, p, n = sizes(g)
                m = 2 * g + which
                x, h = cols("x", g), cols("h", g)
                bank = take((("ss1", "ss2")[which], g, 0))
                V.tensor_scalar(ms[:, 0:n], bank[:, 0:n], 1.0 / D, EPS, ALU.mult, ALU.add).then_inc(taken[("ss1", "ss2")[which]], 1)
                dve.wait_ge(taken[("ss1", "ss2")[which]], g + 1)
                dve.sem_inc(ms_done, 1)
                dve.wait_ge(std_done, m + 1)
                link(V.reciprocal(rstd[:, 0:n], rstd[:, 0:n]))
                r = rstd[:, 0:n].rearrange("p (o n) -> p o n", o=1).broadcast_to([P, KT, n])
                dve.wait_ge(x_in, 16 * (g + 1))
                if g and which == 0:
                    dve.wait_ge(ready["q"], nth(("q", 0, 15)))
                mark(V.tensor_tensor(h, x, r, ALU.mult), h_scaled, m + 1)
                if s:
                    hs = by_seq(h)
                    link(V.tensor_tensor(hs, hs, over_time(coef[:, which, :, 0:SB]), ALU.mult))
                    link(V.tensor_tensor(hs, hs, over_time(mod_t[:, 24 * which:24 * which + 8, 0:SB]), ALU.add))
                    if which:
                        twice = h[:, :, 0:NS].rearrange("p k (o n) -> p k o n", o=1).broadcast_to([P, KT, 2, NS])
                        link(V.tensor_copy(h_twice.rearrange("p k (o n) -> p k o n", o=2), twice))
                    dve.sem_inc(h_sample, 1)
                else:
                    dve.sem_inc(h_sample, 1)
                if which == 0:
                    rows, psmp, pprm = pool_ext(g)
                    if g:
                        link(V.tensor_copy(pprm[:, :, 0:PB], pool_tail[:, :, :]))
                    else:
                        dve.wait_ge(state_in, 48)
                        link(V.tensor_copy(psmp[:, :, :, 0:PB], state_pool))
                        link(V.memset(pprm[:, :, 0:PB], 0.0))

            def conv(g, c):
                s, p, n = sizes(g)
                smp, prm = conv_ext(g)
                xc = cols("xc", g)
                if g and c == 0:
                    link(V.tensor_copy(prm[:, :, 0:CB], conv_tail[:, :, :]))
                dve.wait_ge(taken["xb"], nth(("xb", g, c)))
                parts = [(xc[:, c, s:n], lambda t: prm[:, c, t:t + p])]
                if s:
                    parts.append((by_seq(xc)[:, c], lambda t: smp[:, c, :, t:t + ST]))
                for out, tap in parts:
                    V.tensor_scalar(out, tap(0), vec("conv_w0")[:, c:c + 1], vec("conv_b")[:, c:c + 1], ALU.mult, ALU.add).then_inc(dve_step, 1)
                    steps[0] += 1
                for t in range(1, CW):
                    dve.wait_ge(dve_step, steps[0])
                    for out, tap in parts:
                        V.scalar_tensor_tensor(out=out, in0=tap(t), scalar=vec(f"conv_w{t}")[:, c:c + 1], in1=out, op0=ALU.mult, op1=ALU.add).then_inc(dve_step, 1)
                        steps[0] += 1
                dve.wait_ge(dve_step, steps[0])
                if s:
                    link(V.tensor_copy(conv_s[:, c, :, :], smp[:, c, :, ST:]))
                V.tensor_copy(conv_tail[:, c, :], prm[:, c, p:]).then_inc(conv_done, 1)
                if c == KT - 1:
                    dve.wait_ge(conv_done, KT * (g + 1))
                    dve.sem_inc(tails, 1)

            def lru(g, q):
                s, p, n = sizes(g)
                two = slice(2 * q, 2 * q + 2)
                a, bx, xc, root = (cols(x, g)[:, two, :] for x in ("conv", "i", "xc", "gb"))
                dve.wait_ge(taken["rgig"], nth(("rgig", g, 4 * q + 3)))
                link(V.tensor_tensor(bx, bx, xc, ALU.mult))
                if g == 0:
                    link(V.tensor_copy(bx_first[:, two], bx[:, :, s]))
                dve.wait_ge(sqrt_done, 4 * g + q + 1)
                link(V.tensor_tensor(bx, bx, root, ALU.mult))
                link(V.scalar_tensor_tensor(out=bx, in0=a, scalar=1.0, in1=bx, op0=ALU.add, op1=ALU.mult))
                if g == 0:
                    link(V.tensor_copy(bx[:, :, s], bx_first[:, two]))
                    a0, b0 = by_seq(a)[:, :, :, 0], by_seq(bx)[:, :, :, 0]
                    link(V.tensor_tensor(lru_s[:, two, :], a0, state_lru[:, two, :], ALU.mult))
                    link(V.tensor_tensor(b0, b0, lru_s[:, two, :], ALU.add))
                    link(V.memset(a0, 0.0))
                else:
                    link(V.tensor_tensor(lru_tail[:, two], lru_tail[:, two], a[:, :, 0], ALU.mult))
                    link(V.tensor_tensor(bx[:, :, 0], bx[:, :, 0], lru_tail[:, two], ALU.add))
                link(V.memset(a[:, :, s], 0.0))
                flat = [arena[:, place[x] + 2 * q * n:place[x] + (2 * q + 2) * n] for x in ("xc", "conv", "i")]
                link(V.tensor_tensor_scan(out=flat[0], data0=flat[1], data1=flat[2], initial=0.0, op0=ALU.mult, op1=ALU.add))
                if s:
                    link(V.tensor_copy(lru_s[:, two, :], by_seq(xc)[:, :, :, ST - 1]))
                link(V.tensor_copy(lru_tail[:, two], xc[:, :, n - 1]))
                if q == 3:
                    dve.sem_inc(tails, 1)
                dve.sem_inc(scan_done, 1)
                dve.wait_ge(taken["yb"], max(nth(("yb", g, c)) for c in (2 * q, 2 * q + 1)))
                gy = cols("gy", g)[:, two, :]
                V.tensor_tensor(gy, gy, xc, ALU.mult).then_inc(gy_done, 1)

            def pooling(g, q):
                s, p, n = sizes(g)
                rows, smp, prm = pool_ext(g)
                w = rows.shape[2]
                pooled = cols("i", g)
                two = slice(2 * q, 2 * q + 2)
                dve.wait_ge(taken["u"], nth(("u", g, 2 * q + 1)))
                half = 2 * w
                sums = [region("gb", NB)[:, i * half:(i + 1) * half].rearrange("p (k w) -> p k w", k=2) for i in range(2)]
                src, lag = rows[:, two, :], 1
                for level in range(q + 1):
                    dst = sums[level % 2]
                    lo = 2 * lag - 1
                    link(V.tensor_tensor(dst[:, :, lo:w], src[:, :, lo:w], src[:, :, lo - lag:w - lag], ALU.add))
                    src, lag = dst, 2 * lag
                base = w - p - PB
                window = float(WINDOWS[q])
                V.scalar_tensor_tensor(out=pooled[:, two, s:n], in0=src[:, :, base + PB:w], scalar=1.0 / window,
                                       in1=prm[:, two, PB:], op0=ALU.mult, op1=ALU.subtract).then_inc(dve_step, 1)
                steps[0] += 1
                if s:
                    for c in range(2):
                        in0 = src[:, c, 0:base].rearrange("p (b t) -> p b t", b=SB)[:, :, PB:]
                        link(V.scalar_tensor_tensor(out=by_seq(pooled)[:, 2 * q + c], in0=in0, scalar=1.0 / window,
                                                    in1=smp[:, 2 * q + c, :, PB:], op0=ALU.mult, op1=ALU.subtract))
                    tmp = small[:, 0:32].rearrange("p (k t) -> p k t", k=2)
                    inv = inv_count[:, q:q + 1, :].broadcast_to([P, 2, 16])
                    link(V.tensor_tensor(tmp, src[:, :, base + PB:base + PB + 16], inv, ALU.mult))
                    link(V.tensor_tensor(pooled[:, two, s:s + 16], tmp, prm[:, two, PB:PB + 16], ALU.subtract))
                    link(V.tensor_copy(pool_s[:, two, :, :], smp[:, two, :, ST:]))
                link(V.tensor_copy(pool_tail[:, two, :], prm[:, two, p:]))
                dve.sem_inc(pooled_done, 1)
                if q == 3:
                    dve.sem_inc(tails, 2)

            def gated(kind, g, c):
                s, p, n = sizes(g)
                ga, gb, x = cols("conv", g), cols("gb", g), cols("x", g)
                if kind == "ba" and c == 0:
                    dve.wait_ge(taken["mg"], nth(("mg", g, 15)))
                bank = take((kind, g, c))
                if kind == "ba":
                    V.tensor_tensor(ga[:, c, :], ga[:, c, :], bank[:, 0:n], ALU.mult).then_inc(taken[kind], 1)
                elif kind == "bb":
                    link(V.tensor_tensor(gb[:, c, :], gb[:, c, :], bank[:, 0:n], ALU.mult))
                    dve.wait_ge(taken["ba"], nth(("ba", g, c)))
                    V.tensor_tensor(gb[:, c, :], gb[:, c, :], ga[:, c, :], ALU.add).then_inc(taken[kind], 1)
                else:
                    if s:
                        gate = over_time(mod_t[:, 16 + c:17 + c, 0:SB])
                        tmp = small[:, 0:NS].rearrange("p (o b t) -> p o b t", o=1, b=SB)
                        link(V.tensor_tensor(tmp, bank[:, 0:NS].rearrange("p (o b t) -> p o b t", o=1, b=SB), gate, ALU.mult))
                        link(V.tensor_tensor(x[:, c, 0:NS], x[:, c, 0:NS], small[:, 0:NS], ALU.add))
                    V.scalar_tensor_tensor(out=x[:, c, s:n], in0=bank[:, s:n], scalar=mod_t[:, 16 + c, SB:NR], in1=x[:, c, s:n],
                                           op0=ALU.mult, op1=ALU.add).then_inc(taken[kind], 1)

            H2 = 2

            def scratch(t):
                area, rows = region("gb", NB)[:, 2 * N_MAX:], rows_g0 if t < 2 else kept
                sizes = dict(grid=1024, top_v=256, top_f=256, best_v=SLOTS, part_f=2 * SLOTS,
                             chosen=2 * SLOTS, sums8=HEADS)
                at, out = 0, {}
                for name, size in sizes.items():
                    out[name] = area[:, at:at + size]
                    at += size
                for name in ("top_v", "top_f", "part_f", "chosen"):
                    out[name] = out[name].rearrange("p (h k) -> p h k", h=2 * HEADS)
                out["best_v"] = out["best_v"].rearrange("p (h k) -> p h k", h=HEADS)
                out["cand"], out["less"] = out["grid"][:, 0:512], out["grid"][:, 512:]
                out["less4"] = out["cand"].rearrange("p (i n) -> p i n", i=4)
                out["top_i"] = rows[:, 0:2, :].bitcast(U32).rearrange("p a (h k) -> p (a h) k", k=TOPK)
                out["best_j"] = rows[:, 2, :].bitcast(U32)
                out["part_u"] = rows[:, 3:5, :].bitcast(U32).rearrange("p a (h k) -> p (a h) k", k=TOPK)
                return out

            def batch(instructions):
                for ins in instructions:
                    ins.then_inc(dve_step, 1)
                    steps[0] += 1
                dve.wait_ge(dve_step, steps[0])

            def key_tops(t, y):
                w = scratch(t)
                top_v, top_i, less4 = w["top_v"], w["top_i"], w["less4"]
                bank = take(("score", t, y))
                s = [bank[:, j * P:(j + 1) * P] for j in range(4)]
                hp = range(4 * y, 4 * y + 4)
                batch(V.max(top_v[:, h, 0:8], s[j]) for j, h in enumerate(hp))
                batch(V.max_index(top_i[:, h, 0:8], top_v[:, h, 0:8], s[j]) for j, h in enumerate(hp))
                batch(V.match_replace(less4[:, j, :], top_v[:, h, 0:8], s[j], LOWEST) for j, h in enumerate(hp))
                dve.sem_inc(taken["score"], 1)
                batch(V.max(top_v[:, h, 8:16], less4[:, j, :]) for j, h in enumerate(hp))
                batch(V.max_index(top_i[:, h, 8:16], top_v[:, h, 8:16], less4[:, j, :]) for j, h in enumerate(hp))

            def grid_of(x, n):
                return x.rearrange("p (h k m) -> p h k m", h=n, k=TOPK)

            def down(x):
                return x.rearrange("p h (k o) -> p h k o", o=1).broadcast_to([P, x.shape[1], TOPK, TOPK])

            def across(x):
                return x.rearrange("p h (o k) -> p h o k", o=1).broadcast_to([P, x.shape[1], TOPK, TOPK])

            def pair_tops(t, y):
                w = scratch(t)
                heads = range(y * H2, (y + 1) * H2)
                halves = w["top_v"].rearrange("p (h a) k -> p h a k", a=2)[:, y * H2:(y + 1) * H2]
                link(V.tensor_tensor(grid_of(w["cand"], H2), down(halves[:, :, 0, :]), across(halves[:, :, 1, :]), ALU.add))
                c, l = ([w[x][:, 256 * h:256 * h + 256] for h in range(H2)] for x in ("cand", "less"))
                v = [w["best_v"][:, h, :] for h in heads]
                j = [w["best_j"][:, h * TOPK:(h + 1) * TOPK] for h in heads]
                batch(V.max(v[h][:, 0:8], c[h]) for h in range(H2))
                batch(V.max_index(j[h][:, 0:8], v[h][:, 0:8], c[h]) for h in range(H2))
                batch(V.match_replace(l[h], v[h][:, 0:8], c[h], LOWEST) for h in range(H2))
                batch(V.max(v[h][:, 8:16], l[h]) for h in range(H2))
                batch(V.max_index(j[h][:, 8:16], v[h][:, 8:16], l[h]) for h in range(H2))

            def numbers(t, y):
                w = scratch(t)
                mine = slice(y * H2 * TOPK, (y + 1) * H2 * TOPK)
                heads = slice(y * H2, (y + 1) * H2)
                best_v, sums8 = w["best_v"], w["sums8"]
                top = best_v[:, heads, 0:1].broadcast_to([P, H2, TOPK])
                exps = exps_of(t)[:, mine]
                e3 = exps.rearrange("p (h k) -> p h k", h=H2)
                V.tensor_tensor(e3, best_v[:, heads, :], top, ALU.subtract).then_inc(centered, 1)
                parts = slice(2 * y * H2, 2 * (y + 1) * H2)
                part_u, part_f, top_f, chosen = (w[x][:, parts, :] for x in ("part_u", "part_f", "top_f", "chosen"))
                of_half = [part_u.rearrange("p (h a) k -> p h a k", a=2)[:, :, a, :] for a in range(2)]
                bj = w["best_j"][:, mine].rearrange("p (h k) -> p h k", h=H2)
                batch([V.tensor_scalar(of_half[0], bj, 4, None, ALU.logical_shift_right),
                       V.tensor_scalar(of_half[1], bj, 15, None, ALU.bitwise_and),
                       V.tensor_copy(top_f, w["top_i"][:, parts, :])])
                link(V.tensor_copy(part_f, part_u))
                count = iota16[:, :].rearrange("p (h k m) -> p h k m", h=1, k=1).broadcast_to([P, 2 * H2, TOPK, TOPK])
                grid = grid_of(w["grid"], 2 * H2)
                link(V.tensor_tensor(grid, count, down(part_f), ALU.is_equal))
                link(V.tensor_tensor(grid, grid, across(top_f), ALU.mult))
                link(V.reduce_sum(chosen, grid, axis=AX.X))
                first, second = (chosen.rearrange("p (h a) k -> p h a k", a=2)[:, :, a, :] for a in range(2))
                link(V.scalar_tensor_tensor(out=first, in0=first, scalar=float(NKEYS), in1=second, op0=ALU.mult, op1=ALU.add))
                step = slice(y * TOPK, (y + 1) * TOPK)
                doubled = ((0, slice(0, NS)), (1, slice(NS, P)))
                if t:
                    link(V.tensor_copy(idx_of(t)[:, mine].rearrange("p (h k) -> p h k", h=H2), first))
                else:
                    batch(V.tensor_copy(idx0[rows, 0, step], first[rows, odd, :]) for odd, rows in doubled)
                dve.sem_inc(idx_done, 1)
                dve.wait_ge(exp_done, 4 * t + y + 2)
                link(V.reduce_sum(sums8[:, heads], e3, axis=AX.X))
                link(V.reciprocal(sums8[:, heads], sums8[:, heads]))
                inv = sums8[:, heads].rearrange("p (h o) -> p h o", o=1).broadcast_to([P, H2, TOPK])
                if t:
                    link(V.tensor_tensor(gsm_of(t)[:, mine].rearrange("p (h k) -> p h k", h=H2), e3, inv, ALU.mult))
                else:
                    link(V.tensor_tensor(e3, e3, inv, ALU.mult))
                    batch(V.tensor_copy(gsm0[rows, 0, step], exps[rows, odd * TOPK:(odd + 1) * TOPK]) for odd, rows in doubled)

            def dot(t, number, k):
                row = u_rows[:, k % NU, :]
                dve.wait_ge(u_in[k % NU], number * (16 * TOPK // NU) + 16 * (k // NU + 1))
                ins = V.tensor_tensor_reduce(out=row, in0=row, in1=h2_rows(t), scale=1.0, scalar=0.0, op0=ALU.mult, op1=ALU.add,
                                             accum_out=dots[:, k:k + 1])
                ins.then_inc(u_free if k < TOPK - 1 else dots_done, 1)
                if k == TOPK - 1:
                    dve.wait_ge(dots_done, number + 1)
                    dve.sem_inc(u_free, 1)

            def weigh(t, i, number):
                if t or i:
                    dve.wait_ge(paired_done, number * PAIRS)
                dve.wait_ge(gelu_done, number + 1)
                mark(V.tensor_tensor(wts[:, :], gelus[:, :], gsm_of(t)[:, bass.ds(i * TOPK, TOPK)], ALU.mult), wts_done, number + 1)

            def pair(t, i, number, j, dots_tile):
                if j == 0:
                    weigh(t, i, number)
                if dots_tile is not None:
                    dot(dots_tile, number + 1, 2 * j)
                    dot(dots_tile, number + 1, 2 * j + 1)
                k = 2 * j
                one, two = v_rows[:, k % NV, :], v_rows[:, (k + 1) % NV, :]
                dve.wait_ge(v_in[k % NV], number * (16 * TOPK // NV) + 16 * (k // NV + 1))
                dve.wait_ge(scaled_done, number * PAIRS + (j + 1))
                V.scalar_tensor_tensor(out=two, in0=one, scalar=wts[:, k:k + 1], in1=two, op0=ALU.mult, op1=ALU.add).then_inc(paired_done, 1)

            def final(t, stage):
                m = NS if t == 0 else P
                y, x1 = h2_rows(t)[0:m, :], x1_rows(t)[0:m, :]
                if stage == 1:
                    dve.wait_ge(v_read, t + 1)
                    for i in range(2):
                        bank = take(("g2", t, i))
                        half = slice(i * 512, (i + 1) * 512)
                        mark(V.tensor_tensor(y[:, half], y[:, half], bank[0:m, :], ALU.mult), taken["g2"], nth(("g2", t, i)))
                    V.tensor_tensor(y, y, x1, ALU.add).then_inc(yfin, 1)
                if stage == 2:
                    dve.wait_ge(ysq, t + 1)
                    mark(V.tensor_scalar(fin[0:m, 1:2], fin[0:m, 0:1], 1.0 / D, EPS, ALU.mult, ALU.add), ymean, t + 1)
                if stage == 3:
                    dve.wait_ge(ystd, t + 1)
                    link(V.reciprocal(fin[0:m, 3:4], fin[0:m, 2:3]))
                    if t == 0:
                        dve.wait_ge(norm_in, 16)
                    V.scalar_tensor_tensor(out=y, in0=y, scalar=fin[0:m, 3:4], in1=final_norm[0:m, :], op0=ALU.mult, op1=ALU.mult).then_inc(yready, 1)

            begin()
            for role, kind, g, b in SCHEDULE:
                if kind == "loop":
                    first, end = b
                    with dve.Fori(0, end - first) as i:
                        for j in range(PAIRS):
                            pair(g, i + first, i + (STEP0[g] + first), j, g)
                elif role == "pair":
                    i, j = b
                    next_tile = g if i + 1 < TILE_STEPS[g] else g + 1 if g + 1 < TILES else None
                    pair(g, i, STEP0[g] + i, j, next_tile)
                elif role in ("make", "sum"):
                    continue
                elif kind == "dots":
                    for k in quarter(b):
                        dot(0, 0, k)
                elif kind == "ada":
                    ada(b)
                elif kind == "modT":
                    coefficients(b)
                    if b == 1:
                        conv_histories()
                elif kind == "norm":
                    norm(g, b)
                elif kind == "conv":
                    conv(g, b)
                elif kind == "lru":
                    lru(g, b)
                elif kind == "pool":
                    pooling(g, b)
                elif kind in ("ba", "bb", "out"):
                    gated(kind, g, b)
                elif kind == "keytop":
                    key_tops(g, b)
                elif kind == "pairtop":
                    pair_tops(g, b)
                elif kind == "number":
                    numbers(g, b)
                elif kind == "final":
                    final(g, b)


OUTPUTS = {"y_prompt": (SEQ, D), "y_sample": (NS, D), "pool_p": (P, KT, PB), "conv_p": (P, KT, CB), "lru_p": (P, KT),
           "pool_s": (P, KT, SB, PB), "conv_s": (P, KT, SB, CB), "lru_s": (P, KT, SB)}


def kernel(x_prompt, x_sample, c_prompt, c_sample, state_pool, state_conv, state_lru, norm1, norm2, w_ada, b_ada,
           w_in, b_gate, pool_mix, pool_scale, conv_w, conv_b, w_rg, b_rg, w_ig, b_ig, lru_lambda, w_branch_a,
           w_branch_b, w_out, w_q, sub_keys, expert_u, expert_v, final_norm):
    import numpy as np
    import concourse.bacc as bacc
    from concourse.bass_utils import run_bass_kernel_spmd

    def features_first(a):
        a = np.asarray(a)
        return np.ascontiguousarray(np.moveaxis(a.reshape(a.shape[:-1] + (KT, P)), (-1, -2), (0, 1)))

    def rows(a):
        return np.asarray(a)[0]

    xs, xp = np.asarray(x_sample).reshape(NS, D), np.asarray(x_prompt)[0]
    vectors = [rows(norm1), rows(norm2), rows(pool_scale), rows(conv_b), rows(b_rg), rows(b_ig), rows(lru_lambda),
               *rows(conv_w), rows(b_gate)[:D], rows(b_gate)[D:]]
    n = np.arange(P)
    select = np.zeros((NR, 2, P), np.float32)
    select[n % NS // ST, 0, n] = 1.0
    select[SB, 1, :] = 1.0
    counts = np.minimum(np.arange(16)[None, :] + 1, np.array(WINDOWS)[:, None])
    arrays = {
        "x_t0": features_first(np.concatenate([xs, xp[:GROUP_P[0]]])),
        "x_t1": features_first(xp[GROUP_P[0]:]),
        "c_t": features_first(np.concatenate([np.asarray(c_sample), np.asarray(c_prompt)])),
        "state_pool_t": features_first(rows(state_pool)),
        "state_conv_t": features_first(rows(state_conv)),
        "state_lru_t": features_first(rows(state_lru)),
        "vecs": np.ascontiguousarray(np.stack([features_first(v) for v in vectors], axis=1)),
        "keys_t": np.ascontiguousarray(rows(sub_keys).reshape(2 * HEADS, NKEYS, P).transpose(2, 0, 1).reshape(P, -1)),
        "ident": np.eye(P, dtype=np.float32),
        "ident2": np.concatenate([np.eye(NS, dtype=np.float32)] * 2),
        "select": select,
        "inv_count": np.ascontiguousarray(np.broadcast_to((1.0 / counts).astype(np.float32), (P, len(WINDOWS), 16))),
        "iota16": np.ascontiguousarray(np.broadcast_to(np.arange(16, dtype=np.float32), (P, 16))),
        "b_ada": np.asarray(b_ada), "final_norm": np.asarray(final_norm).reshape(1, D),
        "w_ada": rows(w_ada), "w_in": rows(w_in), "w_branch_a": rows(w_branch_a), "w_branch_b": rows(w_branch_b),
        "w_out": rows(w_out), "w_q": rows(w_q), "pool_mix": rows(pool_mix), "w_rg": rows(w_rg), "w_ig": rows(w_ig),
        "expert_u": rows(expert_u), "expert_v": rows(expert_v),
    }
    nc = bacc.Bacc("TRN2", target_bir_lowering=False, num_devices=1)
    A, launched = {}, {}
    for name, a in arrays.items():
        a = np.ascontiguousarray(a)
        launched["in_" + name] = a
        A[name] = nc.dram_tensor("in_" + name, a.shape, mybir.dt.from_np(a.dtype), kind="ExternalInput").ap()
    for name, shape in OUTPUTS.items():
        A[name] = nc.dram_tensor("out_" + name, shape, F32, kind="ExternalOutput").ap()
    for name in ("w_ada", "w_in", "w_branch_a", "w_branch_b", "w_out", "w_q"):
        A[name] = A[name].rearrange("(k p) n -> p k n", p=P)
    A["pool_mix"] = A["pool_mix"].rearrange("g (k p) n -> p g k n", p=P)
    A["w_rg"], A["w_ig"] = (A[x].rearrange("h p n -> p h n") for x in ("w_rg", "w_ig"))
    trunk(nc, A)
    r = run_bass_kernel_spmd(nc, [launched], core_ids=[0]).results[0]

    def features_last(name):
        a = np.moveaxis(r["out_" + name], (0, 1), (-1, -2))
        return np.ascontiguousarray(a.reshape(a.shape[:-2] + (D,)))

    return (r["out_y_prompt"].reshape(1, SEQ, D), r["out_y_sample"].reshape(SB, ST, D),
            features_last("pool_p")[None, None], features_last("conv_p")[None, None], features_last("lru_p")[None, None],
            features_last("pool_s")[None], features_last("conv_s")[None], features_last("lru_s")[None])
```
